# Optimizing a Trainium2 kernel written in Bass

```python
import jax, jax.numpy as jnp
from jax import lax
import numpy as np

D_MODEL = 1024
BATCH = 1
SEQ = 512
DEPTH = 2

N_META = 16
CHUNK = 128
PAD = CHUNK - N_META
EPS = 1e-6
SSD_HEADS = 16
SSD_HEAD_DIM = 64
SSD_D_INNER = SSD_HEADS * SSD_HEAD_DIM
SSD_GROUPS = 2
SSD_HEADS_PER_GROUP = SSD_HEADS // SSD_GROUPS
SSD_STATE = 128
SSD_CONV = 4
SSD_CONV_CH = SSD_D_INNER + 2 * SSD_GROUPS * SSD_STATE
MLA_HEADS = 16
MLA_NOPE = 64
MLA_ROPE = 32
MLA_V = 64
MLA_Q_RANK = 384
MLA_KV_RANK = 256
ROPE_BASE = 10000.0
IN_SPLITS = (SSD_D_INNER, SSD_CONV_CH, SSD_HEADS, MLA_Q_RANK, MLA_KV_RANK, MLA_ROPE)
D_IN = sum(IN_SPLITS)
AB_WIDTH = SSD_D_INNER + MLA_HEADS * MLA_V
LRU_WIDTH = 1280
LRU_BLOCKS = 10
LRU_BLOCK = LRU_WIDTH // LRU_BLOCKS
LRU_CONV = 4
LRU_C = 8.0
D_FF = 4 * D_MODEL
N_EVEN = (DEPTH + 1) // 2
N_ODD = DEPTH // 2

kernel_name = 'hybrid_ssd_mla_rglru_sandwich_meta'

def rmsnorm(x, g):
    xf = x.astype(jnp.float32)
    y = xf * lax.rsqrt(jnp.mean(xf * xf, axis=-1, keepdims=True) + EPS)
    return (y * g.astype(jnp.float32)).astype(x.dtype)

def _split(x, sizes):
    offs = np.cumsum(sizes)[:-1].tolist()
    return jnp.split(x, offs, axis=-1)

def pad_front(x, n):
    return jnp.pad(x, [(0, 0), (n, 0)] + [(0, 0)] * (x.ndim - 2))

def causal_dwconv(x, w, b):
    k, t = w.shape[0], x.shape[1]
    xp = jnp.pad(x, ((0, 0), (k - 1, 0), (0, 0)))
    out = b
    for i in range(k):
        out = out + xp[:, i:i + t] * w[i]
    return out

def rope_tables(t, dim):
    inv = ROPE_BASE ** (-jnp.arange(0, dim, 2, dtype=jnp.float32) / dim)
    ang = jnp.arange(t, dtype=jnp.float32)[:, None] * inv[None, :]
    return jnp.cos(ang), jnp.sin(ang)

def apply_rope(x, cos, sin):
    half = x.shape[-1] // 2
    x1, x2 = x[..., :half], x[..., half:]
    return jnp.concatenate([x1 * cos - x2 * sin, x2 * cos + x1 * sin], axis=-1).astype(x.dtype)

def ssd_chunked_scan(xdt, da, bm, cm):
    b, tp = xdt.shape[:2]
    nc = tp // CHUNK
    g, k = SSD_GROUPS, SSD_HEADS_PER_GROUP
    x = xdt.reshape(b, nc, CHUNK, g, k, SSD_HEAD_DIM)
    a = da.reshape(b, nc, CHUNK, g, k).transpose(0, 1, 3, 4, 2)
    bc = bm.reshape(b, nc, CHUNK, g, SSD_STATE)
    cc = cm.reshape(b, nc, CHUNK, g, SSD_STATE)
    a_cs = jnp.cumsum(a, axis=-1)
    causal = jnp.tril(jnp.ones((CHUNK, CHUNK), dtype=bool))
    seg = a_cs[..., :, None] - a_cs[..., None, :]
    decay_in = jnp.exp(jnp.where(causal, seg, -jnp.inf))
    cb = jnp.einsum('bclgn,bcsgn->bcgls', cc, bc)
    y_diag = jnp.einsum('bcgkls,bcsgkp->bclgkp', cb[:, :, :, None] * decay_in, x)
    decay_to_end = jnp.exp(a_cs[..., -1:] - a_cs)
    states = jnp.einsum('bclgn,bcgkl,bclgkp->bcgkpn', bc, decay_to_end, x).astype(jnp.float32)
    chunk_decay = jnp.exp(a_cs[..., -1])

    def step(h, inp):
        dec, st = inp
        return dec[..., None, None] * h + st, h

    h0 = jnp.zeros((b, g, k, SSD_HEAD_DIM, SSD_STATE), jnp.float32)
    _, prev = lax.scan(step, h0, (jnp.moveaxis(chunk_decay, 1, 0), jnp.moveaxis(states, 1, 0)))
    prev = jnp.moveaxis(prev, 0, 1)
    y_off = jnp.einsum('bclgn,bcgkpn,bcgkl->bclgkp', cc.astype(jnp.float32), prev, jnp.exp(a_cs))
    y = y_diag.astype(jnp.float32) + y_off
    return y.reshape(b, tp, SSD_HEADS, SSD_HEAD_DIM).astype(xdt.dtype)

def ssd_branch(z, xbc, dt_raw, conv_w, conv_b, dt_bias, a_log, d_skip, norm_g):
    b, t, _ = z.shape
    xbc = jax.nn.silu(causal_dwconv(xbc, conv_w, conv_b))
    xs, bm, cm = _split(xbc, (SSD_D_INNER, SSD_GROUPS * SSD_STATE, SSD_GROUPS * SSD_STATE))
    dt = jax.nn.softplus(dt_raw.astype(jnp.float32) + dt_bias.astype(jnp.float32))
    a = -jnp.exp(a_log.astype(jnp.float32))
    xh = xs.reshape(b, t, SSD_HEADS, SSD_HEAD_DIM)
    xdt = pad_front(xh * dt[..., None].astype(xh.dtype), PAD)
    da = pad_front(dt * a, PAD)
    bm = pad_front(bm.reshape(b, t, SSD_GROUPS, SSD_STATE), PAD)
    cm = pad_front(cm.reshape(b, t, SSD_GROUPS, SSD_STATE), PAD)
    y = ssd_chunked_scan(xdt, da, bm, cm)[:, PAD:]
    y = y + d_skip[:, None] * xh
    y = y.reshape(b, t, SSD_D_INNER)
    return rmsnorm(y * jax.nn.silu(z), norm_g)

def mla_branch(cq, ckv, krope, q_norm_g, w_q_up, kv_norm_g, w_kv_up, cos, sin):
    b, t, _ = cq.shape
    q = (rmsnorm(cq, q_norm_g) @ w_q_up).reshape(b, t, MLA_HEADS, MLA_NOPE + MLA_ROPE)
    q = jnp.concatenate([q[..., :MLA_NOPE], apply_rope(q[..., MLA_NOPE:], cos[:, None], sin[:, None])], axis=-1)
    kv = (rmsnorm(ckv, kv_norm_g) @ w_kv_up).reshape(b, t, MLA_HEADS, MLA_NOPE + MLA_V)
    k_r = apply_rope(krope, cos, sin)
    k = jnp.concatenate([kv[..., :MLA_NOPE],
                         jnp.broadcast_to(k_r[:, :, None], (b, t, MLA_HEADS, MLA_ROPE))], axis=-1)
    v = kv[..., MLA_NOPE:]
    qp, kp, vp = pad_front(q, PAD), pad_front(k, PAD), pad_front(v, PAD)
    tp = t + PAD
    nb = tp // CHUNK
    scale = (MLA_NOPE + MLA_ROPE) ** -0.5
    kidx = jnp.arange(tp)

    def block(j):
        q_blk = lax.dynamic_slice_in_dim(qp, j * CHUNK, CHUNK, axis=1)
        s = jnp.einsum('bqhd,bkhd->bhqk', q_blk, kp).astype(jnp.float32) * scale
        qidx = j * CHUNK + jnp.arange(CHUNK)
        mask = (kidx[None, :] <= qidx[:, None]) & (kidx[None, :] >= PAD)
        s = jnp.where(mask, s, -1e30)
        p = jax.nn.softmax(s, axis=-1).astype(vp.dtype)
        return jnp.einsum('bhqk,bkhd->bqhd', p, vp)

    o = lax.map(block, jnp.arange(nb))
    o = o.transpose(1, 0, 2, 3, 4).reshape(b, tp, MLA_HEADS * MLA_V)
    return o[:, PAD:]

def mixer_ssd_mla(h, w_in, conv_w, conv_b, dt_bias, a_log, d_skip, ssd_norm_g,
                  q_norm_g, w_q_up, kv_norm_g, w_kv_up, w_out, cos, sin):
    z, xbc, dt_raw, cq, ckv, krope = _split(h @ w_in, IN_SPLITS)
    y_ssd = ssd_branch(z, xbc, dt_raw, conv_w, conv_b, dt_bias, a_log, d_skip, ssd_norm_g)
    y_att = mla_branch(cq, ckv, krope, q_norm_g, w_q_up, kv_norm_g, w_kv_up, cos, sin)
    return jnp.concatenate([y_ssd, y_att], axis=-1) @ w_out

def _lru_combine(c1, c2):
    a1, b1 = c1
    a2, b2 = c2
    return a1 * a2, a2 * b1 + b2

def mixer_rglru(h, w_x, w_y, conv_w, conv_b, w_a, b_a, w_i, b_i, lam, w_out):
    b, t, _ = h.shape
    gate = jax.nn.gelu(h @ w_y)
    xr = causal_dwconv(h @ w_x, conv_w, conv_b)
    xb = xr.reshape(b, t, LRU_BLOCKS, LRU_BLOCK)
    r = jax.nn.sigmoid(jnp.einsum('btni,nij->btnj', xb, w_a).reshape(b, t, LRU_WIDTH) + b_a)
    i = jax.nn.sigmoid(jnp.einsum('btni,nij->btnj', xb, w_i).reshape(b, t, LRU_WIDTH) + b_i)
    log_a = -LRU_C * r.astype(jnp.float32) * jax.nn.softplus(-lam.astype(jnp.float32))
    a = jnp.exp(log_a)
    u = jnp.sqrt(-jnp.expm1(2.0 * log_a)) * (i * xr).astype(jnp.float32)
    _, hs = lax.associative_scan(_lru_combine, (a, u), axis=1)
    return (hs.astype(h.dtype) * gate) @ w_out

def _normal(k, shape, fan_in):
    return jax.random.normal(k, shape, jnp.float32) * (fan_in ** -0.5)

def setup_inputs(seed: int = 0) -> dict:
    key = jax.random.key(seed)
    ks = iter(jax.random.split(key, 40))
    gain = lambda k, shape: 1.0 + 0.02 * jax.random.normal(k, shape, jnp.float32)
    small = lambda k, shape: 0.02 * jax.random.normal(k, shape, jnp.float32)
    x = jax.random.normal(next(ks), (BATCH, SEQ, D_MODEL), jnp.float32)
    meta_tokens = jax.random.normal(next(ks), (N_META, D_MODEL), jnp.float32)
    mix_pre_g = gain(next(ks), (DEPTH, D_MODEL))
    mix_post_g = gain(next(ks), (DEPTH, D_MODEL))
    mlp_pre_g = gain(next(ks), (DEPTH, D_MODEL))
    mlp_post_g = gain(next(ks), (DEPTH, D_MODEL))
    w_up = _normal(next(ks), (DEPTH, D_MODEL, D_FF), D_MODEL)
    w_down = _normal(next(ks), (DEPTH, D_FF, D_MODEL), D_FF)
    w_in = _normal(next(ks), (N_EVEN, D_MODEL, D_IN), D_MODEL)
    ssd_conv_w = _normal(next(ks), (N_EVEN, SSD_CONV, SSD_CONV_CH), SSD_CONV)
    ssd_conv_b = small(next(ks), (N_EVEN, SSD_CONV_CH))
    dt = jnp.exp(jax.random.uniform(next(ks), (N_EVEN, SSD_HEADS), jnp.float32,
                                    minval=np.log(1e-3), maxval=np.log(1e-1)))
    ssd_dt_bias = dt + jnp.log(-jnp.expm1(-dt))
    ssd_a_log = jnp.log(jax.random.uniform(next(ks), (N_EVEN, SSD_HEADS), jnp.float32, minval=1.0, maxval=16.0))
    ssd_d = 1.0 + 0.1 * jax.random.normal(next(ks), (N_EVEN, SSD_HEADS), jnp.float32)
    ssd_norm_g = gain(next(ks), (N_EVEN, SSD_D_INNER))
    mla_q_norm_g = gain(next(ks), (N_EVEN, MLA_Q_RANK))
    mla_w_q_up = _normal(next(ks), (N_EVEN, MLA_Q_RANK, MLA_HEADS * (MLA_NOPE + MLA_ROPE)), MLA_Q_RANK)
    mla_kv_norm_g = gain(next(ks), (N_EVEN, MLA_KV_RANK))
    mla_w_kv_up = _normal(next(ks), (N_EVEN, MLA_KV_RANK, MLA_HEADS * (MLA_NOPE + MLA_V)), MLA_KV_RANK)
    w_out_ab = _normal(next(ks), (N_EVEN, AB_WIDTH, D_MODEL), AB_WIDTH)
    rg_w_x = _normal(next(ks), (N_ODD, D_MODEL, LRU_WIDTH), D_MODEL)
    rg_w_y = _normal(next(ks), (N_ODD, D_MODEL, LRU_WIDTH), D_MODEL)
    rg_conv_w = _normal(next(ks), (N_ODD, LRU_CONV, LRU_WIDTH), LRU_CONV)
    rg_conv_b = small(next(ks), (N_ODD, LRU_WIDTH))
    rg_w_a = _normal(next(ks), (N_ODD, LRU_BLOCKS, LRU_BLOCK, LRU_BLOCK), LRU_BLOCK)
    rg_b_a = small(next(ks), (N_ODD, LRU_WIDTH))
    rg_w_i = _normal(next(ks), (N_ODD, LRU_BLOCKS, LRU_BLOCK, LRU_BLOCK), LRU_BLOCK)
    rg_b_i = small(next(ks), (N_ODD, LRU_WIDTH))
    a8 = jax.random.uniform(next(ks), (N_ODD, LRU_WIDTH), jnp.float32, minval=0.9, maxval=0.999)
    base = a8 ** (1.0 / LRU_C)
    rg_lambda = jnp.log(base) - jnp.log1p(-base)
    rg_w_out = _normal(next(ks), (N_ODD, LRU_WIDTH, D_MODEL), LRU_WIDTH)
    return {'x': x, 'meta_tokens': meta_tokens, 'mix_pre_g': mix_pre_g, 'mix_post_g': mix_post_g,
            'mlp_pre_g': mlp_pre_g, 'mlp_post_g': mlp_post_g, 'w_up': w_up, 'w_down': w_down,
            'w_in': w_in, 'ssd_conv_w': ssd_conv_w, 'ssd_conv_b': ssd_conv_b, 'ssd_dt_bias': ssd_dt_bias,
            'ssd_a_log': ssd_a_log, 'ssd_d': ssd_d, 'ssd_norm_g': ssd_norm_g,
            'mla_q_norm_g': mla_q_norm_g, 'mla_w_q_up': mla_w_q_up, 'mla_kv_norm_g': mla_kv_norm_g,
            'mla_w_kv_up': mla_w_kv_up, 'w_out_ab': w_out_ab, 'rg_w_x': rg_w_x, 'rg_w_y': rg_w_y,
            'rg_conv_w': rg_conv_w, 'rg_conv_b': rg_conv_b, 'rg_w_a': rg_w_a, 'rg_b_a': rg_b_a,
            'rg_w_i': rg_w_i, 'rg_b_i': rg_b_i, 'rg_lambda': rg_lambda, 'rg_w_out': rg_w_out}

def reference(x, meta_tokens, mix_pre_g, mix_post_g, mlp_pre_g, mlp_post_g, w_up, w_down,
              w_in, ssd_conv_w, ssd_conv_b, ssd_dt_bias, ssd_a_log, ssd_d, ssd_norm_g,
              mla_q_norm_g, mla_w_q_up, mla_kv_norm_g, mla_w_kv_up, w_out_ab,
              rg_w_x, rg_w_y, rg_conv_w, rg_conv_b, rg_w_a, rg_b_a, rg_w_i, rg_b_i, rg_lambda, rg_w_out):
    b = x.shape[0]
    meta = jnp.broadcast_to(meta_tokens[None].astype(x.dtype), (b, N_META, D_MODEL))
    h = jnp.concatenate([meta, x], axis=1)
    cos, sin = rope_tables(h.shape[1], MLA_ROPE)
    for layer in range(DEPTH):
        hn = rmsnorm(h, mix_pre_g[layer])
        if layer % 2 == 0:
            e = layer // 2
            m = mixer_ssd_mla(hn, w_in[e], ssd_conv_w[e], ssd_conv_b[e], ssd_dt_bias[e], ssd_a_log[e],
                              ssd_d[e], ssd_norm_g[e], mla_q_norm_g[e], mla_w_q_up[e], mla_kv_norm_g[e],
                              mla_w_kv_up[e], w_out_ab[e], cos, sin)
        else:
            o = layer // 2
            m = mixer_rglru(hn, rg_w_x[o], rg_w_y[o], rg_conv_w[o], rg_conv_b[o], rg_w_a[o], rg_b_a[o],
                            rg_w_i[o], rg_b_i[o], rg_lambda[o], rg_w_out[o])
        h = h + rmsnorm(m, mix_post_g[layer])
        hn = rmsnorm(h, mlp_pre_g[layer])
        u = jnp.square(jax.nn.relu(hn @ w_up[layer]))
        h = h + rmsnorm(u @ w_down[layer], mlp_post_g[layer])
    return h[:, N_META:]


_drawn_inputs = setup_inputs


def setup_inputs(seed=0):
    import zlib

    import numpy as np

    out = dict(_drawn_inputs(seed))
    spreads = {}
    factors = {'mix_post_g': 3.019,
     'mlp_pre_g': 8.762,
     'mlp_post_g': 3.066,
     'ssd_norm_g': 21.093,
     'mla_q_norm_g': 8.0,
     'mla_kv_norm_g': 8.0,
     'rg_b_a': 28.32,
     'rg_b_i': 8.0,
     'ssd_conv_b': 3.952}
    for name, (base, spread) in spreads.items():
        noise = np.random.default_rng([zlib.crc32(name.encode()), seed]).standard_normal(out[name].shape)
        drawn = base * np.exp(spread * noise) if base else spread * noise
        out[name] = __import__('jax').numpy.asarray(drawn.astype(out[name].dtype))
    for name, factor in factors.items():
        out[name] = (out[name] * factor).astype(out[name].dtype)
    return out
```

```python
from contextlib import ExitStack

import concourse.bass as bass
from concourse import mybir

F32 = mybir.dt.float32
F32R = mybir.dt.float32r
ACT = mybir.ActivationFunctionType
ALU = mybir.AluOpType
AX = mybir.AxisListType

P = 128
D = 1024
KT = D // P
SEQ = 512
META = 16
T = META + SEQ
HALF = T // 2
DFF = 4 * D
EPS = 1e-6

INNER = 1024
XBC = 1536
DT_COL = INNER + XBC
CQ_COL = DT_COL + 16
CKV_COL = CQ_COL + 384
KR_COL = CKV_COL + 256
HEADS = 16
NOPE, ROPE, VD = 64, 32, 64
QRANK, KVRANK = 384, 256
SCALE = float(NOPE + ROPE) ** -0.5
CHUNKS = [(0, META)] + [(META + P * c, P) for c in range(SEQ // P)]

LRU = 1280
LT = LRU // P

PACK_A = {"mix_pre_g": (0, 16), "mix_post_g": (16, 16), "mlp_pre_g": (32, 16), "mlp_post_g": (48, 16),
          "ssd_conv_w": (64, 48), "ssd_conv_b": (112, 12)}
PACK_B = {"ssd_norm_g": (0, 8), "mla_q_norm_g": (8, 3), "mla_kv_norm_g": (11, 2), "rg_conv_w": (13, 40),
          "rg_conv_b": (53, 10), "rg_b_a": (63, 10), "rg_b_i": (73, 10), "rg_lambda": (83, 10)}
ROWS_A, ROWS_B = 124, 93
CONSTS = 4 + 1 + len(PACK_A) + len(PACK_B) + 3
BEFORE = {"qn": (0, 0), "kvn": (3, 1), "yn": (5, 2), "prep0": (0, 0), "prep1": (KT, 1), "prep2": (2 * KT, 2),
          "prep3": (3 * KT, 3)}
DT_STEPS = 11

STREAM = [("win", 10, 1, 2048), ("cq", 1, 1, 2048), ("misc", 1, 5, 2048), ("ckv", 1, 1, 2048),
          ("att", 8, 13, 1280), ("wout", 8, 1, 2048), ("mlp0", 32, 1, 2048),
          ("lru", 10, 1, 2048), ("rgo", 8, 1, 1280), ("mlp1", 32, 1, 2048)]
FIRST, _b = {}, 0
for _n, _k, _, _ in STREAM:
    FIRST[_n] = _b
    _b += _k
BLOCKS = _b
_of = [row for row in STREAM for _ in range(row[1])]


def landed(b):
    return 16 * sum(_of[i][2] for i in range(b % 2, b + 1, 2))


def floats(b):
    return _of[b][3]

G_FIRST, _t = {}, 0
for _n, _k in [("win", 20), ("cq", 2), ("misc", 2), ("ckv", 2), ("wout", 8), ("mlp0", 48), ("lru", 20),
               ("rgo", 8), ("mlp1", 48)]:
    G_FIRST[_n] = _t
    _t += _k

DONE = {}
_t = 0
for _n, _k in [("win", 10), ("cq", 1), ("misc", 1), ("ckv", 1), ("att", 24), ("wout", 4), ("mlp0", 24),
               ("lru", 10), ("rgo", 0), ("mlp1", 24)]:
    DONE[_n] = _t
    _t += _k


def build(nc, A, out):
    with ExitStack() as ctx:
        def sem(name):
            return ctx.enter_context(nc.semaphore(name))

        TB = 4 * T
        base = (nc.sbuf_base + 31) // 32 * 32

        def at(name, tile, shape, dt=F32, extra=0):
            return nc.alloc_sbuf_tensor_at(name, shape, dt, offset=base + tile * TB + extra)

        H = at("h_res", 0, [P, KT, T])
        RAW = at("w_raw", 8, [P, 2, 2048])
        WHI = at("w_hi", 8, [P, 2, 2048], F32R, 16384)
        WLO = at("w_lo", 8, [P, 2, 2048], F32R, 32768)
        Z0 = 32
        RS = at("rstd", Z0, [P, T])
        SQA = at("sq_sum", Z0 + 1, [P, T])
        SQT = at("sq_tmp", Z0 + 2, [P, 2, T])
        TMP = at("tmp", Z0 + 4, [P, 2, T])
        U0 = Z0 + 6
        UHI = at("u_hi", U0, [P, 16, T], F32R)
        ULO = at("u_lo", U0 + 16, [P, 16, T], F32R)
        A0 = U0 + 32
        AHI = at("a_hi", A0, [P, KT, T], F32R)
        ALO = at("a_lo", A0 + 8, [P, KT, T], F32R)
        M0 = A0 + 16
        M = at("mix_out", M0, [P, KT, T])
        C0 = M0 + 10
        ident = at("ident", C0, [P, P])
        neg = at("neg_mask", C0, [P, P], F32, 512)
        triu = at("triu", C0, [P, P], F32, 1024)
        ones = at("ones", C0, [P, P], F32, 1536)
        CS = at("rope_cs", C0 + 1, [P, T])
        VA = at("vec_a", C0 + 2, [P, ROWS_A])
        VB = at("vec_b", C0 + 2, [P, ROWS_B], F32, 512)
        heads_in = at("heads_in", C0 + 2, [P, 2, HEADS], F32, 1024)
        expA = at("exp_a", C0 + 2, [P, HEADS], F32, 1152)
        dskip = at("d_skip", C0 + 2, [P, KT], F32, 1216)
        dtb = at("dt_bias", C0 + 2, [HEADS, 1], F32, 1248)
        cl = at("lru_c", C0 + 2, [P, LT], F32, 1280)
        nba = at("neg_b", C0 + 2, [P, 2 * LT], F32, 1344)
        LAM = at("lam_work", C0 + 2, [P, 4, LT], F32, 1440)
        assert base + (C0 + 4) * TB <= nc.sbuf_usable_end, (base, C0)
        XN = at("x_rows", U0, [P, 4, D])
        MN = at("meta_rows", U0 + 8, [META, D])
        PKA = at("pack_a", U0 + 10, [ROWS_A, P])
        PKB = at("pack_b", U0 + 10, [ROWS_B, P], F32, 512)
        C5 = at("latent_raw", U0, [P, 5, T])
        MISC = at("misc", U0 + 5, [P, T])
        CACC = at("conv_acc", U0 + 6, [P, 2, T])
        Z = at("z_gate", U0 + 8, [P, KT, T])
        XC = at("xbc_conv", U0 + 16, [P, 12, T])
        XRAW = at("conv_in", U0 + 28, [P, 2, T + 3])
        LHI = at("latent_hi", M0, [P, 5, T], F32R)
        LLO = at("latent_lo", M0 + 5, [P, 5, T], F32R)
        KRS = at("k_rope", C0 + 3, [P, T])
        DTC = at("dt_work", U0, [HEADS, 4, T])
        YT = at("ssd_y", U0 + 1, [P, KT, P])
        XS = at("ssd_chunk", U0 + 3, [P, 12, P])
        DTT = at("ssd_dt", U0 + 6, [P, 5, HEADS])
        DA = at("ssd_da", U0 + 6, [P, 5, HEADS], F32, 320)
        DTE = at("ssd_to_end", U0 + 6, [P, HEADS], F32, 640)
        CD = at("ssd_chunk_decay", U0 + 6, [P, HEADS], F32, 704)
        ACS = at("ssd_acs", U0 + 6, [P, HEADS], F32, 768)
        DAC = at("ssd_da_chunk", U0 + 6, [P, HEADS], F32, 832)
        MT = at("ssd_mt", U0 + 28, [P, HEADS, P])
        E = at("ssd_decay", A0, [P, HEADS, P])
        ER = at("ssd_exp", A0 + 4, [P, HEADS, P])
        HST = at("ssd_state", A0 + 8, [P, HEADS, VD])
        XDT = at("ssd_xdt", A0 + 10, [P, HEADS, VD])
        XDE = at("ssd_xde", A0 + 12, [P, HEADS, VD])
        BT = at("ssd_bt", A0 + 14, [P, 2, P])
        CBM = at("ssd_cb", A0 + 14, [P, 2, P], F32, 1024)
        QB = at("q_heads", A0, [P, 2, T])
        KB = at("k_heads", A0 + 2, [P, 2, T])
        VH = at("v_heads", A0 + 4, [P, 5, 2, P])
        PR = at("probs", A0 + 7, [P, 2, T])
        PTS = at("probs_t", A0 + 9, [P, 2, 5, P])
        ATT = at("att_pair", A0 + 12, [P, 2, T])
        RC = at("row_recip", A0 + 14, [VD, P])
        MX = at("row_max", A0 + 14, [P, 2, 2], F32, 512)
        GATE = at("lru_gate", U0, [P, LT, T])
        GHI = at("lru_hi", U0, [P, LT, T], F32R)
        GLO = at("lru_lo", U0 + 10, [P, LT, T], F32R)
        GWR = at("gate_w_raw", M0, [P, 2, 2, P])
        GWH = at("gate_w_hi", M0 + 1, [P, 2, 2, P], F32R)
        GWL = at("gate_w_lo", M0 + 2, [P, 2, 2, P], F32R)
        LRAW = at("lru_in", U0 + 20, [P, 2, T + 3])
        LACC = at("lru_conv", U0 + 23, [P, 2, T])
        XRH = at("lru_x_hi", U0 + 25, [P, 2, T], F32R)
        XRL = at("lru_x_lo", U0 + 27, [P, 2, T], F32R)
        RG = at("lru_r", U0 + 29, [P, T])
        IG = at("lru_i", U0 + 30, [P, T])
        TH = at("lru_tanh", U0 + 31, [P, T])
        OUTN = at("out_rows", U0, [P, 4, D])
        RP = at("rstd_post", C0 + 3, [P, T])

        PS = ctx.enter_context(nc.psum_tensor("psum", [P, 8, 512], F32))

        made = {}

        def sg(name):
            if name not in made:
                made[name] = ctx.enter_context(nc.semaphore(name))
            return made[name]

        def step(name, what):
            return sg(("pre_" if name.startswith("prep") else "norm_") + what)

        def g_tile(q, w, rows=slice(0, P)):
            return PS[rows, 2 * q:2 * q + 2, 0:w // 2]

        def two(ap):
            if len(ap.shape) == 3:
                return ap.rearrange("p o (h t) -> p (o h) t", h=2)
            return ap.rearrange("p (h t) -> p h t", h=2)

        def vec(name, j):
            if name in PACK_A:
                return VA[:, bass.ds(PACK_A[name][0] + j, 1)]
            return VB[:, bass.ds(PACK_B[name][0] + j, 1)]

        def placed(b, i, turns):
            if isinstance(i, int):
                b += 2 * i
                return (b % 2, floats(b), landed(b), b + 1) if b < BLOCKS else None
            step = landed(b + 2) - landed(b)
            for j in range(turns):
                assert landed(b + 2 * j) == landed(b) + step * j and floats(b + 2 * j) == floats(b)
            return b % 2, floats(b), i * step + landed(b), i * 2 + b + 1

        def chunk(c, it):
            return (0, META, 1) if c == 0 else (it * P + META, P, it + 2)

        def unit(n):
            t0, L = CHUNKS[n % 5]
            return t0, L, t0 + L

        block = ctx.enter_context(nc.Block())

        @block.sync
        def _(sp):
            for c in range(4):
                sp.dma_start(XN[:, c, :], A["x"][0, P * c:P * (c + 1), :]).then_inc(sg("x_landed"), 16)

            def wait_slot(b):
                sp.wait_ge(sg("w_hi_made"), b - 1)
                sp.wait_ge(sg("w_lo_made"), b - 1)

            def put(s, src, k=KT):
                m = src.shape[1]
                sp.dma_start(RAW[:, s, 0:k * m].rearrange("p (k m) -> p k m", k=k),
                             src.rearrange("(k p) m -> p k m", p=P)).then_inc(sg(f"w_landed_{s}"), 16)

            w_in = A["w_in"][0]
            for s in range(2):
                put(s, w_in[:, INNER + 256 * s:INNER + 256 * (s + 1)])
            with sp.Fori(1, 3) as i:
                for s in range(2):
                    wait_slot(i * 2 + s)
                    put(s, w_in[:, bass.ds(i * 512 + INNER + 256 * s, 256)])
            with sp.Fori(0, 2) as i:
                for s in range(2):
                    wait_slot(i * 2 + 6 + s)
                    put(s, w_in[:, bass.ds(i * 512 + 256 * s, 256)])
            wait_slot(FIRST["cq"])
            put(FIRST["cq"] % 2, w_in[:, CQ_COL:CQ_COL + 256])
            b = FIRST["misc"]
            wait_slot(b)
            slot = RAW[:, b % 2, :].rearrange("p (k m) -> p k m", k=KT)
            for dst, src, n in [(0, CQ_COL + 256, P), (P, DT_COL, HEADS), (P + 64, KR_COL, ROPE),
                                (P + 96, KR_COL + ROPE // 2, ROPE // 2), (P + 112, KR_COL, ROPE // 2)]:
                sp.dma_start(slot[:, :, dst:dst + n], w_in[:, src:src + n].rearrange("(k p) m -> p k m", p=P)
                             ).then_inc(sg(f"w_landed_{b % 2}"), 16)
            wait_slot(FIRST["ckv"])
            put(FIRST["ckv"] % 2, w_in[:, CKV_COL:CKV_COL + 256])

            wq = A["mla_w_q_up"][0].rearrange("(k p) (h c) -> p k h c", p=P, h=HEADS)
            wkv = A["mla_w_kv_up"][0].rearrange("(k p) (h c) -> p k h c", p=P, h=HEADS)

            def put_heads(s, pair):
                landed_s = sg(f"w_landed_{s}")
                q = RAW[:, s, 0:768].rearrange("p (k h c) -> p k h c", k=3, h=2)
                kv = RAW[:, s, 768:1280].rearrange("p (v k h c) -> p v k h c", v=2, k=2, h=2)
                hs = bass.ds(pair * 2, 2)
                for k in range(3):
                    sp.dma_start(q[:, k, :, 0:96], wq[:, k, hs, :]).then_inc(landed_s, 16)
                    sp.dma_start(q[:, k, :, 96:112], wq[:, k, hs, 80:96]).then_inc(landed_s, 16)
                    sp.dma_start(q[:, k, :, 112:128], wq[:, k, hs, 64:80]).then_inc(landed_s, 16)
                for k in range(2):
                    for v in range(2):
                        sp.dma_start(kv[:, v, k], wkv[:, k, hs, VD * v:VD * (v + 1)]).then_inc(landed_s, 16)

            b0 = FIRST["att"]
            with sp.Fori(0, 4) as i:
                for s in range(2):
                    wait_slot(i * 2 + b0 + s)
                    put_heads((b0 + s) % 2, i * 2 + s)

            b0 = FIRST["wout"]
            with sp.Fori(0, 4) as i:
                for s in range(2):
                    wait_slot(i * 2 + b0 + s)
                    put((b0 + s) % 2, A["w_out_ab"][0, D * s:D * (s + 1), bass.ds(i * 256, 256)])

            def mlp(layer):
                b0 = FIRST[f"mlp{layer}"]
                for f in range(2):
                    with sp.Fori(0, 4) as i:
                        for s in range(2):
                            wait_slot(i * 2 + b0 + 16 * f + s)
                            put((b0 + s) % 2, A["w_up"][layer, :, bass.ds(i * 512 + DFF // 2 * f + 256 * s, 256)])
                    with sp.Fori(0, 4) as i:
                        for s in range(2):
                            wait_slot(i * 2 + b0 + 16 * f + 8 + s)
                            r = DFF // 2 * f + D * s
                            put((b0 + s) % 2, A["w_down"][layer, r:r + D, bass.ds(i * 256, 256)])

            def put_gates(s, n):
                for g, name in enumerate(("rg_w_a", "rg_w_i")):
                    sp.dma_start(GWR[:, s, g, :], A[name][0, bass.ds(n, 1), :, :].rearrange("o i j -> (o i) j")
                                 ).then_inc(sg(f"gw_landed_{s}"), 16)

            mlp(0)
            b0 = FIRST["lru"]
            names = ("rg_w_x", "rg_w_y")
            for s in range(2):
                wait_slot(b0 + s)
                put((b0 + s) % 2, A[names[s]][0, :, 0:256])
            sp.wait_ge(sg("fuse_term"), 2 * KT)
            for s in range(2):
                put_gates(s, s)
            with sp.Fori(1, LT // 2) as i:
                for s in range(2):
                    wait_slot(i * 2 + b0 + s)
                    put((b0 + s) % 2, A[names[s]][0, :, bass.ds(i * 256, 256)])
                for s in range(2):
                    sp.wait_ge(sg("gw_hi_made"), i * 2 + s - 1)
                    sp.wait_ge(sg("gw_lo_made"), i * 2 + s - 1)
                    put_gates(s, i * 2 + s)
            b0 = FIRST["rgo"]
            with sp.Fori(0, 4) as i:
                for s in range(2):
                    wait_slot(i * 2 + b0 + s)
                    put((b0 + s) % 2, A["rg_w_out"][0, :, bass.ds(i * 256 + P * s, P)], k=LT)
            mlp(1)
            for c in range(4):
                sp.wait_ge(sg("out_rows_act"), c + 1)
                sp.wait_ge(sg("out_rows_dve"), c + 1)
                sp.dma_start(out[0, P * c:P * (c + 1), :], OUTN[:, c, :]).then_inc(sg("out_stored"), 16)
            sp.wait_ge(sg("out_stored"), 64)

        @block.gpsimd
        def _(pool):
            pool.memset(ones[:, :], 1.0).then_inc(sg("ones_ready"), 1)
            pool.memset(SQA[:, :], 0.0).then_inc(sg("sqa_zero"), 1)
            pool.sem_inc(sg("m_summed"), 2)

            def sums(first, n, c0):
                with pool.Fori(0, n // 2) as i:
                    for s in range(2):
                        pool.wait_ge(sg("m_squared"), i * 2 + first + s + 1)
                        pool.wait_ge(sg("m_summed"), i * 2 + first + s + 2)
                        pool.tensor_tensor(SQA[:, c0:T], SQA[:, c0:T], SQT[:, s, c0:T], ALU.add
                                           ).then_inc(sg("m_summed"), 1)

            def residual(u, c0):
                for k in range(KT):
                    pool.wait_ge(sg("fuse_term"), KT * u + k + 1)
                    pool.tensor_tensor(H[:, k, c0:T], H[:, k, c0:T], TMP[:, k % 2, c0:T], ALU.add
                                       ).then_inc(sg("fuse_h"), 1)
                if u < 3:
                    pool.memset(SQA[:, :], 0.0).then_inc(sg("sqa_zero"), 1)
                    pool.wait_ge(sg("sqa_zero"), u + 2)

            def squares_up(first, c0):
                with pool.Fori(0, 8) as i:
                    for s in range(2):
                        pool.wait_ge(sg("g_evac"), i * 2 + first + s + 3)
                        pool.tensor_tensor(SQT[:, s, c0:T], TMP[:, s, c0:T], TMP[:, s, c0:T], ALU.mult
                                           ).then_inc(sg("up_square"), 1)

            def skip_term(c, it=None):
                t0, L, v = chunk(c, it)
                pool.wait_ge(sg("ssd_staged"), v)
                if c > 0:
                    pool.wait_ge(sg("ssd_y_done"), v - 1)
                pool.tensor_tensor(YT[:, :, 0:L], XS[:, 0:KT, 0:L],
                                   dskip[:, :].unsqueeze(2).to_broadcast([P, KT, L]), ALU.mult
                                   ).then_inc(sg("ssd_skip"), 1)

            pool.wait_ge(sg("sqa_zero"), 1)
            pool.memset(XRAW[:, :, 0:3], 0.0).then_inc(sg("halo_ready"), 1)
            pool.wait_ge(sg("d_skip_ready"), 2)
            skip_term(0)
            with pool.Fori(0, 4) as it:
                skip_term(1, it)

            pool.wait_ge(sg("ssd_y_done"), 5)
            pool.wait_ge(sg("ssd_state"), 5)
            pool.memset(PR[:, :, :], 0.0).then_inc(sg("v_ones"), 1)
            pool.memset(VH[:, :, :, VD:P], 1.0).then_inc(sg("v_ones"), 1)

            sums(0, 8, 0)
            residual(0, 0)
            for f in range(2):
                squares_up(G_FIRST["mlp0"] + 24 * f, 0)
            sums(8, 8, 0)
            residual(1, 0)
            pool.memset(LRAW[:, :, 0:3], 0.0).then_inc(sg("halo_ready"), 1)

            one = ones[:, 0:1].to_broadcast([P, T])
            with pool.Fori(0, LT // 2) as i:
                for s in range(2):
                    n = i * 2 + s
                    pool.wait_ge(sg("lru_er"), n + 1)
                    pool.tensor_tensor(RG[:, :], RG[:, :], one, ALU.add).then_inc(sg("lru_er1"), 1)
                    pool.wait_ge(sg("lru_ei"), n + 2)
                    pool.tensor_tensor(IG[:, :], IG[:, :], one, ALU.add).then_inc(sg("lru_ei1"), 1)
                    pool.wait_ge(sg("lru_th"), n + 1)
                    pool.tensor_tensor(TMP[:, 0, :], one, TH[:, :], ALU.subtract
                                       ).then_inc(sg("lru_den"), 1)
                    pool.wait_ge(sg("lru_i"), n + 1)
                    pool.tensor_tensor(IG[:, :], IG[:, :], LACC[:, s, :], ALU.mult).then_inc(sg("lru_ix"), 1)
            sums(16, 8, META)
            residual(2, META)
            for f in range(2):
                squares_up(G_FIRST["mlp1"] + 24 * f, META)
            sums(24, 8, META)
            residual(3, META)

        @block.scalar
        def _(act):
            landed_c = sg("consts_landed")
            for name, dst in (("c_ident", ident), ("c_neg", neg), ("c_triu", triu), ("c_cs", CS)):
                act.dma_start(dst[:, :], A[name]).then_inc(landed_c, 16)
            act.dma_start(MN[:, :], A["meta_tokens"]).then_inc(landed_c, 16)
            for pack, dst in ((PACK_A, PKA), (PACK_B, PKB)):
                for name, (row, n) in pack.items():
                    src = A[name]
                    src = src.rearrange("a b c -> (a b c)") if len(src.shape) == 3 else src.rearrange("a b -> (a b)")
                    act.dma_start(dst[row:row + n, :], src.rearrange("(n p) -> n p", p=P)).then_inc(landed_c, 16)
            act.dma_start(heads_in[:, 0, :], A["ssd_a_log"].to_broadcast([P, HEADS])).then_inc(landed_c, 16)
            act.dma_start(heads_in[:, 1, :], A["ssd_d"].to_broadcast([P, HEADS])).then_inc(landed_c, 16)
            act.dma_start(dtb[:, :], A["ssd_dt_bias"].rearrange("a b -> b a"), allow_slow_non_contiguous=True
                          ).then_inc(landed_c, 16)

            def split(b, i=0, turns=1):
                at_b = placed(b, i, turns)
                if at_b:
                    s, n, landed_at, free_at = at_b
                    act.wait_ge(sg(f"w_landed_{s}"), landed_at)
                    act.wait_ge(sg("w_used"), free_at)
                    act.activation(WHI[:, s, 0:n], RAW[:, s, 0:n], ACT.Copy).then_inc(sg("w_hi_made"), 1)

            for tau in range(5):
                t0, L = CHUNKS[tau]
                act.wait_ge(sg("x_turned"), 2 * tau + 1)
                act.copy(H[:, 0:4, t0:t0 + L], PS[:, 4 + 2 * tau % 4, :].rearrange("p (k t) -> p k t", k=4)[:, :, 0:L]
                         ).then_inc(sg("x_in_act"), 1)
            split(0)
            split(1)

            def prep(u, name, layer, c0, after):
                name_u, t = f"prep{u}", KT * u
                for k in range(KT):
                    if after:
                        act.wait_ge(sg("fuse_h"), t - KT + k + 1)
                    act.activation(AHI[:, k, c0:T], H[:, k, c0:T], ACT.Identity, scale=vec(name, KT * layer + k)
                                   ).then_inc(step(name_u, "hi"), 1)
                    if k >= 2:
                        act.wait_ge(step(name_u, "ss"), t + k - 1)
                    act.activation(SQT[:, k % 2, c0:T], H[:, k, c0:T], ACT.Square).then_inc(step(name_u, "sq"), 1)
                act.wait_ge(step(name_u, "mean"), u + 1)
                act.activation(RS[:, c0:T], RS[:, c0:T], ACT.Sqrt).then_inc(step(name_u, "root"), 1)

            act.wait_ge(sg("vecs_ready"), 2)
            act.wait_ge(sg("x_in_act"), 5)
            act.wait_ge(sg("x_in_dve"), 5)
            prep(0, "mix_pre_g", 0, 0, False)

            act.wait_ge(sg("halo_ready"), 1)

            def conv_tile(m, q):
                act.wait_ge(sg("g_evac"), m + 3)
                act.activation(CACC[:, q, :], XRAW[:, q, 3:T + 3], ACT.Identity, scale=vec("ssd_conv_w", m + 36),
                               bias=vec("ssd_conv_b", m)).then_inc(sg("conv_tap3"), 1)
                act.wait_ge(sg("conv_tap2"), m + 1)
                act.activation(XC[:, bass.ds(m, 1), :], CACC[:, q:q + 1, :], ACT.Silu).then_inc(sg("xbc_ready"), 1)

            with act.Fori(0, 3) as i:
                for s in range(2):
                    conv_tile(i * 4 + 2 * s, 0)
                    split(s + 2, i, 3)
                    conv_tile(i * 4 + 2 * s + 1, 1)
            with act.Fori(0, 2) as i:
                for s in range(2):
                    for q in range(2):
                        act.wait_ge(sg("g_evac"), i * 4 + 2 * s + q + 12 + 3)
                        zt = Z[:, bass.ds(i * 4 + 2 * s + q, 1), :]
                        act.activation(zt, zt, ACT.Silu).then_inc(sg("z_ready"), 1)
                        if q == 0:
                            split(s + 8, i, 2)
            for b in range(12, 15):
                split(b)

            def norm_split(name, src, n, dst):
                t, u = BEFORE[name]
                for k in range(n):
                    if k >= 2:
                        act.wait_ge(step(name, "ss"), t + k - 1)
                    act.activation(SQT[:, k % 2, :], src(k), ACT.Square).then_inc(step(name, "sq"), 1)
                act.wait_ge(step(name, "mean"), u + 1)
                act.activation(RS[:, :], RS[:, :], ACT.Sqrt).then_inc(step(name, "root"), 1)
                for k in range(n):
                    act.wait_ge(step(name, "full"), t + k + 1)
                    act.activation(dst(k), TMP[:, k % 2, :], ACT.Copy).then_inc(step(name, "hi"), 1)

            act.wait_ge(sg("g_evac"), 26 + 2)
            norm_split("qn", lambda k: C5[:, k, :], 3, lambda k: LHI[:, k, :])
            norm_split("kvn", lambda k: C5[:, 3 + k, :], 2, lambda k: LHI[:, 3 + k, :])
            act.wait_ge(sg("k_rope_terms"), 1)
            act.copy(TMP[64:96, 1, :], TMP[96:128, 0, :]).then_inc(sg("k_rope_moved"), 1)

            act.wait_ge(landed_c, 16 * CONSTS)
            act.activation(expA[:, :], heads_in[:, 0, :], ACT.Exp).then_inc(sg("exp_a"), 1)

            def softplus_parts(name, x):
                act.wait_ge(sg(f"{name}_step"), 2)
                act.activation(x[:, 2, :], x[:, 1, :], ACT.Exp).then_inc(sg(f"{name}_act"), 1)
                act.wait_ge(sg(f"{name}_step"), 3)
                act.activation(x[:, 3, :], x[:, 1, :], ACT.Ln).then_inc(sg(f"{name}_act"), 1)

            softplus_parts("dt", DTC)

            def ssd(c, it=None):
                t0, L, v = chunk(c, it)
                if c > 0:
                    act.wait_ge(sg("ssd_y_mm"), v - 1)
                    act.wait_ge(sg("ssd_y_done"), v - 1)
                act.copy(XS[:, :, 0:L], XC[:, :, bass.ds(t0, L)]).then_inc(sg("ssd_staged"), 1)
                act.wait_ge(sg("ssd_bt_mm"), v)
                act.copy(BT[0:L, :, :], PS[0:L, 7, 0:256].rearrange("p (g n) -> p g n", g=2)).then_inc(sg("ssd_bt"), 1)
                act.wait_ge(sg("ssd_e_arg"), v)
                act.activation(ER[:, :, 0:L].rearrange("p (b h) l -> p b h l", b=4),
                               PS[:, 0:4, :].rearrange("p b (h l) -> p b h l", h=4)[:, :, :, 0:L], ACT.Exp
                               ).then_inc(sg("ssd_er"), 1)
                act.wait_ge(sg("ssd_to_end_arg"), v)
                act.activation(DTE[0:L, :], DTE[0:L, :], ACT.Exp).then_inc(sg("ssd_to_end"), 1)
                act.wait_ge(sg("ssd_e_min"), v)
                act.activation(E[0:L, :, 0:L], E[0:L, :, 0:L], ACT.Exp).then_inc(sg("ssd_e"), 1)

            act.wait_ge(sg("xbc_ready"), 12)
            act.wait_ge(sg("k_rope"), 1)
            act.wait_ge(sg("dt_turned"), 1)
            ssd(0)
            with act.Fori(0, 4) as it:
                ssd(1, it)
            act.wait_ge(sg("ssd_y_done"), 5)
            norm_split("yn", lambda k: Z[:, k, :], KT, lambda k: UHI[:, k, :])

            for h in range(2):
                for rows in (slice(64, 96), slice(96, 128)):
                    act.copy(KB[rows, h, :], KRS[64:96, :]).then_inc(sg("k_rope_placed"), 1)
            act.sem_inc(sg("p_ready"), 2)
            act.sem_inc(sg("pt_ready"), 1)

            def turn_out(u, n):
                t0, L, _ = unit(n)
                act.wait_ge(sg("pt_mm"), u + n + 1)
                if n % 5:
                    act.copy(PTS[:, n % 2, 1:n % 5 + 1, 0:L],
                             PS[:, 6, :].rearrange("p (j l) -> p j l", j=4)[:, 0:n % 5, 0:L]).then_inc(sg("pt_part"), 1)
                act.copy(PTS[0:META, n % 2, 0, 0:L], PS[0:META, n % 2, 0:L]).then_inc(sg("pt_ready"), 1)

            def attend(i, s):
                pair, u = i * 2 + s, i * 20 + 10 * s
                act.wait_ge(sg("tile_done"), pair * 3 + DONE["att"] + 3)
                act.copy(two(KB[0:64, 0, :]), g_tile(0, T, slice(0, 64))).then_inc(sg("k_first"), 1)
                act.copy(two(KB[0:64, 1, :]), g_tile(0, T, slice(64, 128))).then_inc(sg("k_ready"), 1)
                for n in range(10):
                    if n:
                        turn_out(u, n - 1)
                    _, L, w = unit(n)
                    act.wait_ge(sg("neg_max"), u + n + 1)
                    act.activation(PR[0:L, n % 2, 0:w], PS[0:L, 2 + 2 * (n % 2):4 + 2 * (n % 2), :].rearrange(
                        "p b t -> p (b t)")[:, 0:w], ACT.Exp, bias=MX[0:L, n % 2, 1:2], scale=SCALE
                                   ).then_inc(sg("p_ready"), 1)
                    if n == 1:
                        split(FIRST["att"] + s + 2, i, 3)
                turn_out(u, 9)
                act.wait_ge(sg("o_done"), u + 11)
                act.activation(UHI[:, bass.ds(pair + KT, 1), :], ATT[:, s:s + 1, :], ACT.Copy
                               ).then_inc(sg("att_hi"), 1)

            with act.Fori(0, 3) as i:
                for s in range(2):
                    attend(i, s)
            for s in range(2):
                attend(3, s)

            def square(t, m, s, c0, i):
                act.wait_ge(sg("g_evac"), i * 2 + t + s + 3)
                act.wait_ge(sg("m_summed"), i * 2 + m + s + 1)
                act.activation(SQT[:, s:s + 1, c0:T], M[:, bass.ds(i * 2 + s, 1), c0:T], ACT.Square
                               ).then_inc(sg("m_squared"), 1)

            def outputs(b, t, m, c0, uniform):
                n = 4 if uniform else 3

                def turn(i):
                    for s in range(2):
                        split(b + 2 + s, i, n)
                        square(t, m, s, c0, i)
                with act.Fori(0, n) as i:
                    turn(i)
                if not uniform:
                    turn(3)

            def post_root(u, c0):
                act.wait_ge(sg("fuse_mean"), u + 1)
                act.activation(RP[:, c0:T], RP[:, c0:T], ACT.Sqrt).then_inc(sg("fuse_root"), 1)

            def mlp(layer, c0):
                b0, t0 = FIRST[f"mlp{layer}"], G_FIRST[f"mlp{layer}"]
                for f in range(2):
                    with act.Fori(0, 4) as i:
                        for s in range(2):
                            for q in range(2):
                                n = i * 4 + 2 * s + q
                                act.wait_ge(sg("g_evac"), n + t0 + 24 * f + 3)
                                act.activation(UHI[:, bass.ds(n, 1), c0:T], TMP[:, q:q + 1, c0:T], ACT.Square
                                               ).then_inc(sg("up_hi"), 1)
                                if q == 0:
                                    split(b0 + 16 * f + 2 + s, i, 4)
                    if f == 0:
                        with act.Fori(0, 4) as i:
                            for s in range(2):
                                split(b0 + 8 + 2 + s, i, 4)
                outputs(b0 + 24, t0 + 40, 8 + 16 * layer, c0, layer == 0)

            outputs(FIRST["wout"], G_FIRST["wout"], 0, 0, True)
            post_root(0, 0)
            prep(1, "mlp_pre_g", 0, 0, True)
            mlp(0, 0)
            post_root(1, 0)
            prep(2, "mix_pre_g", 1, 0, True)
            softplus_parts("lam", LAM)
            act.sem_inc(sg("lru_ei"), 1)
            act.wait_ge(sg("halo_ready"), 2)

            def lru_input(i, s):
                b0, t0 = FIRST["lru"], G_FIRST["lru"]
                act.wait_ge(sg(f"gw_landed_{s}"), i * 32 + 32)
                act.activation(GWH[:, s, :, :], GWR[:, s, :, :], ACT.Copy).then_inc(sg("gw_hi_made"), 1)
                act.wait_ge(sg("g_evac"), i * 4 + s + t0 + 3)
                act.activation(LACC[:, s, :], LRAW[:, s, 3:T + 3], ACT.Identity, scale=vec("rg_conv_w", i * 2 + s + 30),
                               bias=vec("rg_conv_b", i * 2 + s)).then_inc(sg("lconv_tap3"), 1)
                act.wait_ge(sg("lconv_tap2"), i * 2 + s + 1)
                act.activation(XRH[:, s, :], LACC[:, s, :], ACT.Copy).then_inc(sg("xr_hi"), 1)

            def lru_gates(i, s):
                n = i * 2 + s
                act.wait_ge(sg("gates_mm"), n + 1)
                act.activation(two(RG[:, :]), g_tile(2, T), ACT.Exp, scale=-1.0, bias=nba[:, bass.ds(n, 1)]
                               ).then_inc(sg("lru_er"), 1)
                act.activation(two(IG[:, :]), g_tile(3, T), ACT.Exp, scale=-1.0, bias=nba[:, bass.ds(n + LT, 1)]
                               ).then_inc(sg("lru_ei"), 1)
                act.wait_ge(sg("lru_r"), n + 1)
                act.activation(TH[:, :], RG[:, :], ACT.Tanh, scale=cl[:, bass.ds(n, 1)]).then_inc(sg("lru_th"), 1)
                act.activation(RG[:, :], RG[:, :], ACT.Exp, scale=cl[:, bass.ds(n, 1)]).then_inc(sg("lru_a"), 1)
                act.wait_ge(sg("lru_q"), n + 1)
                act.activation(TH[:, :], TH[:, :], ACT.Sqrt).then_inc(sg("lru_root"), 1)
                act.wait_ge(sg("lru_gated"), n + 1)
                act.activation(GHI[:, :, :].rearrange("p n t -> p (n t)")[:, bass.ds(i * (2 * T) + s * T, T)], SQT[:, 1, :],
                               ACT.Copy).then_inc(sg("lru_hi"), 1)

            def lru(i):
                b0, t0 = FIRST["lru"], G_FIRST["lru"]
                for s in range(2):
                    lru_input(i, s)
                split(b0 + 2, i, 4)
                for s in range(2):
                    if s == 1:
                        split(b0 + 3, i, 4)
                    act.wait_ge(sg("g_evac"), i * 4 + s + 2 + t0 + 3)
                    gt = GATE[:, bass.ds(i * 2 + s, 1), :]
                    act.activation(gt, gt, ACT.Gelu_apprx_tanh).then_inc(sg("gelu_ready"), 1)
                    lru_gates(i, s)

            with act.Fori(0, LT // 2 - 1) as i:
                lru(i)
            lru(LT // 2 - 1)
            outputs(FIRST["rgo"], G_FIRST["rgo"], 16, META, False)
            post_root(2, META)
            prep(3, "mlp_pre_g", 1, META, True)
            mlp(1, META)
            post_root(3, META)
            for c in range(4):
                act.wait_ge(sg("out_turned"), 2 * c + 1)
                act.copy(OUTN[:, c, 0:512], PS[:, 4 + 2 * c % 4, :]).then_inc(sg("out_rows_act"), 1)

        @block.tensor
        def _(pe):
            pe.sem_inc(sg("w_used"), 2)

            pe.wait_ge(sg("consts_landed"), 16 * CONSTS)
            for tau in range(5):
                t0, L = CHUNKS[tau]
                if tau:
                    pe.wait_ge(sg("x_landed"), 16 * 4)
                for j in range(2):
                    if tau >= 2:
                        pe.wait_ge(sg("x_in_dve" if j else "x_in_act"), tau - 1)
                    for k in range(4):
                        cols = slice(P * (4 * j + k), P * (4 * j + k + 1))
                        src = XN[:, tau - 1, cols] if tau else MN[:, cols]
                        mm = pe.transpose(PS[:, 4 + (2 * tau + j) % 4, P * k:P * k + L], src, ident[0:L, 0:L])
                    mm.then_inc(sg("x_turned"), 1)
            pe.transpose(PS[:, 0, 0:ROWS_A], PKA[:, :], ident[0:ROWS_A, 0:ROWS_A]).then_inc(sg("vecs_turned"), 1)
            pe.transpose(PS[:, 1, 0:ROWS_B], PKB[:, :], ident[0:ROWS_B, 0:ROWS_B]).then_inc(sg("vecs_turned"), 1)
            pe.wait_ge(sg("ones_ready"), 1)

            def sum_squares(name, n, c0=0):
                w = (T - c0) // 2
                t, _ = BEFORE[name]
                for k in range(n):
                    pe.wait_ge(step(name, "sq"), t + k + 1)
                    for h in range(2):
                        mm = pe.matmul(PS[:, 4 + h, 0:w], ones[:, :], SQT[:, k % 2, c0 + h * w:c0 + (h + 1) * w],
                                       start=(k == 0), stop=(k == n - 1))
                    mm.then_inc(step(name, "ss"), 1)

            def product(q, ks, weight, x, c0=0, first=True, last=True, banks=None):
                w = (T - c0) // 2
                for k in ks:
                    (whi, wlo), (xhi, xlo) = weight(k), x(k)
                    for p, (a, b) in enumerate(((whi, xhi), (whi, xlo), (wlo, xhi))):
                        for h in range(2):
                            mm = pe.matmul(PS[:, 2 * q + h, 0:w], a, b[:, c0 + h * w:c0 + (h + 1) * w],
                                           start=(first and k == ks[0] and p == 0),
                                           stop=(last and k == ks[-1] and p == 2))
                return mm

            def take(b, i=0):
                pe.wait_ge(sg("w_hi_made"), i * 2 + b + 1)
                pe.wait_ge(sg("w_lo_made"), i * 2 + b + 1)

            def weights(s, m, width=256, ks=KT, base=0):
                def get(k):
                    c = base + k % ks * width + m * P
                    return WHI[:, s, c:c + P], WLO[:, s, c:c + P]
                return get

            def stream_of(hi, lo, base=0):
                return lambda k: (hi[:, base + k, :], lo[:, base + k, :])

            normed = stream_of(AHI, ALO)

            def two_tiles(b, t, i=0, c0=0, per=4):
                take(b, i)
                pe.wait_ge(sg("g_evac"), i * per + t + 1)
                product(0, range(KT), weights(b % 2, 0), normed, c0).then_inc(sg("tile_done"), 1)
                pe.wait_ge(sg("g_evac"), i * per + t + 2)
                product(1, range(KT), weights(b % 2, 1), normed, c0).then_inc(sg("w_used"), 1)

            sum_squares("prep0", KT)
            pe.wait_ge(step("prep0", "lo"), KT)
            with pe.Fori(0, 5) as i:
                for s in range(2):
                    two_tiles(s, 2 * s, i)
            for name in ("cq", "misc", "ckv"):
                two_tiles(FIRST[name], G_FIRST[name])
            sum_squares("qn", 3)
            pe.wait_ge(step("qn", "root"), 1)
            sum_squares("kvn", 2)

            pe.wait_ge(sg("dt_step"), DT_STEPS)
            pe.wait_ge(step("kvn", "root"), 2)
            for tau in range(5):
                t0, L = CHUNKS[tau]
                mm = pe.transpose(PS[0:L, 7, HEADS * tau:HEADS * (tau + 1)], DTC[:, 0, t0:t0 + L],
                                  ident[0:HEADS, 0:HEADS])
            mm.then_inc(sg("dt_turned"), 1)

            def ssd(c, it=None):
                t0, L, v = chunk(c, it)
                pe.wait_ge(sg("ssd_staged"), v)
                pe.wait_ge(sg("ssd_da_staged"), v)
                if c > 0:
                    pe.wait_ge(sg("ssd_y_out"), v - 1)
                    pe.wait_ge(sg("ssd_state"), v - 1)
                pe.matmul(PS[0:L, 6, 0:HEADS], triu[0:L, 0:L], DAC[0:L, :], start=True, stop=True)
                for g in range(2):
                    mm = pe.matmul(PS[0:L, 6, P + P * g:P + P * g + L], XS[:, 8 + g, 0:L], XS[:, 10 + g, 0:L],
                                   start=True, stop=True)
                mm.then_inc(sg("ssd_cb_mm"), 1)
                for g in range(2):
                    mm = pe.transpose(PS[0:L, 7, P * g:P * (g + 1)], XS[:, 8 + g, 0:L], ident[:, :])
                mm.then_inc(sg("ssd_bt_mm"), 1)
                if c > 0:
                    pe.wait_ge(sg("ssd_er"), v - 1)
                for h in range(HEADS):
                    mm = pe.matmul(PS[:, h // 4, P * (h % 4):P * (h % 4) + L],
                                   DAC[0:L, h:h + 1].to_broadcast([L, P]), triu[0:L, 0:L], start=True, stop=True)
                mm.then_inc(sg("ssd_r_mm"), 1)
                for j in range(KT):
                    mm = pe.transpose(PS[0:L, 4 + j // 4, P * (j % 4):P * (j % 4 + 1)], XS[:, j, 0:L], ident[:, :])
                mm.then_inc(sg("ssd_x_turned"), 1)
                for name in ("ssd_mt", "ssd_xdt", "ssd_c_decayed", "ssd_bt", "ssd_cb"):
                    pe.wait_ge(sg(name), v)
                for h in range(HEADS):
                    j = h // 2
                    o = PS[64 * (h % 2):64 * (h % 2 + 1), 6 + j // 4, P * (j % 4):P * (j % 4) + L]
                    mm = pe.matmul(o, XDT[0:L, h, :], MT[0:L, h, 0:L], start=True, stop=(c == 0))
                    if c > 0:
                        mm = pe.matmul(o, HST[:, h, :], ER[:, h, 0:L], start=False, stop=True)
                mm.then_inc(sg("ssd_y_mm"), 1)
                pe.wait_ge(sg("ssd_xde"), v)
                for g in range(2):
                    mm = pe.matmul(PS[:, 4 + g, :], BT[0:L, g, :], XDE[0:L, 8 * g:8 * g + 8, :],
                                   start=True, stop=True)
                mm.then_inc(sg("ssd_s_mm"), 1)

            ssd(0)
            with pe.Fori(0, 4) as it:
                ssd(1, it)
            pe.wait_ge(sg("ssd_state"), 5)
            pe.wait_ge(sg("ssd_y_out"), 5)
            sum_squares("yn", KT)

            latent = stream_of(LHI, LLO)
            latent_kv = stream_of(LHI, LLO, 3)
            pe.wait_ge(step("kvn", "lo"), 5)
            pe.wait_ge(sg("k_rope_placed"), 4)
            pe.wait_ge(sg("v_ones"), 2)

            def scores(i, s, n):
                t0, L, w = unit(n)
                u = i * 20 + 10 * s + n
                if n % 5 == 0:
                    pe.wait_ge(sg("q_ready"), i * 4 + 2 * s + n // 5 + 1)
                if n == 0:
                    pe.wait_ge(sg("k_ready"), i * 2 + s + 1)
                pe.wait_ge(sg("p_ready"), u + 1)
                for a in range(0, w, 512):
                    e = min(w, a + 512)
                    mm = pe.matmul(PS[0:L, 2 + 2 * (n % 2) + a // 512, 0:e - a], QB[:, n // 5, t0:t0 + L],
                                   KB[:, n // 5, a:e], start=True, stop=True)
                mm.then_inc(sg("s_mm"), 1)

            def turn(i, s, n):
                _, L, _ = unit(n)
                u = i * 20 + 10 * s + n
                pe.wait_ge(sg("p_ready"), u + 3)
                pe.wait_ge(sg("pt_ready"), u + 1)
                if n == 0:
                    pe.wait_ge(sg("v_ready"), i * 2 + s + 1)
                m = META if n % 5 else P
                mm = pe.matmul(PS[0:m, n % 2, 0:L], PR[0:L, n % 2, 0:m], ident[0:L, 0:L], start=True, stop=True)
                for j in range(n % 5):
                    mm = pe.transpose(PS[:, 6, P * j:P * j + L], PR[0:L, n % 2, META + P * j:META + P * (j + 1)],
                                      ident[0:L, 0:L])
                mm.then_inc(sg("pt_mm"), 1)

            def values(i, s, n):
                _, L, _ = unit(n)
                u = i * 20 + 10 * s + n
                pe.wait_ge(sg("pt_ready"), u + 2)
                pe.wait_ge(sg("o_done"), u + 1)
                for j in range(n % 5 + 1):
                    rows = P if j else META
                    mm = pe.matmul(PS[:, 7, 0:L], VH[0:rows, j, n // 5, :], PTS[0:rows, n % 2, j, 0:L],
                                   start=(j == 0), stop=(j == n % 5))
                mm.then_inc(sg("o_mm"), 1)

            def attend(i, s):
                b = FIRST["att"] + s
                take(b, i)
                w = b % 2
                for h in range(2):
                    if h == 0:
                        pe.wait_ge(sg("pt_ready"), i * 20 + 10 * s + 1)
                    else:
                        pe.wait_ge(sg("q_ready"), i * 4 + 2 * s + 1)
                    product(0, range(3), weights(w, h), latent).then_inc(sg("tile_done"), 1)
                pe.wait_ge(sg("q_ready"), i * 4 + 2 * s + 2)
                product(0, range(2), weights(w, 0, width=P, base=768), latent_kv).then_inc(sg("tile_done"), 1)
                pe.wait_ge(sg("k_ready"), i * 2 + s + 1)
                for j in (1, 2, 3, 4, 0):
                    t0 = CHUNKS[j][0]
                    o = PS[:, 0, P * (j - 1):P * j] if j else PS[:, 1, 0:P]
                    for k in range(2):
                        (whi, wlo), (xhi, xlo) = weights(w, 0, width=P, base=1024)(k), latent_kv(k)
                        for p, (a, x) in enumerate(((whi, xhi), (whi, xlo), (wlo, xhi))):
                            mm = pe.matmul(o, x[:, t0:t0 + P], a, start=(k == 0 and p == 0), stop=(k == 1 and p == 2))
                mm.then_inc(sg("w_used"), 1)
                for n in range(12):
                    if n < 10:
                        scores(i, s, n)
                    if 1 <= n < 11:
                        turn(i, s, n - 1)
                    if n >= 2:
                        values(i, s, n - 2)

            with pe.Fori(0, 4) as i:
                for s in range(2):
                    attend(i, s)

            pe.wait_ge(step("yn", "lo"), 5 + KT)
            pe.wait_ge(sg("att_hi"), 8)
            pe.wait_ge(sg("att_lo"), 8)

            def down(b, t, c0, i):
                for s in range(2):
                    take(b + s, i)
                    x = stream_of(UHI, ULO, KT * s)
                    for q in range(2):
                        if s == 0:
                            pe.wait_ge(sg("g_evac"), i * 2 + t + q + 1)
                        mm = product(q, range(KT), weights((b + s) % 2, q), x, c0, first=(s == 0), last=(s == 1))
                        if q == 1:
                            mm.then_inc(sg("w_used"), 1)
                        elif s == 1:
                            mm.then_inc(sg("tile_done"), 1)

            def post_sum(u, c0):
                w = (T - c0) // 2
                pe.wait_ge(sg("m_summed"), 8 * (u + 1) + 2)
                for h in range(2):
                    mm = pe.matmul(PS[:, 4 + h, 0:w], ones[:, :], SQA[:, c0 + h * w:c0 + (h + 1) * w],
                                   start=True, stop=True)
                mm.then_inc(sg("fuse_ss"), 1)

            def mlp(layer, c0):
                b0, t0 = FIRST[f"mlp{layer}"], G_FIRST[f"mlp{layer}"]
                for f in range(2):
                    with pe.Fori(0, 4) as i:
                        for s in range(2):
                            two_tiles(b0 + 16 * f + s, t0 + 24 * f + 2 * s, i, c0)
                    pe.wait_ge(sg("up_hi"), 32 * layer + 16 * (f + 1))
                    pe.wait_ge(sg("up_lo"), 32 * layer + 16 * (f + 1))
                    with pe.Fori(0, 4) as i:
                        down(b0 + 16 * f + 8, t0 + 24 * f + 16, c0, i)

            with pe.Fori(0, 4) as i:
                down(FIRST["wout"], G_FIRST["wout"], 0, i)
            post_sum(0, 0)
            pe.wait_ge(sg("fuse_root"), 1)
            sum_squares("prep1", KT)
            pe.wait_ge(step("prep1", "lo"), 2 * KT)
            mlp(0, 0)
            post_sum(1, 0)
            pe.wait_ge(sg("fuse_root"), 2)
            sum_squares("prep2", KT)
            pe.wait_ge(step("prep2", "lo"), 3 * KT)
            pe.wait_ge(step("prep2", "root"), 3)

            b0, t0 = FIRST["lru"], G_FIRST["lru"]
            with pe.Fori(0, LT // 2) as i:
                two_tiles(b0, t0, i)
                take(b0 + 1, i)
                for s in range(2):
                    pe.wait_ge(sg("g_evac"), i * 4 + t0 + 2 + s + 1)
                    mm = product(s, range(KT), weights((b0 + 1) % 2, s), normed)
                    mm.then_inc(sg("w_used" if s else "tile_done"), 1)
                    n = i * 2 + s
                    pe.wait_ge(sg("xr_hi"), n + 1)
                    pe.wait_ge(sg("xr_lo"), n + 1)
                    pe.wait_ge(sg("gw_hi_made"), n + 1)
                    pe.wait_ge(sg("gw_lo_made"), n + 1)
                    pe.wait_ge(sg("lru_ei"), n + 1)
                    for g in range(2):
                        mm = product(2 + g, [0], lambda k: (GWH[:, s, g, :], GWL[:, s, g, :]),
                                     lambda k: (XRH[:, s, :], XRL[:, s, :]))
                    mm.then_inc(sg("gates_mm"), 1)
            pe.wait_ge(sg("lru_hi"), LT)
            pe.wait_ge(sg("lru_lo"), LT)
            with pe.Fori(0, 4) as i:
                for s in range(2):
                    b = FIRST["rgo"] + s
                    take(b, i)
                    pe.wait_ge(sg("g_evac"), i * 2 + G_FIRST["rgo"] + s + 1)
                    product(s, range(LT), weights(b % 2, 0, width=P, ks=LT), stream_of(GHI, GLO), META
                            ).then_inc(sg("w_used"), 1)
            post_sum(2, META)
            pe.wait_ge(sg("fuse_root"), 3)
            sum_squares("prep3", KT, META)
            pe.wait_ge(step("prep3", "lo"), 4 * KT)
            mlp(1, META)
            post_sum(3, META)
            pe.wait_ge(sg("fuse_root"), 4)

            for c in range(4):
                for j in range(2):
                    if c == 0 and j == 0:
                        pe.wait_ge(sg("fuse_h"), 4 * KT)
                    if c >= 2:
                        pe.wait_ge(sg("out_rows_dve" if j else "out_rows_act"), c - 1)
                    for k in range(4):
                        mm = pe.transpose(PS[:, 4 + (2 * c + j) % 4, P * k:P * (k + 1)],
                                          H[:, 4 * j + k, META + P * c:META + P * (c + 1)], ident[:, :])
                    mm.then_inc(sg("out_turned"), 1)

        @block.vector
        def _(dve):
            dve.sem_inc(sg("g_evac"), 2)

            def split(b, i=0, turns=1):
                at_b = placed(b, i, turns)
                if at_b:
                    s, n, _, free_at = at_b
                    dve.wait_ge(sg("w_hi_made"), free_at)
                    dve.tensor_tensor(WLO[:, s, 0:n], RAW[:, s, 0:n], WHI[:, s, 0:n].bitcast(F32), ALU.subtract
                                      ).then_inc(sg("w_lo_made"), 1)

            for tau in range(5):
                t0, L = CHUNKS[tau]
                dve.wait_ge(sg("x_turned"), 2 * tau + 2)
                dve.tensor_copy(H[:, 4:8, t0:t0 + L],
                                PS[:, 4 + (2 * tau + 1) % 4, :].rearrange("p (k t) -> p k t", k=4)[:, :, 0:L]
                                ).then_inc(sg("x_in_dve"), 1)
            dve.wait_ge(sg("vecs_turned"), 2)
            dve.tensor_copy(VA[:, :], PS[:, 0, 0:ROWS_A]).then_inc(sg("vecs_ready"), 1)
            dve.tensor_copy(VB[:, :], PS[:, 1, 0:ROWS_B]).then_inc(sg("vecs_ready"), 1)
            dve.wait_ge(sg("vecs_ready"), 2)
            dve.wait_ge(sg("consts_landed"), 16 * CONSTS)
            for o in range(2):
                dve.tensor_copy(dskip[64 * o:64 * (o + 1), :],
                                heads_in[64 * o:64 * (o + 1), 1, :].rearrange("p (j o) -> p j o", o=2)[:, :, o]
                                ).then_inc(sg("d_skip_ready"), 1)
            dve.tensor_scalar(nba[:, :], VB[:, 63:83], -1.0, None, ALU.mult).then_inc(sg("neg_bias"), 1)
            split(0)
            split(1)

            def mean(name, n, width, dst, c0=0):
                t, u = BEFORE[name] if name in BEFORE else (0, int(name[4:]))
                ss, mean_made, root = ((step(name, "ss"), step(name, "mean"), step(name, "root")) if name in BEFORE
                                       else (sg("fuse_ss"), sg("fuse_mean"), sg("fuse_root")))
                dve.wait_ge(ss, t + n if name in BEFORE else u + 1)
                dve.tensor_scalar(two(dst[:, c0:T]), g_tile(2, T - c0), 1.0 / width, EPS, ALU.mult, ALU.add
                                  ).then_inc(mean_made, 1)
                dve.wait_ge(root, u + 1)
                dve.reciprocal(dst[:, c0:T], dst[:, c0:T]).then_inc(sg("rstd_made"), 1)
                mean.made += 1
                dve.wait_ge(sg("rstd_made"), mean.made)
            mean.made = 0

            def low_part(u, k, name, layer, c0):
                dve.wait_ge(step(f"prep{u}", "hi"), KT * u + k + 1)
                dve.scalar_tensor_tensor(out=ALO[:, k, c0:T], in0=H[:, k, c0:T], scalar=vec(name, KT * layer + k),
                                         in1=AHI[:, k, c0:T].bitcast(F32), op0=ALU.mult, op1=ALU.subtract
                                         ).then_inc(step(f"prep{u}", "lo"), 1)

            dve.wait_ge(sg("x_in_dve"), 5)
            for k in range(KT):
                low_part(0, k, "mix_pre_g", 0, 0)
            mean("prep0", KT, D, RS)

            def tile_out(dst, q, c0=0, rows=slice(0, P)):
                return dve.tensor_tensor(two(dst), g_tile(q, T - c0, rows), two(RS[rows, c0:T]), ALU.mult)

            def done(stage, q, block_no, i, per_i, tiles_i):
                if q == 0:
                    dve.wait_ge(sg("tile_done"), i * tiles_i + DONE[stage] + block_no + 1)
                else:
                    dve.wait_ge(sg("w_used"), i * per_i + FIRST[stage] + block_no + 3)

            def taps(x, acc, weight, m, names, n, own):
                dve.wait_ge(sg(names[3]), n)
                dve.wait_ge(sg("g_evac"), own)
                for j in range(3):
                    dve.scalar_tensor_tensor(out=acc, in0=x[:, j:T + j], scalar=vec(weight, m(j)), in1=acc,
                                             op0=ALU.mult, op1=ALU.add).then_inc(sg(names[j]), 1)
                    if j < 2:
                        dve.wait_ge(sg(names[j]), n)

            dve.wait_ge(sg("halo_ready"), 1)
            names = ["conv_tap0", "conv_tap1", "conv_tap2", "conv_tap3"]
            with dve.Fori(0, 3) as i:
                for s in range(2):
                    for q in range(2):
                        m = i * 4 + 2 * s + q
                        done("win", q, s, i, 2, 2)
                        tile_out(XRAW[:, q, 3:T + 3], q).then_inc(sg("g_evac"), 1)
                        taps(XRAW[:, q, :], CACC[:, q, :], "ssd_conv_w", lambda j: m + 12 * j, names, m + 1, m + 3)
                        if q == 0:
                            split(s + 2, i, 3)
            with dve.Fori(0, 2) as i:
                for s in range(2):
                    for q in range(2):
                        done("win", q, 6 + s, i, 2, 2)
                        tile_out(Z[:, bass.ds(i * 4 + 2 * s + q, 1), :], q).then_inc(sg("g_evac"), 1)
                        if q == 0:
                            split(s + 8, i, 2)
            outs = [C5[:, 0, :], C5[:, 1, :], C5[:, 2, :], MISC[:, :], C5[:, 3, :], C5[:, 4, :]]
            for n, stage in enumerate(("cq", "misc", "ckv")):
                for q in range(2):
                    done(stage, q, 0, 0, 0, 0)
                    tile_out(outs[2 * n + q], q).then_inc(sg("g_evac"), 1)
                    if q == 0:
                        split(12 + n)

            def norm_split(name, src, g, n, width, hi, lo):
                mean(name, n, width, RS)
                t, _ = BEFORE[name]
                for k in range(n + 1):
                    if k < n:
                        if k >= 2:
                            dve.wait_ge(step(name, "lo"), t + k - 1)
                        dve.scalar_tensor_tensor(out=TMP[:, k % 2, :], in0=src(k), scalar=vec(g, k), in1=RS[:, :],
                                                 op0=ALU.mult, op1=ALU.mult).then_inc(step(name, "full"), 1)
                    if k:
                        dve.wait_ge(step(name, "hi"), t + k)
                        dve.tensor_tensor(lo(k - 1), TMP[:, (k - 1) % 2, :], hi(k - 1).bitcast(F32), ALU.subtract
                                          ).then_inc(step(name, "lo"), 1)

            dve.wait_ge(sg("g_evac"), 28)
            norm_split("qn", lambda k: C5[:, k, :], "mla_q_norm_g", 3, QRANK,
                       lambda k: LHI[:, k, :], lambda k: LLO[:, k, :])
            norm_split("kvn", lambda k: C5[:, 3 + k, :], "mla_kv_norm_g", 2, KVRANK,
                       lambda k: LHI[:, 3 + k, :], lambda k: LLO[:, 3 + k, :])
            dve.wait_ge(step("kvn", "lo"), 5)
            dve.tensor_tensor(TMP[64:128, 0, :], MISC[64:128, :], CS[64:128, :], ALU.mult).then_inc(sg("k_rope_terms"), 1)
            dve.wait_ge(sg("k_rope_moved"), 1)
            dve.tensor_tensor(KRS[64:96, :], TMP[64:96, 0, :], TMP[64:96, 1, :], ALU.add).then_inc(sg("k_rope"), 1)

            def softplus(name, x, first):
                step, done_act = sg(f"{name}_step"), sg(f"{name}_act")
                x0, x1, e, ln = (x[:, j, :] for j in range(4))
                first().then_inc(step, 1)
                dve.wait_ge(step, 1)
                dve.scalar_tensor_tensor(out=x1, in0=x0, scalar=-1.0, in1=x0, op0=ALU.mult, op1=ALU.min
                                         ).then_inc(step, 1)
                dve.wait_ge(done_act, 1)
                dve.tensor_scalar(x1, e, 1.0, None, ALU.add).then_inc(step, 1)
                dve.wait_ge(done_act, 2)
                dve.wait_ge(step, 3)
                dve.tensor_scalar(x1, x1, -1.0, 1e-30, ALU.add, ALU.max).then_inc(step, 1)
                dve.wait_ge(step, 4)
                dve.reciprocal(x1, x1).then_inc(step, 1)
                dve.tensor_tensor(ln, ln, e, ALU.mult).then_inc(step, 1)
                dve.wait_ge(step, 6)
                dve.tensor_tensor(ln, ln, x1, ALU.mult).then_inc(step, 1)
                dve.wait_ge(step, 7)
                dve.tensor_scalar(x1, e, -0.5, 1.0, ALU.mult, ALU.add).then_inc(step, 1)
                dve.wait_ge(step, 8)
                dve.tensor_tensor(x1, x1, e, ALU.mult).then_inc(step, 1)
                dve.wait_ge(step, 9)
                dve.tensor_tensor(ln, ln, x1, ALU.max).then_inc(step, 1)
                dve.wait_ge(step, 10)
                dve.scalar_tensor_tensor(out=x0, in0=x0, scalar=0.0, in1=ln, op0=ALU.max, op1=ALU.add
                                         ).then_inc(step, 1)
                dve.wait_ge(step, DT_STEPS)

            softplus("dt", DTC, lambda: dve.tensor_scalar(DTC[:, 0, :], MISC[0:HEADS, :], dtb[:, :], None, ALU.add))
            dve.wait_ge(sg("dt_turned"), 1)
            dve.wait_ge(sg("exp_a"), 1)
            turned = PS[:, 7, 0:5 * HEADS].rearrange("p (c h) -> p c h", c=5)
            dve.tensor_copy(DTT[0:META, 0, :], turned[0:META, 0, :]).then_inc(sg("dt_rows"), 1)
            dve.tensor_copy(DTT[:, 1:5, :], turned[:, 1:5, :]).then_inc(sg("dt_rows"), 1)
            dve.wait_ge(sg("dt_rows"), 2)
            dve.scalar_tensor_tensor(out=DA[0:META, 0, :], in0=DTT[0:META, 0, :], scalar=-1.0, in1=expA[0:META, :],
                                     op0=ALU.mult, op1=ALU.mult).then_inc(sg("da_rows"), 1)
            dve.scalar_tensor_tensor(out=DA[:, 1:5, :], in0=DTT[:, 1:5, :], scalar=-1.0,
                                     in1=expA[:, :].unsqueeze(1).to_broadcast([P, 4, HEADS]),
                                     op0=ALU.mult, op1=ALU.mult).then_inc(sg("da_rows"), 1)
            dve.wait_ge(sg("da_rows"), 2)

            def heads_of(b):
                return b.rearrange("p b (h d) -> p b h d", h=8)

            def ssd(c, it=None):
                t0, L, v = chunk(c, it)
                tau = slice(0, 1) if c == 0 else bass.ds(it + 1, 1)
                rows = slice(0, L)
                if c > 0:
                    dve.wait_ge(sg("ssd_y_mm"), v - 1)
                dve.tensor_copy(DAC[rows, :].unsqueeze(1), DA[rows, tau, :]).then_inc(sg("ssd_da_staged"), 1)
                dve.wait_ge(sg("ssd_cb_mm"), v)
                dve.tensor_copy(ACS[rows, :], PS[rows, 6, 0:HEADS]).then_inc(sg("ssd_acs"), 1)
                dve.tensor_tensor(CBM[rows, :, 0:L],
                                  PS[rows, 6, P:3 * P].rearrange("p (g l) -> p g l", g=2)[:, :, 0:L],
                                  triu[rows, 0:L].unsqueeze(1).to_broadcast([L, 2, L]), ALU.mult).then_inc(sg("ssd_cb"), 1)
                dve.wait_ge(sg("ssd_r_mm"), v)
                dve.wait_ge(sg("ssd_acs"), v)
                acs4 = ACS[rows, :].rearrange("p (b h) -> p b h", b=4)
                r4 = PS[rows, 0:4, :].rearrange("p b (h l) -> p b h l", h=4)
                dve.tensor_tensor(DTE[rows, :].rearrange("p (b h) -> p b h", b=4), r4[:, :, :, L - 1], acs4,
                                  ALU.subtract).then_inc(sg("ssd_to_end_arg"), 1)
                e4 = E[rows, :, 0:L].rearrange("p (b h) l -> p b h l", b=4)
                dve.tensor_tensor(e4, r4[:, :, :, 0:L], acs4.unsqueeze(3).to_broadcast([L, 4, 4, L]), ALU.subtract
                                  ).then_inc(sg("ssd_e_arg"), 1)
                dve.wait_ge(sg("ssd_e_arg"), v)
                dve.tensor_scalar(E[rows, :, 0:L], E[rows, :, 0:L], 0.0, None, ALU.min).then_inc(sg("ssd_e_min"), 1)
                dve.wait_ge(sg("ssd_x_turned"), v)
                dtt = DTT[rows, tau, :].rearrange("p o (b h) -> p (o b) h", b=2)
                dve.tensor_tensor(XDT[rows, :, :].rearrange("p (b h) d -> p b h d", b=2), heads_of(PS[rows, 4:6, :]),
                                  dtt.unsqueeze(3).to_broadcast([L, 2, 8, VD]), ALU.mult).then_inc(sg("ssd_xdt"), 1)
                dve.wait_ge(sg("ssd_er"), v)
                dve.tensor_copy(CD[:, :], ER[:, :, L - 1]).then_inc(sg("ssd_cd"), 1)
                dve.wait_ge(sg("ssd_cd"), v)
                er = ER[:, :, 0:L].rearrange("p (g h) l -> p g h l", g=2)
                dve.tensor_tensor(er, er, XS[:, 10:12, 0:L].unsqueeze(2).to_broadcast([P, 2, 8, L]), ALU.mult
                                  ).then_inc(sg("ssd_c_decayed"), 1)
                dve.wait_ge(sg("ssd_e"), v)
                dve.wait_ge(sg("ssd_cb"), v)
                dve.tensor_tensor(MT[rows, :, 0:L].rearrange("p (g h) l -> p g h l", g=2),
                                  E[rows, :, 0:L].rearrange("p (g h) l -> p g h l", g=2),
                                  CBM[rows, :, 0:L].unsqueeze(2).to_broadcast([L, 2, 8, L]), ALU.mult
                                  ).then_inc(sg("ssd_mt"), 1)
                dve.wait_ge(sg("ssd_to_end"), v)
                dve.wait_ge(sg("ssd_xdt"), v)
                dve.tensor_tensor(XDE[rows, :, :], XDT[rows, :, :], DTE[rows, :].unsqueeze(2).to_broadcast([L, HEADS, VD]),
                                  ALU.mult).then_inc(sg("ssd_xde"), 1)
                if c > 0:
                    dve.wait_ge(sg("ssd_y_mm"), v)
                    dve.tensor_tensor(HST[:, :, :], HST[:, :, :], CD[:, :].unsqueeze(2).to_broadcast([P, HEADS, VD]),
                                      ALU.mult).then_inc(sg("ssd_state_decayed"), 1)
                dve.wait_ge(sg("ssd_y_mm"), v)
                dve.wait_ge(sg("ssd_skip"), v)
                yt = YT[:, :, 0:L].rearrange("p (b j) l -> p b j l", b=2)
                dve.tensor_tensor(yt, PS[:, 6:8, :].rearrange("p b (j l) -> p b j l", j=4)[:, :, :, 0:L], yt, ALU.add
                                  ).then_inc(sg("ssd_y_out"), 1)
                dve.wait_ge(sg("ssd_s_mm"), v)
                hst = HST[:, :, :].rearrange("p (b h) d -> p b h d", b=2)
                if c == 0:
                    dve.tensor_copy(hst, heads_of(PS[:, 4:6, :])).then_inc(sg("ssd_state"), 1)
                else:
                    dve.wait_ge(sg("ssd_state_decayed"), v - 1)
                    dve.tensor_tensor(hst, heads_of(PS[:, 4:6, :]), hst, ALU.add).then_inc(sg("ssd_state"), 1)
                dve.wait_ge(sg("ssd_y_out"), v)
                z = Z[:, :, bass.ds(t0, L)]
                dve.tensor_tensor(z, z, YT[:, :, 0:L], ALU.mult).then_inc(sg("ssd_y_done"), 1)

            dve.wait_ge(sg("z_ready"), 8)
            ssd(0)
            with dve.Fori(0, 4) as it:
                ssd(1, it)
            dve.wait_ge(sg("ssd_y_done"), 5)
            norm_split("yn", lambda k: Z[:, k, :], "ssd_norm_g", KT, INNER,
                       lambda k: UHI[:, k, :], lambda k: ULO[:, k, :])

            dve.sem_inc(sg("o_done"), 1)

            def soften(i, s, n):
                _, L, w = unit(n)
                u = i * 20 + 10 * s
                sc = PS[0:L, 2 + 2 * (n % 2):4 + 2 * (n % 2), :].rearrange("p b t -> p (b t)")
                dve.wait_ge(sg("s_mm"), u + n + 1)
                if w - L < 512 < w:
                    for k, (a, e) in enumerate(((w - L, 512), (512, w))):
                        dve.tensor_tensor(sc[:, a:e], sc[:, a:e], neg[0:L, a - w + L:e - w + L], ALU.add
                                          ).then_inc(sg("masked"), 1)
                else:
                    dve.tensor_tensor(sc[:, w - L:w], sc[:, w - L:w], neg[0:L, 0:L], ALU.add).then_inc(sg("masked"), 1)
                dve.wait_ge(sg("masked"), i * 24 + 12 * s + n + 1 + (n + 1) // 5)
                dve.tensor_reduce(MX[0:L, n % 2, 0:1], sc[:, 0:w], AX.X, ALU.max).then_inc(sg("row_max"), 1)
                dve.wait_ge(sg("row_max"), u + n + 1)
                dve.tensor_scalar(MX[0:L, n % 2, 1:2], MX[0:L, n % 2, 0:1], -SCALE, None, ALU.mult
                                  ).then_inc(sg("neg_max"), 1)

            def divide(u, n, s):
                t0, L, _ = unit(n)
                hp = slice(64 * (n // 5), 64 * (n // 5) + 64)
                dve.wait_ge(sg("o_mm"), u + n + 1)
                dve.reciprocal(RC[:, 0:L], PS[VD:P, 7, 0:L]).then_inc(sg("sum_recip"), 1)
                dve.wait_ge(sg("sum_recip"), u + n + 1)
                dve.tensor_tensor(ATT[hp, s, t0:t0 + L], PS[0:VD, 7, 0:L], RC[:, 0:L], ALU.mult).then_inc(sg("o_done"), 1)

            def attend(i, s):
                pair, u = i * 2 + s, i * 20 + 10 * s
                for h in range(2):
                    dve.wait_ge(sg("tile_done"), pair * 3 + DONE["att"] + h + 1)
                    dve.tensor_tensor(two(QB[:, h, :]), g_tile(0, T), two(CS[:, :]), ALU.mult).then_inc(sg("q_ready"), 1)
                dve.wait_ge(sg("w_used"), pair + FIRST["att"] + 3)
                dve.tensor_copy(VH[:, 1:5, :, 0:VD], PS[:, 0, :].rearrange("p (j h d) -> p j h d", j=4, h=2)
                                ).then_inc(sg("v_rows"), 1)
                dve.tensor_copy(VH[0:META, 0, :, 0:VD], PS[0:META, 1, 0:P].rearrange("p (h d) -> p h d", h=2)
                                ).then_inc(sg("v_ready"), 1)
                for n in range(12):
                    if n < 10:
                        soften(i, s, n)
                    if n == 1:
                        split(FIRST["att"] + s + 2, i, 3)
                    if n >= 2:
                        divide(u, n - 2, s)
                dve.wait_ge(sg("o_done"), u + 11)
                dve.wait_ge(sg("att_hi"), pair + 1)
                dve.tensor_tensor(ULO[:, bass.ds(pair + KT, 1), :], ATT[:, s:s + 1, :],
                                  UHI[:, bass.ds(pair + KT, 1), :].bitcast(F32), ALU.subtract).then_inc(sg("att_lo"), 1)

            dve.wait_ge(sg("v_ones"), 2)
            with dve.Fori(0, 3) as i:
                for s in range(2):
                    attend(i, s)
            for s in range(2):
                attend(3, s)

            def out_tile(m, q, c0, add):
                dst, src = two(M[:, bass.ds(m, 1), c0:T]), g_tile(q, T - c0)
                if add:
                    return dve.tensor_tensor(dst, src, dst, ALU.add)
                return dve.tensor_copy(dst, src)

            def outputs(stage, b, td, c0, uniform, add=False):
                n = 4 if uniform else 3

                def turn(i):
                    split(b + 2, i, n)
                    dve.wait_ge(sg("tile_done"), i + DONE[stage] + td + 1)
                    out_tile(i * 2, 0, c0, add).then_inc(sg("g_evac"), 1)
                    split(b + 3, i, n)
                    dve.wait_ge(sg("w_used"), i * 2 + b + 2 + 2)
                    out_tile(i * 2 + 1, 1, c0, add).then_inc(sg("g_evac"), 1)
                with dve.Fori(0, n) as i:
                    turn(i)
                if not uniform:
                    turn(3)

            def fuse(u, post, pre, layer, pre_layer, t_end, c0):
                mean(f"fuse{u}", 1, D, RP, c0)
                dve.wait_ge(sg("g_evac"), t_end + 2)
                for k in range(KT + 1):
                    if k < KT:
                        if k >= 2:
                            dve.wait_ge(sg("fuse_h"), KT * u + k - 1)
                        dve.scalar_tensor_tensor(out=TMP[:, k % 2, c0:T], in0=M[:, k, c0:T],
                                                 scalar=vec(post, KT * layer + k), in1=RP[:, c0:T],
                                                 op0=ALU.mult, op1=ALU.mult).then_inc(sg("fuse_term"), 1)
                    if k and pre:
                        low_part(u + 1, k - 1, pre, pre_layer, c0)
                if pre:
                    mean(f"prep{u + 1}", KT, D, RS, c0)

            def mlp(layer, c0):
                b0, first = FIRST[f"mlp{layer}"], 32 * layer
                stage = f"mlp{layer}"
                for f in range(2):
                    with dve.Fori(0, 4) as i:
                        for s in range(2):
                            for q in range(2):
                                n = i * 4 + 2 * s + q
                                if q == 0:
                                    dve.wait_ge(sg("tile_done"), i * 2 + DONE[stage] + 12 * f + s + 1)
                                else:
                                    dve.wait_ge(sg("w_used"), i * 2 + b0 + 16 * f + s + 3)
                                dve.scalar_tensor_tensor(out=two(TMP[:, q, c0:T]), in0=g_tile(q, T - c0), scalar=0.0,
                                                         in1=two(RS[:, c0:T]), op0=ALU.max, op1=ALU.mult
                                                         ).then_inc(sg("g_evac"), 1)
                                up_low(n, q, c0, first + 16 * f)
                                if q == 0:
                                    split(b0 + 16 * f + 2 + s, i, 4)
                    if f == 0:
                        outputs(stage, b0 + 8, 8, c0, True)
                outputs(stage, b0 + 24, 20, c0, layer == 0, add=True)

            def up_low(n, q, c0, first):
                dve.wait_ge(sg("up_square"), n + first + 1)
                dve.wait_ge(sg("up_hi"), n + first + 1)
                dve.tensor_tensor(ULO[:, bass.ds(n, 1), c0:T], SQT[:, q:q + 1, c0:T],
                                  UHI[:, bass.ds(n, 1), c0:T].bitcast(F32), ALU.subtract).then_inc(sg("up_lo"), 1)

            outputs("wout", FIRST["wout"], 0, 0, True)
            fuse(0, "mix_post_g", "mlp_pre_g", 0, 0, G_FIRST["mlp0"], 0)
            mlp(0, 0)
            fuse(1, "mlp_post_g", "mix_pre_g", 0, 1, G_FIRST["lru"], 0)

            lam = VB[:, PACK_B["rg_lambda"][0]:PACK_B["rg_lambda"][0] + LT]
            softplus("lam", LAM, lambda: dve.tensor_scalar(LAM[:, 0, :], lam, -1.0, None, ALU.mult))
            dve.tensor_scalar(cl[:, :], LAM[:, 0, :], -8.0, None, ALU.mult).then_inc(sg("lru_c"), 1)
            dve.wait_ge(sg("halo_ready"), 2)
            lnames = ["lconv_tap0", "lconv_tap1", "lconv_tap2", "lconv_tap3"]

            def lru_input(i, s):
                b0, t0 = FIRST["lru"], G_FIRST["lru"]
                n = i * 2 + s
                dve.wait_ge(sg("gw_hi_made"), n + 1)
                dve.tensor_tensor(GWL[:, s, :, :], GWR[:, s, :, :], GWH[:, s, :, :].bitcast(F32), ALU.subtract
                                  ).then_inc(sg("gw_lo_made"), 1)
                if s == 0:
                    dve.wait_ge(sg("tile_done"), i * 2 + DONE["lru"] + 1)
                else:
                    dve.wait_ge(sg("w_used"), i * 2 + b0 + 3)
                tile_out(LRAW[:, s, 3:T + 3], s).then_inc(sg("g_evac"), 1)
                taps(LRAW[:, s, :], LACC[:, s, :], "rg_conv_w", lambda j: n + 10 * j, lnames, n + 1,
                     i * 4 + s + t0 + 3)
                dve.wait_ge(sg("xr_hi"), n + 1)
                dve.wait_ge(sg("lconv_tap2"), n + 1)
                dve.tensor_tensor(XRL[:, s, :], LACC[:, s, :], XRH[:, s, :].bitcast(F32), ALU.subtract
                                  ).then_inc(sg("xr_lo"), 1)

            def lru_gates(i, s):
                n = i * 2 + s
                dve.wait_ge(sg("lru_er1"), n + 1)
                dve.reciprocal(RG[:, :], RG[:, :]).then_inc(sg("lru_r"), 1)
                dve.wait_ge(sg("lru_ei1"), n + 1)
                dve.reciprocal(IG[:, :], IG[:, :]).then_inc(sg("lru_i"), 1)
                dve.wait_ge(sg("lru_den"), n + 1)
                dve.reciprocal(TMP[:, 0, :], TMP[:, 0, :]).then_inc(sg("lru_den_recip"), 1)
                dve.wait_ge(sg("lru_den_recip"), n + 1)
                dve.scalar_tensor_tensor(out=TH[:, :], in0=TH[:, :], scalar=-2.0, in1=TMP[:, 0, :],
                                         op0=ALU.mult, op1=ALU.mult).then_inc(sg("lru_q"), 1)
                dve.wait_ge(sg("lru_root"), n + 1)
                dve.wait_ge(sg("lru_ix"), n + 1)
                dve.tensor_tensor(TMP[:, 1, :], TH[:, :], IG[:, :], ALU.mult).then_inc(sg("lru_u"), 1)
                dve.wait_ge(sg("lru_u"), n + 1)
                dve.wait_ge(sg("lru_a"), n + 1)
                dve.tensor_tensor_scan(SQT[:, 0, :], RG[:, :], TMP[:, 1, :], 0.0, ALU.mult, ALU.add
                                       ).then_inc(sg("lru_scan"), 1)
                dve.wait_ge(sg("lru_scan"), n + 1)
                dve.wait_ge(sg("gelu_ready"), n + 1)
                dve.tensor_tensor(SQT[:, 1:2, :], SQT[:, 0:1, :], GATE[:, bass.ds(n, 1), :], ALU.mult
                                  ).then_inc(sg("lru_gated"), 1)
                dve.wait_ge(sg("lru_hi"), n + 1)
                dve.tensor_tensor(GLO[:, bass.ds(n, 1), :], SQT[:, 1:2, :], GHI[:, bass.ds(n, 1), :].bitcast(F32),
                                  ALU.subtract).then_inc(sg("lru_lo"), 1)

            def lru(i):
                b0 = FIRST["lru"]
                for s in range(2):
                    lru_input(i, s)
                split(b0 + 2, i, 4)
                for s in range(2):
                    if s == 0:
                        dve.wait_ge(sg("tile_done"), i * 2 + DONE["lru"] + 2)
                    else:
                        split(b0 + 3, i, 4)
                        dve.wait_ge(sg("w_used"), i * 2 + b0 + 4)
                    tile_out(GATE[:, bass.ds(i * 2 + s, 1), :], s).then_inc(sg("g_evac"), 1)
                    lru_gates(i, s)

            with dve.Fori(0, LT // 2 - 1) as i:
                lru(i)
            lru(LT // 2 - 1)

            def rgo(i):
                b = FIRST["rgo"]
                for s in range(2):
                    split(b + 2 + s, i, 3)
                    dve.wait_ge(sg("w_used"), i * 2 + b + s + 3)
                    out_tile(i * 2 + s, s, META, False).then_inc(sg("g_evac"), 1)

            with dve.Fori(0, 3) as i:
                rgo(i)
            rgo(3)
            fuse(2, "mix_post_g", "mlp_pre_g", 1, 1, G_FIRST["mlp1"], META)
            mlp(1, META)
            fuse(3, "mlp_post_g", None, 1, 0, G_FIRST["mlp1"] + 48, META)
            for c in range(4):
                dve.wait_ge(sg("out_turned"), 2 * c + 2)
                dve.tensor_copy(OUTN[:, c, 512:1024], PS[:, 4 + (2 * c + 1) % 4, :]).then_inc(sg("out_rows_dve"), 1)



def shape_constants():
    import numpy as np
    rows, cols = np.arange(P)[:, None], np.arange(P)[None, :]
    freq = np.float32(10000.0) ** (-np.arange(0, ROPE, 2, dtype=np.float32) / np.float32(ROPE))
    angle = (freq[:, None] * np.arange(T, dtype=np.float32)[None, :]).astype(np.float64)
    cos, sin = np.cos(angle), np.sin(angle)
    return {"c_ident": np.eye(P, dtype=np.float32),
            "c_neg": np.where(cols <= rows, 0.0, -1e30).astype(np.float32),
            "c_triu": (rows <= cols).astype(np.float32),
            "c_cs": np.concatenate([np.ones((NOPE, T)), cos, cos, -sin, sin]).astype(np.float32)}


def kernel(**inputs):
    import numpy as np
    import concourse.bacc as bacc
    from concourse.bass_utils import run_bass_kernel_spmd

    nc = bacc.Bacc("TRN2", target_bir_lowering=False, num_devices=1)
    arrays, args = {}, {}
    for name, value in {**inputs, **shape_constants()}.items():
        a = np.ascontiguousarray(value)
        arrays[f"in_{name}_dram"] = a
        args[name] = nc.dram_tensor(f"in_{name}_dram", a.shape, mybir.dt.from_np(a.dtype), kind="ExternalInput").ap()
    out = nc.dram_tensor("out_0_dram", (1, SEQ, D), F32, kind="ExternalOutput").ap()
    build(nc, args, out)
    result = run_bass_kernel_spmd(nc, [arrays], core_ids=[0])
    return result.results[0]["out_0_dram"]
```

```python
from contextlib import ExitStack

import concourse.bass as bass
from concourse import mybir

F32 = mybir.dt.float32
F32R = mybir.dt.float32r
ACT = mybir.ActivationFunctionType
ALU = mybir.AluOpType
AX = mybir.AxisListType

P = 128
D = 1024
KT = D // P
SEQ = 512
META = 16
T = META + SEQ
HALF = T // 2
DFF = 4 * D
EPS = 1e-6

INNER = 1024
XBC = 1536
DT_COL = INNER + XBC
CQ_COL = DT_COL + 16
CKV_COL = CQ_COL + 384
KR_COL = CKV_COL + 256
HEADS = 16
NOPE, ROPE, VD = 64, 32, 64
QRANK, KVRANK = 384, 256
SCALE = float(NOPE + ROPE) ** -0.5
CHUNKS = [(0, META)] + [(META + P * c, P) for c in range(SEQ // P)]

LRU = 1280
LT = LRU // P

PACK_A = {"mix_pre_g": (0, 16), "mix_post_g": (16, 16), "mlp_pre_g": (32, 16), "mlp_post_g": (48, 16),
          "ssd_conv_w": (64, 48), "ssd_conv_b": (112, 12)}
PACK_B = {"ssd_norm_g": (0, 8), "mla_q_norm_g": (8, 3), "mla_kv_norm_g": (11, 2), "rg_conv_w": (13, 40),
          "rg_conv_b": (53, 10), "rg_b_a": (63, 10), "rg_b_i": (73, 10), "rg_lambda": (83, 10)}
ROWS_A, ROWS_B = 124, 93
CONSTS = 4 + 1 + len(PACK_A) + len(PACK_B) + 3
BEFORE = {"qn": (0, 0), "kvn": (3, 1), "yn": (5, 2), "prep0": (0, 0), "prep1": (KT, 1), "prep2": (2 * KT, 2),
          "prep3": (3 * KT, 3)}
DT_STEPS = 11

STREAM = [("win", 10, 1, 2048), ("cq", 1, 1, 2048), ("misc", 1, 5, 2048), ("ckv", 1, 1, 2048),
          ("att", 8, 13, 1280), ("wout", 8, 1, 2048), ("mlp0", 32, 1, 2048),
          ("lru", 10, 1, 2048), ("rgo", 8, 1, 1280), ("mlp1", 32, 1, 2048)]
FIRST, _b = {}, 0
for _n, _k, _, _ in STREAM:
    FIRST[_n] = _b
    _b += _k
BLOCKS = _b
_of = [row for row in STREAM for _ in range(row[1])]


def landed(b):
    return 16 * sum(_of[i][2] for i in range(b % 2, b + 1, 2))


def floats(b):
    return _of[b][3]

G_FIRST, _t = {}, 0
for _n, _k in [("win", 20), ("cq", 2), ("misc", 2), ("ckv", 2), ("wout", 8), ("mlp0", 48), ("lru", 20),
               ("rgo", 8), ("mlp1", 48)]:
    G_FIRST[_n] = _t
    _t += _k

DONE = {}
_t = 0
for _n, _k in [("win", 10), ("cq", 1), ("misc", 1), ("ckv", 1), ("att", 24), ("wout", 4), ("mlp0", 24),
               ("lru", 10), ("rgo", 0), ("mlp1", 24)]:
    DONE[_n] = _t
    _t += _k


def build(nc, A, out):
    with ExitStack() as ctx:
        def sem(name):
            return ctx.enter_context(nc.semaphore(name))

        TB = 4 * T
        base = (nc.sbuf_base + 31) // 32 * 32

        def at(name, tile, shape, dt=F32, extra=0):
            return nc.alloc_sbuf_tensor_at(name, shape, dt, offset=base + tile * TB + extra)

        H = at("h_res", 0, [P, KT, T])
        RAW = at("w_raw", 8, [P, 2, 2048])
        WHI = at("w_hi", 8, [P, 2, 2048], F32R, 16384)
        WLO = at("w_lo", 8, [P, 2, 2048], F32R, 32768)
        Z0 = 32
        RS = at("rstd", Z0, [P, T])
        SQA = at("sq_sum", Z0 + 1, [P, T])
        SQT = at("sq_tmp", Z0 + 2, [P, 2, T])
        TMP = at("tmp", Z0 + 4, [P, 2, T])
        U0 = Z0 + 6
        UHI = at("u_hi", U0, [P, 16, T], F32R)
        ULO = at("u_lo", U0 + 16, [P, 16, T], F32R)
        A0 = U0 + 32
        AHI = at("a_hi", A0, [P, KT, T], F32R)
        ALO = at("a_lo", A0 + 8, [P, KT, T], F32R)
        M0 = A0 + 16
        M = at("mix_out", M0, [P, KT, T])
        C0 = M0 + 10
        ident = at("ident", C0, [P, P])
        neg = at("neg_mask", C0, [P, P], F32, 512)
        triu = at("triu", C0, [P, P], F32, 1024)
        ones = at("ones", C0, [P, P], F32, 1536)
        CS = at("rope_cs", C0 + 1, [P, T])
        VA = at("vec_a", C0 + 2, [P, ROWS_A])
        VB = at("vec_b", C0 + 2, [P, ROWS_B], F32, 512)
        heads_in = at("heads_in", C0 + 2, [P, 2, HEADS], F32, 1024)
        expA = at("exp_a", C0 + 2, [P, HEADS], F32, 1152)
        dskip = at("d_skip", C0 + 2, [P, KT], F32, 1216)
        dtb = at("dt_bias", C0 + 2, [HEADS, 1], F32, 1248)
        cl = at("lru_c", C0 + 2, [P, LT], F32, 1280)
        eps = at("eps", C0 + 2, [P, 1], F32, 1600)
        LAM = at("lam_work", C0 + 2, [P, 4, LT], F32, 1440)
        assert base + (C0 + 4) * TB <= nc.sbuf_usable_end, (base, C0)
        XN = at("x_rows", U0, [P, 4, D])
        MN = at("meta_rows", U0 + 8, [META, D])
        PKA = at("pack_a", U0 + 10, [ROWS_A, P])
        PKB = at("pack_b", U0 + 10, [ROWS_B, P], F32, 512)
        C5 = at("latent_raw", U0, [P, 5, T])
        MISC = at("misc", U0 + 5, [P, T])
        CACC = at("conv_acc", U0 + 6, [P, 2, T])
        Z = at("z_gate", U0 + 8, [P, KT, T])
        XC = at("xbc_conv", U0 + 16, [P, 12, T])
        XRAW = at("conv_in", U0 + 28, [P, 2, T + 3])
        LHI = at("latent_hi", M0, [P, 5, T], F32R)
        LLO = at("latent_lo", M0 + 5, [P, 5, T], F32R)
        KRS = at("k_rope", C0 + 3, [P, T])
        DTC = at("dt_work", U0, [HEADS, 4, T])
        YT = at("ssd_y", U0 + 1, [P, KT, P])
        XS = at("ssd_chunk", U0 + 3, [P, 12, P])
        DTT = at("ssd_dt", U0 + 6, [P, 5, HEADS])
        DA = at("ssd_da", U0 + 6, [P, 5, HEADS], F32, 320)
        DTE = at("ssd_to_end", U0 + 6, [P, HEADS], F32, 640)
        CD = at("ssd_chunk_decay", U0 + 6, [P, HEADS], F32, 704)
        ACS = at("ssd_acs", U0 + 6, [P, HEADS], F32, 768)
        DAC = at("ssd_da_chunk", U0 + 6, [P, HEADS], F32, 832)
        MT = at("ssd_mt", U0 + 28, [P, HEADS, P])
        E = at("ssd_decay", A0, [P, HEADS, P])
        ER = at("ssd_exp", A0 + 4, [P, HEADS, P])
        HST = at("ssd_state", A0 + 8, [P, HEADS, VD])
        XDT = at("ssd_xdt", A0 + 10, [P, HEADS, VD])
        XDE = at("ssd_xde", A0 + 12, [P, HEADS, VD])
        BT = at("ssd_bt", A0 + 14, [P, 2, P])
        CBM = at("ssd_cb", A0 + 14, [P, 2, P], F32, 1024)
        QB = at("q_heads", A0, [P, 2, 2, T])
        KB = at("k_heads", A0 + 4, [P, 2, 2, T])
        VH = at("v_heads", A0 + 8, [P, 2, 5, 2, VD])
        PTS = at("probs_t", A0 + 13, [P, 2, 5, P])
        neg_r = at("neg_mask_r", A0 + 15, [P, P], F32R, 1024)
        ident_r = at("ident_r", A0 + 15, [P, P], F32R, 1536)
        MX = at("row_max", A0 + 12, [P, 2, 1])
        SUM = at("row_sum", A0 + 12, [P, 2, 1], F32, 32)
        PR = at("probs", Z0 + 2, [P, 2, T])
        GATE = at("lru_gate", U0, [P, LT, T])
        GHI = at("lru_hi", U0, [P, LT, T], F32R)
        GLO = at("lru_lo", U0 + 10, [P, LT, T], F32R)
        GWR = at("gate_w_raw", M0, [P, 2, 2, P])
        GWH = at("gate_w_hi", M0 + 1, [P, 2, 2, P], F32R)
        GWL = at("gate_w_lo", M0 + 2, [P, 2, 2, P], F32R)
        LRAW = at("lru_in", U0 + 20, [P, 2, T + 3])
        LACC = at("lru_conv", U0 + 23, [P, 2, T])
        XRH = at("lru_x_hi", U0 + 25, [P, 2, T], F32R)
        XRL = at("lru_x_lo", U0 + 27, [P, 2, T], F32R)
        IG = at("lru_i", U0 + 29, [P, 2, T])
        RG = at("lru_r", M0 + 3, [P, 2, T])
        TH = at("lru_tanh", M0 + 5, [P, 2, T])
        A2 = at("lru_a_squared", M0 + 7, [P, 2, T])
        OUTN = at("out_rows", U0, [P, 4, D])
        RP = at("rstd_post", C0 + 3, [P, T])

        PS = ctx.enter_context(nc.psum_tensor("psum", [P, 8, 512], F32))

        made = {}

        def sg(name):
            if name not in made:
                made[name] = ctx.enter_context(nc.semaphore(name))
            return made[name]

        def step(name, what):
            return sg(("pre_" if name.startswith("prep") else "norm_") + what)

        def g_tile(q, w, rows=slice(0, P)):
            return PS[rows, 2 * q:2 * q + 2, 0:w // 2]

        def two(ap):
            if len(ap.shape) == 3:
                return ap.rearrange("p o (h t) -> p (o h) t", h=2)
            return ap.rearrange("p (h t) -> p h t", h=2)

        def vec(name, j):
            if name in PACK_A:
                return VA[:, bass.ds(PACK_A[name][0] + j, 1)]
            return VB[:, bass.ds(PACK_B[name][0] + j, 1)]

        def placed(b, i, turns):
            if isinstance(i, int):
                b += 2 * i
                return (b % 2, floats(b), landed(b), b + 1) if b < BLOCKS else None
            step = landed(b + 2) - landed(b)
            for j in range(turns):
                assert landed(b + 2 * j) == landed(b) + step * j and floats(b + 2 * j) == floats(b)
            return b % 2, floats(b), i * step + landed(b), i * 2 + b + 1

        def chunk(c, it):
            return (0, META, 1) if c == 0 else (it * P + META, P, it + 2)

        def unit(n):
            t0, L = CHUNKS[n % 5]
            return t0, L, t0 + L

        Q_TERMS = {2: (0, [0]), 3: (0, [1, 2]), 4: (1, [0]), 5: (1, [1]), 6: (1, [2])}
        K_TERMS = {7: [0, 1]}
        V_BLOCKS = {8: [1, 2], 9: [3, 4, 0]}
        Q_STEPS, K_STEP, V_STEP = (3, 6), 7, 9
        META_OUT = slice(384, 384 + META)

        def ago(i, s, n, k):
            s, n = (s, n - k) if n >= k else (s - 1, n - k + 10)
            number = i * 20 + (10 * s + n)
            if isinstance(i, int) and number < 0:
                return None
            return s % 2, n, number

        block = ctx.enter_context(nc.Block())

        @block.sync
        def _(sp):
            for c in range(4):
                sp.dma_start(XN[:, c, :], A["x"][0, P * c:P * (c + 1), :]).then_inc(sg("x_landed"), 16)

            def wait_slot(b):
                sp.wait_ge(sg("w_hi_made"), b - 1)
                sp.wait_ge(sg("w_lo_made"), b - 1)

            def put(s, src, k=KT):
                m = src.shape[1]
                sp.dma_start(RAW[:, s, 0:k * m].rearrange("p (k m) -> p k m", k=k),
                             src.rearrange("(k p) m -> p k m", p=P)).then_inc(sg(f"w_landed_{s}"), 16)

            w_in = A["w_in"][0]
            for s in range(2):
                put(s, w_in[:, INNER + 256 * s:INNER + 256 * (s + 1)])
            with sp.Fori(1, 3) as i:
                for s in range(2):
                    wait_slot(i * 2 + s)
                    put(s, w_in[:, bass.ds(i * 512 + INNER + 256 * s, 256)])
            with sp.Fori(0, 2) as i:
                for s in range(2):
                    wait_slot(i * 2 + 6 + s)
                    put(s, w_in[:, bass.ds(i * 512 + 256 * s, 256)])
            wait_slot(FIRST["cq"])
            put(FIRST["cq"] % 2, w_in[:, CQ_COL:CQ_COL + 256])
            b = FIRST["misc"]
            wait_slot(b)
            slot = RAW[:, b % 2, :].rearrange("p (k m) -> p k m", k=KT)
            for dst, src, n in [(0, CQ_COL + 256, P), (P, DT_COL, HEADS), (P + 64, KR_COL, ROPE),
                                (P + 96, KR_COL + ROPE // 2, ROPE // 2), (P + 112, KR_COL, ROPE // 2)]:
                sp.dma_start(slot[:, :, dst:dst + n], w_in[:, src:src + n].rearrange("(k p) m -> p k m", p=P)
                             ).then_inc(sg(f"w_landed_{b % 2}"), 16)
            wait_slot(FIRST["ckv"])
            put(FIRST["ckv"] % 2, w_in[:, CKV_COL:CKV_COL + 256])

            wq = A["mla_w_q_up"][0].rearrange("(k p) (h c) -> p k h c", p=P, h=HEADS)
            wkv = A["mla_w_kv_up"][0].rearrange("(k p) (h c) -> p k h c", p=P, h=HEADS)

            def put_heads(s, pair):
                landed_s = sg(f"w_landed_{s}")
                q = RAW[:, s, 0:768].rearrange("p (k h c) -> p k h c", k=3, h=2)
                kv = RAW[:, s, 768:1280].rearrange("p (v k h c) -> p v k h c", v=2, k=2, h=2)
                hs = bass.ds(pair * 2, 2)
                for k in range(3):
                    sp.dma_start(q[:, k, :, 0:96], wq[:, k, hs, :]).then_inc(landed_s, 16)
                    sp.dma_start(q[:, k, :, 96:112], wq[:, k, hs, 80:96]).then_inc(landed_s, 16)
                    sp.dma_start(q[:, k, :, 112:128], wq[:, k, hs, 64:80]).then_inc(landed_s, 16)
                for k in range(2):
                    for v in range(2):
                        sp.dma_start(kv[:, v, k], wkv[:, k, hs, VD * v:VD * (v + 1)]).then_inc(landed_s, 16)

            b0 = FIRST["att"]
            with sp.Fori(0, 4) as i:
                for s in range(2):
                    wait_slot(i * 2 + b0 + s)
                    put_heads((b0 + s) % 2, i * 2 + s)

            b0 = FIRST["wout"]
            with sp.Fori(0, 4) as i:
                for s in range(2):
                    wait_slot(i * 2 + b0 + s)
                    put((b0 + s) % 2, A["w_out_ab"][0, D * s:D * (s + 1), bass.ds(i * 256, 256)])

            def mlp(layer):
                b0 = FIRST[f"mlp{layer}"]
                for f in range(2):
                    with sp.Fori(0, 4) as i:
                        for s in range(2):
                            wait_slot(i * 2 + b0 + 16 * f + s)
                            put((b0 + s) % 2, A["w_up"][layer, :, bass.ds(i * 512 + DFF // 2 * f + 256 * s, 256)])
                    with sp.Fori(0, 4) as i:
                        for s in range(2):
                            wait_slot(i * 2 + b0 + 16 * f + 8 + s)
                            r = DFF // 2 * f + D * s
                            put((b0 + s) % 2, A["w_down"][layer, r:r + D, bass.ds(i * 256, 256)])

            def put_gates(s, n):
                for g, name in enumerate(("rg_w_a", "rg_w_i")):
                    sp.dma_start(GWR[:, s, g, :], A[name][0, bass.ds(n, 1), :, :].rearrange("o i j -> (o i) j")
                                 ).then_inc(sg(f"gw_landed_{s}"), 16)

            mlp(0)
            b0 = FIRST["lru"]
            names = ("rg_w_x", "rg_w_y")
            for s in range(2):
                wait_slot(b0 + s)
                put((b0 + s) % 2, A[names[s]][0, :, 0:256])
            sp.wait_ge(sg("fuse_term"), 2 * KT)
            for s in range(2):
                put_gates(s, s)
            with sp.Fori(1, LT // 2) as i:
                for s in range(2):
                    wait_slot(i * 2 + b0 + s)
                    put((b0 + s) % 2, A[names[s]][0, :, bass.ds(i * 256, 256)])
                for s in range(2):
                    sp.wait_ge(sg("gw_hi_made"), i * 2 + s - 1)
                    sp.wait_ge(sg("gw_lo_made"), i * 2 + s - 1)
                    put_gates(s, i * 2 + s)
            b0 = FIRST["rgo"]
            with sp.Fori(0, 4) as i:
                for s in range(2):
                    wait_slot(i * 2 + b0 + s)
                    put((b0 + s) % 2, A["rg_w_out"][0, :, bass.ds(i * 256 + P * s, P)], k=LT)
            mlp(1)
            for c in range(4):
                sp.wait_ge(sg("out_rows_act"), c + 1)
                sp.wait_ge(sg("out_rows_dve"), c + 1)
                sp.dma_start(out[0, P * c:P * (c + 1), :], OUTN[:, c, :]).then_inc(sg("out_stored"), 16)
            sp.wait_ge(sg("out_stored"), 64)

        @block.gpsimd
        def _(pool):
            pool.memset(ones[:, :], 1.0).then_inc(sg("ones_ready"), 1)
            pool.memset(eps[:, :], EPS).then_inc(sg("ones_ready"), 1)
            pool.memset(SQA[:, :], 0.0).then_inc(sg("sqa_zero"), 1)
            pool.sem_inc(sg("m_summed"), 2)

            def sums(first, n, c0):
                with pool.Fori(0, n // 2) as i:
                    for s in range(2):
                        pool.wait_ge(sg("m_squared"), i * 2 + first + s + 1)
                        pool.wait_ge(sg("m_summed"), i * 2 + first + s + 2)
                        pool.tensor_tensor(SQA[:, c0:T], SQA[:, c0:T], SQT[:, s, c0:T], ALU.add
                                           ).then_inc(sg("m_summed"), 1)

            def residual(u, c0):
                for k in range(KT):
                    pool.wait_ge(sg("fuse_term"), KT * u + k + 1)
                    pool.tensor_tensor(H[:, k, c0:T], H[:, k, c0:T], TMP[:, k % 2, c0:T], ALU.add
                                       ).then_inc(sg("fuse_h"), 1)
                if u < 3:
                    pool.memset(SQA[:, :], 0.0).then_inc(sg("sqa_zero"), 1)
                    pool.wait_ge(sg("sqa_zero"), u + 2)

            def squares_up(first, c0):
                with pool.Fori(0, 8) as i:
                    for s in range(2):
                        pool.wait_ge(sg("g_evac"), i * 2 + first + s + 3)
                        pool.tensor_tensor(SQT[:, s, c0:T], TMP[:, s, c0:T], TMP[:, s, c0:T], ALU.mult
                                           ).then_inc(sg("up_square"), 1)

            def skip_term(c, it=None):
                t0, L, v = chunk(c, it)
                pool.wait_ge(sg("ssd_staged"), v)
                if c > 0:
                    pool.wait_ge(sg("ssd_y_done"), v - 1)
                pool.tensor_tensor(YT[:, :, 0:L], XS[:, 0:KT, 0:L],
                                   dskip[:, :].unsqueeze(2).to_broadcast([P, KT, L]), ALU.mult
                                   ).then_inc(sg("ssd_skip"), 1)

            pool.wait_ge(sg("sqa_zero"), 1)
            pool.memset(XRAW[:, :, 0:3], 0.0).then_inc(sg("halo_ready"), 1)
            pool.wait_ge(sg("d_skip_ready"), 2)
            skip_term(0)
            with pool.Fori(0, 4) as it:
                skip_term(1, it)

            pool.wait_ge(sg("ssd_y_done"), 5)
            pool.wait_ge(sg("ssd_state"), 5)
            pool.wait_ge(step("yn", "ss"), 5 + KT)
            pool.memset(PR[:, :, :], 0.0).then_inc(sg("probs_zero"), 1)

            sums(0, 8, 0)
            residual(0, 0)
            for f in range(2):
                squares_up(G_FIRST["mlp0"] + 24 * f, 0)
            sums(8, 8, 0)
            residual(1, 0)
            pool.memset(LRAW[:, :, 0:3], 0.0).then_inc(sg("halo_ready"), 1)


            def lru_lows(i):
                for s in range(2):
                    pool.wait_ge(sg("gw_hi_made"), i * 2 + s + 1)
                    pool.tensor_tensor(GWL[:, s, :, :], GWR[:, s, :, :], GWH[:, s, :, :].bitcast(F32), ALU.subtract
                                       ).then_inc(sg("gw_lo_made"), 1)
                for s in range(2):
                    pool.wait_ge(sg("xr_hi"), i * 2 + s + 1)
                    pool.tensor_tensor(XRL[:, s, :], LACC[:, s, :], XRH[:, s, :].bitcast(F32), ALU.subtract
                                       ).then_inc(sg("xr_lo"), 1)

            def lru_input_gated(j):
                for s in range(2):
                    pool.wait_ge(sg("lru_i"), j * 2 + (s + 2))
                    pool.tensor_tensor(IG[:, s, :], IG[:, s, :], LACC[:, s, :], ALU.mult).then_inc(sg("lru_ix"), 1)

            lru_lows(0)
            with pool.Fori(1, LT // 2) as i:
                lru_input_gated(i - 1)
                lru_lows(i)
            lru_input_gated(LT // 2 - 1)
            sums(16, 8, META)
            residual(2, META)
            for f in range(2):
                squares_up(G_FIRST["mlp1"] + 24 * f, META)
            sums(24, 8, META)
            residual(3, META)

        @block.scalar
        def _(act):
            landed_c = sg("consts_landed")
            for name, dst in (("c_ident", ident), ("c_neg", neg), ("c_triu", triu), ("c_cs", CS)):
                act.dma_start(dst[:, :], A[name]).then_inc(landed_c, 16)
            act.dma_start(MN[:, :], A["meta_tokens"]).then_inc(landed_c, 16)
            for pack, dst in ((PACK_A, PKA), (PACK_B, PKB)):
                for name, (row, n) in pack.items():
                    src = A[name]
                    src = src.rearrange("a b c -> (a b c)") if len(src.shape) == 3 else src.rearrange("a b -> (a b)")
                    act.dma_start(dst[row:row + n, :], src.rearrange("(n p) -> n p", p=P)).then_inc(landed_c, 16)
            act.dma_start(heads_in[:, 0, :], A["ssd_a_log"].to_broadcast([P, HEADS])).then_inc(landed_c, 16)
            act.dma_start(heads_in[:, 1, :], A["ssd_d"].to_broadcast([P, HEADS])).then_inc(landed_c, 16)
            act.dma_start(dtb[:, :], A["ssd_dt_bias"].rearrange("a b -> b a"), allow_slow_non_contiguous=True
                          ).then_inc(landed_c, 16)

            def split(b, i=0, turns=1):
                at_b = placed(b, i, turns)
                if at_b:
                    s, n, landed_at, free_at = at_b
                    act.wait_ge(sg(f"w_landed_{s}"), landed_at)
                    act.wait_ge(sg("w_used"), free_at)
                    act.activation(WHI[:, s, 0:n], RAW[:, s, 0:n], ACT.Copy).then_inc(sg("w_hi_made"), 1)

            for tau in range(5):
                t0, L = CHUNKS[tau]
                act.wait_ge(sg("x_turned"), 2 * tau + 1)
                act.copy(H[:, 0:4, t0:t0 + L], PS[:, 4 + 2 * tau % 4, :].rearrange("p (k t) -> p k t", k=4)[:, :, 0:L]
                         ).then_inc(sg("x_in_act"), 1)
            split(0)
            split(1)

            def prep(u, name, layer, c0, after):
                name_u, t = f"prep{u}", KT * u
                for k in range(KT):
                    if after:
                        act.wait_ge(sg("fuse_h"), t - KT + k + 1)
                    act.activation(AHI[:, k, c0:T], H[:, k, c0:T], ACT.Identity, scale=vec(name, KT * layer + k)
                                   ).then_inc(step(name_u, "hi"), 1)
                    if k >= 2:
                        act.wait_ge(step(name_u, "ss"), t + k - 1)
                    act.activation(SQT[:, k % 2, c0:T], H[:, k, c0:T], ACT.Square).then_inc(step(name_u, "sq"), 1)
                act.wait_ge(step(name_u, "ss"), t + KT)
                act.activation(two(RS[:, c0:T]), g_tile(2, T - c0), ACT.Sqrt, scale=1.0 / D, bias=eps[:, :]).then_inc(step(name_u, "root"), 1)

            act.wait_ge(sg("vecs_ready"), 2)
            act.wait_ge(sg("x_in_act"), 5)
            act.wait_ge(sg("x_in_dve"), 5)
            act.wait_ge(sg("ones_ready"), 2)
            prep(0, "mix_pre_g", 0, 0, False)

            act.wait_ge(sg("halo_ready"), 1)

            def conv_tap3(m, q):
                act.wait_ge(sg("g_evac"), m + 3)
                act.activation(CACC[:, q, :], XRAW[:, q, 3:T + 3], ACT.Identity, scale=vec("ssd_conv_w", m + 36),
                               bias=vec("ssd_conv_b", m)).then_inc(sg("conv_tap3"), 1)

            def conv_silu(m, q):
                act.wait_ge(sg("conv_tap2"), m + 1)
                act.activation(XC[:, bass.ds(m, 1), :], CACC[:, q:q + 1, :], ACT.Silu).then_inc(sg("xbc_ready"), 1)

            with act.Fori(0, 3) as i:
                for s in range(2):
                    m = i * 4 + 2 * s
                    conv_tap3(m, 0)
                    conv_silu(m, 0)
                    conv_tap3(m + 1, 1)
                    split(s + 2, i, 3)
                    conv_silu(m + 1, 1)
            with act.Fori(0, 2) as i:
                for s in range(2):
                    for q in range(2):
                        act.wait_ge(sg("g_evac"), i * 4 + 2 * s + q + 12 + 3)
                        zt = Z[:, bass.ds(i * 4 + 2 * s + q, 1), :]
                        act.activation(zt, zt, ACT.Silu).then_inc(sg("z_ready"), 1)
                        if q == 1:
                            split(s + 8, i, 2)
            for b in range(12, 15):
                split(b)

            def norm_split(name, src, n, width, dst):
                t, _ = BEFORE[name]
                for k in range(n):
                    if k >= 2:
                        act.wait_ge(step(name, "ss"), t + k - 1)
                    act.activation(SQT[:, k % 2, :], src(k), ACT.Square).then_inc(step(name, "sq"), 1)
                act.wait_ge(step(name, "ss"), t + n)
                act.activation(two(RS[:, :]), g_tile(2, T), ACT.Sqrt, scale=1.0 / width, bias=eps[:, :]).then_inc(step(name, "root"), 1)
                for k in range(n):
                    act.wait_ge(step(name, "full"), t + k + 1)
                    act.activation(dst(k), TMP[:, k % 2, :], ACT.Copy).then_inc(step(name, "hi"), 1)

            act.wait_ge(sg("g_evac"), 26 + 2)
            norm_split("qn", lambda k: C5[:, k, :], 3, QRANK, lambda k: LHI[:, k, :])
            norm_split("kvn", lambda k: C5[:, 3 + k, :], 2, KVRANK, lambda k: LHI[:, 3 + k, :])
            act.wait_ge(sg("k_rope_terms"), 1)
            act.copy(TMP[64:96, 1, :], TMP[96:128, 0, :]).then_inc(sg("k_rope_moved"), 1)

            act.wait_ge(landed_c, 16 * CONSTS)
            act.activation(expA[:, :], heads_in[:, 0, :], ACT.Exp).then_inc(sg("exp_a"), 1)

            def softplus_parts(name, x):
                act.wait_ge(sg(f"{name}_step"), 2)
                act.activation(x[:, 2, :], x[:, 1, :], ACT.Exp).then_inc(sg(f"{name}_act"), 1)
                act.wait_ge(sg(f"{name}_step"), 3)
                act.activation(x[:, 3, :], x[:, 1, :], ACT.Ln).then_inc(sg(f"{name}_act"), 1)

            softplus_parts("dt", DTC)

            def ssd(c, it=None):
                t0, L, v = chunk(c, it)
                if c > 0:
                    act.wait_ge(sg("ssd_y_mm"), v - 1)
                    act.wait_ge(sg("ssd_y_done"), v - 1)
                act.copy(XS[:, :, 0:L], XC[:, :, bass.ds(t0, L)]).then_inc(sg("ssd_staged"), 1)
                act.wait_ge(sg("ssd_bt_mm"), v)
                act.copy(BT[0:L, :, :], PS[0:L, 7, 0:256].rearrange("p (g n) -> p g n", g=2)).then_inc(sg("ssd_bt"), 1)
                act.wait_ge(sg("ssd_e_arg"), v)
                act.activation(ER[:, :, 0:L].rearrange("p (b h) l -> p b h l", b=4),
                               PS[:, 0:4, :].rearrange("p b (h l) -> p b h l", h=4)[:, :, :, 0:L], ACT.Exp
                               ).then_inc(sg("ssd_er"), 1)
                act.wait_ge(sg("ssd_to_end_arg"), v)
                act.activation(DTE[0:L, :], DTE[0:L, :], ACT.Exp).then_inc(sg("ssd_to_end"), 1)
                act.wait_ge(sg("ssd_e_min"), v)
                act.activation(E[0:L, :, 0:L], E[0:L, :, 0:L], ACT.Exp).then_inc(sg("ssd_e"), 1)

            act.wait_ge(sg("xbc_ready"), 12)
            act.wait_ge(sg("k_rope"), 1)
            act.wait_ge(sg("dt_turned"), 1)
            ssd(0)
            with act.Fori(0, 4) as it:
                ssd(1, it)
            act.wait_ge(sg("ssd_y_done"), 5)
            norm_split("yn", lambda k: Z[:, k, :], KT, INNER, lambda k: UHI[:, k, :])

            for s in range(2):
                for h in range(2):
                    for rows in (slice(64, 96), slice(96, 128)):
                        act.copy(KB[rows, s, h, :], KRS[64:96, :]).then_inc(sg("k_rope_placed"), 1)
            act.activation(ident_r[:, :], ident[:, :], ACT.Copy).then_inc(sg("mask_r"), 1)
            act.activation(neg_r[:, :], neg[:, :], ACT.Copy).then_inc(sg("mask_r"), 1)

            def keys_out(i, s):
                act.wait_ge(sg("tile_done"), i * 6 + (3 * s + DONE["att"] + 3))
                act.copy(two(KB[0:64, s, 0, :]), g_tile(3, T, slice(0, 64))).then_inc(sg("k_first"), 1)
                act.copy(two(KB[0:64, s, 1, :]), g_tile(3, T, slice(64, 128))).then_inc(sg("k_ready"), 1)

            def values_out(i, s):
                act.wait_ge(sg("w_used"), i * 2 + (s + FIRST["att"] + 3))
                act.copy(VH[:, s, 1:5, :, :], PS[:, 6, :].rearrange("p (j h d) -> p j h d", j=4, h=2)
                         ).then_inc(sg("v_rows"), 1)
                act.copy(VH[0:META, s, 0, :, :], PS[0:META, 7, 0:P].rearrange("p (h d) -> p h d", h=2)
                         ).then_inc(sg("v_ready"), 1)

            def att_high(i, s):
                act.wait_ge(sg("o_mm"), i * 20 + (10 * s + 10))
                act.activation(UHI[:, bass.ds(i * 2 + (s + KT), 1), META:T], PS[:, 4 + s:5 + s, :], ACT.Copy
                               ).then_inc(sg("att_hi"), 1)

            def meta_high(i, s):
                act.wait_ge(sg("o_mm"), i * 20 + (10 * s + 6))
                act.activation(UHI[:, bass.ds(i * 2 + (s + KT), 1), 0:META], PS[:, 7:8, META_OUT], ACT.Copy
                               ).then_inc(sg("meta_hi"), 1)

            def attend(i, turns):
                for s in range(2):
                    for n in range(10):
                        _, L, w = unit(n)
                        act.wait_ge(sg("neg_max"), i * 20 + (10 * s + n + 1))
                        act.activation(PR[0:L, n % 2, 0:w], PS[0:L, 2 * (n % 2):2 * (n % 2) + 2, :].rearrange(
                            "p b t -> p (b t)")[:, 0:w], ACT.Exp, bias=MX[0:L, n % 2, :],
                            accum_out=SUM[0:L, n % 2, :]).then_inc(sg("exp_ready"), 1)
                        if n == 1:
                            split(FIRST["att"] + s + 2, i, turns)
                        if n == 2 and not (isinstance(i, int) and i + s == 0):
                            att_high(*((i, 0) if s else (i - 1, 1)))
                        if n == K_STEP and not (isinstance(i, int) and i * 2 + s == 7):
                            keys_out(*((i + 1, 0) if s else (i, 1)))
                        if n == 8:
                            meta_high(i, s)
                        if n == V_STEP and not (isinstance(i, int) and i * 2 + s == 7):
                            values_out(*((i + 1, 0) if s else (i, 1)))

            keys_out(0, 0)
            values_out(0, 0)
            attend(0, 1)
            with act.Fori(1, 3) as i:
                attend(i, 3)
            attend(3, 1)
            att_high(3, 1)

            def square(t, m, s, c0, i):
                act.wait_ge(sg("g_evac"), i * 2 + t + s + 3)
                act.wait_ge(sg("m_summed"), i * 2 + m + s + 1)
                act.activation(SQT[:, s:s + 1, c0:T], M[:, bass.ds(i * 2 + s, 1), c0:T], ACT.Square
                               ).then_inc(sg("m_squared"), 1)

            def outputs(b, t, m, c0, uniform, two_blocks=True):
                n = 4 if uniform else 3

                def turn(i):
                    for s in range(2):
                        if two_blocks and s == 0:
                            split(b + 2, i, n)
                        square(t, m, s, c0, i)
                        if s == 1 or not two_blocks:
                            split(b + 2 + s, i, n)
                with act.Fori(0, n) as i:
                    turn(i)
                if not uniform:
                    turn(3)

            def post_root(u, c0):
                act.wait_ge(sg("fuse_ss"), u + 1)
                act.activation(two(RP[:, c0:T]), g_tile(2, T - c0), ACT.Sqrt, scale=1.0 / D, bias=eps[:, :]).then_inc(sg("fuse_root"), 1)

            def mlp(layer, c0):
                b0, t0 = FIRST[f"mlp{layer}"], G_FIRST[f"mlp{layer}"]
                for f in range(2):
                    with act.Fori(0, 4) as i:
                        for s in range(2):
                            for q in range(2):
                                n = i * 4 + 2 * s + q
                                act.wait_ge(sg("g_evac"), n + t0 + 24 * f + 3)
                                act.activation(UHI[:, bass.ds(n, 1), c0:T], TMP[:, q:q + 1, c0:T], ACT.Square
                                               ).then_inc(sg("up_hi"), 1)
                                if q == 1:
                                    split(b0 + 16 * f + 2 + s, i, 4)
                    if f == 0:
                        with act.Fori(0, 4) as i:
                            for s in range(2):
                                split(b0 + 8 + 2 + s, i, 4)
                outputs(b0 + 24, t0 + 40, 8 + 16 * layer, c0, layer == 0)

            outputs(FIRST["wout"], G_FIRST["wout"], 0, 0, True)
            post_root(0, 0)
            prep(1, "mlp_pre_g", 0, 0, True)
            mlp(0, 0)
            post_root(1, 0)
            prep(2, "mix_pre_g", 1, 0, True)
            softplus_parts("lam", LAM)
            act.sem_inc(sg("lru_i"), 1)
            act.wait_ge(sg("halo_ready"), 2)

            b_lru, t_lru = FIRST["lru"], G_FIRST["lru"]

            def gate_weights(i):
                for s in range(2):
                    act.wait_ge(sg(f"gw_landed_{s}"), i * 32 + 32)
                    act.activation(GWH[:, s, :, :], GWR[:, s, :, :], ACT.Copy).then_inc(sg("gw_hi_made"), 1)

            def lru_tap3(i, s):
                if not isinstance(i, int) or i > 0:
                    act.wait_ge(sg("lru_ix"), i * 2 + (s - 1))
                act.wait_ge(sg("g_evac"), i * 4 + s + t_lru + 3)
                act.activation(LACC[:, s, :], LRAW[:, s, 3:T + 3], ACT.Identity, scale=vec("rg_conv_w", i * 2 + s + 30),
                               bias=vec("rg_conv_b", i * 2 + s)).then_inc(sg("lconv_tap3"), 1)

            def lru_x_high(i, s):
                act.wait_ge(sg("lconv_tap2"), i * 2 + s + 1)
                act.activation(XRH[:, s, :], LACC[:, s, :], ACT.Copy).then_inc(sg("xr_hi"), 1)

            def lru_gates(i):
                for s in range(2):
                    n = i * 2 + s
                    act.wait_ge(sg("gates_mm"), n + 1)
                    act.activation(two(RG[:, s, :]), g_tile(2, T), ACT.Sigmoid, bias=vec("rg_b_a", n)
                                   ).then_inc(sg("lru_r"), 1)
                    act.activation(two(IG[:, s, :]), g_tile(3, T), ACT.Sigmoid, bias=vec("rg_b_i", n)).then_inc(sg("lru_i"), 1)

            def lru_decays(j):
                for s in range(2):
                    n1 = j * 2 + (s + 1)
                    act.wait_ge(sg("lru_r"), n1)
                    act.activation(TH[:, s, :], RG[:, s, :], ACT.Tanh, scale=cl[:, bass.ds(j * 2 + s, 1)]
                                   ).then_inc(sg("lru_th"), 1)
                    act.activation(RG[:, s, :], RG[:, s, :], ACT.Exp, scale=cl[:, bass.ds(j * 2 + s, 1)]
                                   ).then_inc(sg("lru_a"), 1)
                    act.wait_ge(sg("lru_a"), n1)
                    act.activation(A2[:, s, :], RG[:, s, :], ACT.Square).then_inc(sg("lru_a2"), 1)

            def lru_roots(j):
                for s in range(2):
                    act.wait_ge(sg("lru_q"), j * 2 + (s + 1))
                    act.activation(TH[:, s, :], TH[:, s, :], ACT.Sqrt, scale=-1.0).then_inc(sg("lru_root"), 1)

            def lru_gelu(j):
                for s in range(2):
                    act.wait_ge(sg("g_evac"), j * 4 + (s + 2 + t_lru + 3))
                    gt = GATE[:, bass.ds(j * 2 + s, 1), :]
                    act.activation(gt, gt, ACT.Gelu_apprx_tanh).then_inc(sg("gelu_ready"), 1)

            def lru_high(j):
                for s in range(2):
                    act.wait_ge(sg("lru_gated"), j * 2 + (s + 1))
                    act.activation(GHI[:, :, :].rearrange("p n t -> p (n t)")[:, bass.ds(j * (2 * T) + s * T, T)],
                                   SQT[:, s, :], ACT.Copy).then_inc(sg("lru_hi"), 1)

            def lru_turn(i, j, turns):
                split(b_lru + 1, i, turns)
                lru_decays(j)
                gate_weights(i)
                lru_tap3(i, 0)
                lru_roots(j)
                lru_x_high(i, 0)
                lru_tap3(i, 1)
                lru_gelu(j)
                lru_x_high(i, 1)
                split(b_lru + 2, i, turns)
                lru_high(j)
                lru_gates(i)

            gate_weights(0)
            lru_tap3(0, 0)
            lru_x_high(0, 0)
            lru_tap3(0, 1)
            lru_x_high(0, 1)
            split(b_lru + 2)
            lru_gates(0)
            with act.Fori(1, LT // 2 - 1) as i:
                lru_turn(i, i - 1, LT // 2 - 1)
            lru_turn(LT // 2 - 1, LT // 2 - 2, 1)
            j = LT // 2 - 1
            split(b_lru + 1, LT // 2)
            lru_decays(j)
            lru_roots(j)
            lru_gelu(j)
            lru_high(j)
            outputs(FIRST["rgo"], G_FIRST["rgo"], 16, META, False, two_blocks=False)
            post_root(2, META)
            prep(3, "mlp_pre_g", 1, META, True)
            mlp(1, META)
            post_root(3, META)
            for c in range(4):
                act.wait_ge(sg("out_turned"), 2 * c + 1)
                act.copy(OUTN[:, c, 0:512], PS[:, 4 + 2 * c % 4, :]).then_inc(sg("out_rows_act"), 1)

        @block.tensor
        def _(pe):
            pe.sem_inc(sg("w_used"), 2)

            pe.wait_ge(sg("consts_landed"), 16 * CONSTS)
            for tau in range(5):
                t0, L = CHUNKS[tau]
                if tau:
                    pe.wait_ge(sg("x_landed"), 16 * 4)
                for j in range(2):
                    if tau >= 2:
                        pe.wait_ge(sg("x_in_dve" if j else "x_in_act"), tau - 1)
                    for k in range(4):
                        cols = slice(P * (4 * j + k), P * (4 * j + k + 1))
                        src = XN[:, tau - 1, cols] if tau else MN[:, cols]
                        mm = pe.transpose(PS[:, 4 + (2 * tau + j) % 4, P * k:P * k + L], src, ident[0:L, 0:L])
                    mm.then_inc(sg("x_turned"), 1)
            pe.transpose(PS[:, 0, 0:ROWS_A], PKA[:, :], ident[0:ROWS_A, 0:ROWS_A]).then_inc(sg("vecs_turned"), 1)
            pe.transpose(PS[:, 1, 0:ROWS_B], PKB[:, :], ident[0:ROWS_B, 0:ROWS_B]).then_inc(sg("vecs_turned"), 1)
            pe.wait_ge(sg("ones_ready"), 2)

            def sum_squares(name, n, c0=0):
                w = (T - c0) // 2
                t, _ = BEFORE[name]
                for k in range(n):
                    pe.wait_ge(step(name, "sq"), t + k + 1)
                    for h in range(2):
                        mm = pe.matmul(PS[:, 4 + h, 0:w], ones[:, :], SQT[:, k % 2, c0 + h * w:c0 + (h + 1) * w],
                                       start=(k == 0), stop=(k == n - 1))
                    mm.then_inc(step(name, "ss"), 1)

            def product(q, ks, weight, x, c0=0, first=True, last=True, banks=None):
                w = (T - c0) // 2
                for k in ks:
                    (whi, wlo), (xhi, xlo) = weight(k), x(k)
                    for p, (a, b) in enumerate(((whi, xhi), (whi, xlo), (wlo, xhi))):
                        for h in range(2):
                            mm = pe.matmul(PS[:, 2 * q + h, 0:w], a, b[:, c0 + h * w:c0 + (h + 1) * w],
                                           start=(first and k == ks[0] and p == 0),
                                           stop=(last and k == ks[-1] and p == 2))
                return mm

            def take(b, i=0):
                pe.wait_ge(sg("w_hi_made"), i * 2 + b + 1)
                pe.wait_ge(sg("w_lo_made"), i * 2 + b + 1)

            def weights(s, m, width=256, ks=KT, base=0):
                def get(k):
                    c = base + k % ks * width + m * P
                    return WHI[:, s, c:c + P], WLO[:, s, c:c + P]
                return get

            def stream_of(hi, lo, base=0):
                return lambda k: (hi[:, base + k, :], lo[:, base + k, :])

            normed = stream_of(AHI, ALO)

            def two_tiles(b, t, i=0, c0=0, per=4):
                take(b, i)
                pe.wait_ge(sg("g_evac"), i * per + t + 1)
                product(0, range(KT), weights(b % 2, 0), normed, c0).then_inc(sg("tile_done"), 1)
                pe.wait_ge(sg("g_evac"), i * per + t + 2)
                product(1, range(KT), weights(b % 2, 1), normed, c0).then_inc(sg("w_used"), 1)

            def first_block(name, b, t, c0=0):
                w = (T - c0) // 2
                before, _ = BEFORE[name]
                take(b)
                pe.wait_ge(sg("g_evac"), t + 2)
                if before:
                    pe.wait_ge(sg("fuse_root"), BEFORE[name][1])
                for k in range(KT):
                    pe.wait_ge(step(name, "sq"), before + k + 1)
                    for h in range(2):
                        mm = pe.matmul(PS[:, 4 + h, 0:w], ones[:, :], SQT[:, k % 2, c0 + h * w:c0 + (h + 1) * w],
                                       start=(k == 0), stop=(k == KT - 1))
                    mm.then_inc(step(name, "ss"), 1)
                    pe.wait_ge(step(name, "lo"), before + k + 1)
                    for q in range(2):
                        mm = product(q, [k], weights(b % 2, q), normed, c0, first=(k == 0), last=(k == KT - 1))
                        if k == KT - 1:
                            mm.then_inc(sg("w_used" if q else "tile_done"), 1)

            first_block("prep0", 0, 0)
            two_tiles(1, 2)
            with pe.Fori(1, 5) as i:
                for s in range(2):
                    two_tiles(s, 2 * s, i)
            for name in ("cq", "misc", "ckv"):
                two_tiles(FIRST[name], G_FIRST[name])
            sum_squares("qn", 3)
            pe.wait_ge(step("qn", "root"), 1)
            sum_squares("kvn", 2)

            pe.wait_ge(sg("dt_step"), DT_STEPS)
            pe.wait_ge(step("kvn", "root"), 2)
            for tau in range(5):
                t0, L = CHUNKS[tau]
                mm = pe.transpose(PS[0:L, 7, HEADS * tau:HEADS * (tau + 1)], DTC[:, 0, t0:t0 + L],
                                  ident[0:HEADS, 0:HEADS])
            mm.then_inc(sg("dt_turned"), 1)

            def ssd(c, it=None):
                t0, L, v = chunk(c, it)
                pe.wait_ge(sg("ssd_staged"), v)
                pe.wait_ge(sg("ssd_da_staged"), v)
                if c > 0:
                    pe.wait_ge(sg("ssd_y_out"), v - 1)
                    pe.wait_ge(sg("ssd_state"), v - 1)
                pe.matmul(PS[0:L, 6, 0:HEADS], triu[0:L, 0:L], DAC[0:L, :], start=True, stop=True)
                for g in range(2):
                    mm = pe.matmul(PS[0:L, 6, P + P * g:P + P * g + L], XS[:, 8 + g, 0:L], XS[:, 10 + g, 0:L],
                                   start=True, stop=True)
                mm.then_inc(sg("ssd_cb_mm"), 1)
                for g in range(2):
                    mm = pe.transpose(PS[0:L, 7, P * g:P * (g + 1)], XS[:, 8 + g, 0:L], ident[:, :])
                mm.then_inc(sg("ssd_bt_mm"), 1)
                if c > 0:
                    pe.wait_ge(sg("ssd_er"), v - 1)
                for h in range(HEADS):
                    mm = pe.matmul(PS[:, h // 4, P * (h % 4):P * (h % 4) + L],
                                   DAC[0:L, h:h + 1].to_broadcast([L, P]), triu[0:L, 0:L], start=True, stop=True)
                mm.then_inc(sg("ssd_r_mm"), 1)
                for j in range(KT):
                    mm = pe.transpose(PS[0:L, 4 + j // 4, P * (j % 4):P * (j % 4 + 1)], XS[:, j, 0:L], ident[:, :])
                mm.then_inc(sg("ssd_x_turned"), 1)
                for name in ("ssd_mt", "ssd_xdt", "ssd_c_decayed", "ssd_bt", "ssd_cb"):
                    pe.wait_ge(sg(name), v)
                for h in range(HEADS):
                    j = h // 2
                    o = PS[64 * (h % 2):64 * (h % 2 + 1), 6 + j // 4, P * (j % 4):P * (j % 4) + L]
                    mm = pe.matmul(o, XDT[0:L, h, :], MT[0:L, h, 0:L], start=True, stop=(c == 0))
                    if c > 0:
                        mm = pe.matmul(o, HST[:, h, :], ER[:, h, 0:L], start=False, stop=True)
                mm.then_inc(sg("ssd_y_mm"), 1)
                pe.wait_ge(sg("ssd_xde"), v)
                for g in range(2):
                    mm = pe.matmul(PS[:, 4 + g, :], BT[0:L, g, :], XDE[0:L, 8 * g:8 * g + 8, :],
                                   start=True, stop=True)
                mm.then_inc(sg("ssd_s_mm"), 1)

            ssd(0)
            with pe.Fori(0, 4) as it:
                ssd(1, it)
            pe.wait_ge(sg("ssd_state"), 5)
            pe.wait_ge(sg("ssd_y_out"), 5)
            sum_squares("yn", KT)

            latent = stream_of(LHI, LLO)
            latent_kv = stream_of(LHI, LLO, 3)
            pe.wait_ge(step("kvn", "lo"), 5)
            pe.wait_ge(sg("k_rope_placed"), 8)
            pe.wait_ge(sg("mask_r"), 2)
            pe.wait_ge(sg("probs_zero"), 1)

            def scores(i, s, n):
                t0, L, w = unit(n)
                u = i * 20 + (10 * s + n)
                if n % 5 == 0:
                    pe.wait_ge(sg("q_ready"), i * 4 + 2 * s + n // 5 + 1)
                if n == 0:
                    pe.wait_ge(sg("k_ready"), i * 2 + s + 1)
                if ago(i, s, n, 2):
                    pe.wait_ge(sg("pt_ready"), u - 1)
                o = PS[0:L, 2 * (n % 2):2 * (n % 2) + 2, :].rearrange("p b t -> p (b t)")
                q = QB[:, s, n // 5, t0:t0 + L]
                for a in range(0, w, 512):
                    e = min(w, a + 512)
                    pe.matmul(o[:, a:e], q, KB[:, s, n // 5, a:e], start=True, stop=(e <= w - L))
                d = w - L
                for a, e in ((d, 512), (512, w)) if d < 512 < w else ((d, w),):
                    one, mask = (ident_r, neg_r) if L == P else (ident, neg)
                    mm = pe.matmul(o[:, a:e], one[0:L, 0:L], mask[0:L, a - d:e - d], start=False, stop=True)
                mm.then_inc(sg("s_mm"), 1)

            def turn(before):
                s, n, u = before
                _, L, _ = unit(n)
                b = 2 * (n % 2)
                pe.wait_ge(sg("p_ready"), u + 1)
                m = META if n % 5 else P
                mm = pe.matmul(PS[0:m, b + 1, 256:256 + L], PR[0:L, n % 2, 0:m], ident[0:L, 0:L], start=True, stop=True)
                for j in range(n % 5):
                    mm = pe.transpose(PS[:, b, P * j:P * j + L], PR[0:L, n % 2, META + P * j:META + P * (j + 1)],
                                      ident[0:L, 0:L])
                mm.then_inc(sg("pt_mm"), 1)

            def values(before, i, s):
                sv, n, u = before
                _, L, _ = unit(n)
                c, h = n % 5, n // 5
                pe.wait_ge(sg("pt_ready"), u + 1)
                if n == 0:
                    pe.wait_ge(sg("v_ready"), i * 2 + s + 1)
                if c == 0:
                    pe.wait_ge(sg("v_ready"), i * 2 + s + 1)
                    if h == 1 and not last_pair(i, s):
                        pe.wait_ge(sg("q_ready"), i * 4 + 2 * s + 4)
                pairs_out = i * 2 + (s - 1)
                if n == 1 and not (isinstance(i, int) and pairs_out <= 0):
                    pe.wait_ge(sg("att_lo"), pairs_out)
                rows_h = slice(VD * h, VD * (h + 1))
                o = PS[rows_h, 4 + sv, P * (c - 1):P * c] if c else PS[rows_h, 7, META_OUT]
                for j in range(c + 1):
                    rows = P if j else META
                    mm = pe.matmul(o, VH[0:rows, sv, j, h, :], PTS[0:rows, n % 2, j, 0:L], start=(j == 0), stop=(j == c))
                mm.then_inc(sg("o_mm"), 1)

            def last_pair(i, s):
                return isinstance(i, int) and i * 2 + s == 7

            def query(i, s, h, ks):
                if h == 0 and ks[0] == 0:
                    take(FIRST["att"] + s, i)
                    if not isinstance(i, int) or i + s > 0:
                        pe.wait_ge(sg("v_ready"), i * 2 + s)
                elif ks[0] == 0:
                    pe.wait_ge(sg("q_ready"), i * 4 + (2 * s + 1))
                mm = product(3, ks, weights((FIRST["att"] + s) % 2, h), latent, first=(ks[0] == 0), last=(ks[-1] == 2))
                if ks[-1] == 2:
                    mm.then_inc(sg("tile_done"), 1)

            def key(i, s, ks):
                if ks[0] == 0:
                    pe.wait_ge(sg("q_ready"), i * 4 + (2 * s + 2))
                mm = product(3, ks, weights((FIRST["att"] + s) % 2, 0, width=P, base=768), latent_kv,
                             first=(ks[0] == 0), last=(ks[-1] == 1))
                if ks[-1] == 1:
                    mm.then_inc(sg("tile_done"), 1)

            def value(i, s, js):
                if js[0] == 1:
                    pe.wait_ge(sg("k_ready"), i * 2 + s + 1)
                for j in js:
                    if j == 0 and (not isinstance(i, int) or i + s > 0):
                        pe.wait_ge(sg("meta_lo"), i * 2 + s)
                    t0 = CHUNKS[j][0]
                    o = PS[:, 6, P * (j - 1):P * j] if j else PS[:, 7, 0:P]
                    for k in range(2):
                        (whi, wlo), (xhi, xlo) = weights((FIRST["att"] + s) % 2, 0, width=P, base=1024)(k), latent_kv(k)
                        for p, (a, x) in enumerate(((whi, xhi), (whi, xlo), (wlo, xhi))):
                            mm = pe.matmul(o, x[:, t0:t0 + P], a, start=(k == 0 and p == 0), stop=(k == 1 and p == 2))
                if js[-1] == 0:
                    mm.then_inc(sg("w_used"), 1)

            def attend(i):
                for s in range(2):
                    i2, s2 = (i, 1) if s == 0 else (i + 1, 0)
                    for n in range(10):
                        scores(i, s, n)
                        if ago(i, s, n, 1):
                            turn(ago(i, s, n, 1))
                        if ago(i, s, n, 2):
                            values(ago(i, s, n, 2), i, s)
                        if last_pair(i, s):
                            continue
                        if n in Q_TERMS:
                            query(i2, s2, *Q_TERMS[n])
                        if n in K_TERMS:
                            key(i2, s2, K_TERMS[n])
                        if n in V_BLOCKS:
                            value(i2, s2, V_BLOCKS[n])

            query(0, 0, 0, [0, 1, 2])
            query(0, 0, 1, [0, 1, 2])
            key(0, 0, [0, 1])
            value(0, 0, [1, 2, 3, 4, 0])
            attend(0)
            with pe.Fori(1, 3) as i:
                attend(i)
            attend(3)
            turn(ago(4, 0, 0, 1))
            values(ago(4, 0, 0, 2), 4, 0)
            values(ago(4, 0, 1, 2), 4, 0)
            pe.wait_ge(sg("pt_ready"), 80)

            pe.wait_ge(step("yn", "lo"), 5 + KT)

            def down(b, t, c0, i, ready=None):
                for s in range(2):
                    take(b + s, i)
                    if s == 1 and ready:
                        ready()
                    x = stream_of(UHI, ULO, KT * s)
                    for q in range(2):
                        if s == 0:
                            pe.wait_ge(sg("g_evac"), i * 2 + t + q + 1)
                        mm = product(q, range(KT), weights((b + s) % 2, q), x, c0, first=(s == 0), last=(s == 1))
                        if q == 1:
                            mm.then_inc(sg("w_used"), 1)
                        elif s == 1:
                            mm.then_inc(sg("tile_done"), 1)

            def post_sum(u, c0):
                w = (T - c0) // 2
                pe.wait_ge(sg("m_summed"), 8 * (u + 1) + 2)
                for h in range(2):
                    mm = pe.matmul(PS[:, 4 + h, 0:w], ones[:, :], SQA[:, c0 + h * w:c0 + (h + 1) * w],
                                   start=True, stop=True)
                mm.then_inc(sg("fuse_ss"), 1)

            def mlp(layer, c0):
                b0, t0 = FIRST[f"mlp{layer}"], G_FIRST[f"mlp{layer}"]
                for f in range(2):
                    if f == 0:
                        first_block(f"prep{2 * layer + 1}", b0, t0, c0)
                        two_tiles(b0 + 1, t0 + 2, c0=c0)
                    with pe.Fori(1 if f == 0 else 0, 4) as i:
                        for s in range(2):
                            two_tiles(b0 + 16 * f + s, t0 + 24 * f + 2 * s, i, c0)
                    pe.wait_ge(sg("up_lo"), 32 * layer + 16 * f + 8)
                    down(b0 + 16 * f + 8, t0 + 24 * f + 16, c0, 0,
                         lambda: pe.wait_ge(sg("up_lo"), 32 * layer + 16 * (f + 1)))
                    with pe.Fori(1, 4) as i:
                        down(b0 + 16 * f + 8, t0 + 24 * f + 16, c0, i)

            down(FIRST["wout"], G_FIRST["wout"], 0, 0, lambda: (pe.wait_ge(sg("att_lo"), 8), pe.wait_ge(sg("meta_lo"), 8)))
            with pe.Fori(1, 4) as i:
                down(FIRST["wout"], G_FIRST["wout"], 0, i)
            post_sum(0, 0)
            mlp(0, 0)
            post_sum(1, 0)

            b0, t0 = FIRST["lru"], G_FIRST["lru"]
            def lru_turn(i):
                if isinstance(i, int):
                    first_block("prep2", b0, t0)
                    pe.wait_ge(step("prep2", "root"), 3)
                else:
                    two_tiles(b0, t0, i)
                take(b0 + 1, i)
                for s in range(2):
                    pe.wait_ge(sg("g_evac"), i * 4 + t0 + 2 + s + 1)
                    mm = product(s, range(KT), weights((b0 + 1) % 2, s), normed)
                    mm.then_inc(sg("w_used" if s else "tile_done"), 1)
                    n = i * 2 + s
                    pe.wait_ge(sg("xr_hi"), n + 1)
                    pe.wait_ge(sg("xr_lo"), n + 1)
                    pe.wait_ge(sg("gw_hi_made"), n + 1)
                    pe.wait_ge(sg("gw_lo_made"), n + 1)
                    pe.wait_ge(sg("lru_i"), n + 1)
                    for g in range(2):
                        mm = product(2 + g, [0], lambda k: (GWH[:, s, g, :], GWL[:, s, g, :]),
                                     lambda k: (XRH[:, s, :], XRL[:, s, :]))
                    mm.then_inc(sg("gates_mm"), 1)

            lru_turn(0)
            with pe.Fori(1, LT // 2) as i:
                lru_turn(i)

            b, t, gated = FIRST["rgo"], G_FIRST["rgo"], stream_of(GHI, GLO)
            pe.wait_ge(sg("lru_lo"), LT - 2)
            for ks in (range(LT - 2), range(LT - 2, LT)):
                for s in range(2):
                    if ks[0] == 0:
                        take(b + s)
                        pe.wait_ge(sg("g_evac"), t + s + 1)
                    else:
                        pe.wait_ge(sg("lru_lo"), LT)
                    mm = product(s, ks, weights((b + s) % 2, 0, width=P, ks=LT), gated, META,
                                 first=(ks[0] == 0), last=(ks[0] > 0))
                    if ks[0] > 0:
                        mm.then_inc(sg("w_used"), 1)
            with pe.Fori(1, 4) as i:
                for s in range(2):
                    take(b + s, i)
                    pe.wait_ge(sg("g_evac"), i * 2 + t + s + 1)
                    product(s, range(LT), weights((b + s) % 2, 0, width=P, ks=LT), gated, META
                            ).then_inc(sg("w_used"), 1)
            post_sum(2, META)
            mlp(1, META)
            post_sum(3, META)
            pe.wait_ge(sg("fuse_root"), 4)

            for c in range(4):
                for j in range(2):
                    if c == 0 and j == 0:
                        pe.wait_ge(sg("fuse_h"), 4 * KT)
                    if c >= 2:
                        pe.wait_ge(sg("out_rows_dve" if j else "out_rows_act"), c - 1)
                    for k in range(4):
                        mm = pe.transpose(PS[:, 4 + (2 * c + j) % 4, P * k:P * (k + 1)],
                                          H[:, 4 * j + k, META + P * c:META + P * (c + 1)], ident[:, :])
                    mm.then_inc(sg("out_turned"), 1)

        @block.vector
        def _(dve):
            dve.sem_inc(sg("g_evac"), 2)

            def split(b, i=0, turns=1):
                at_b = placed(b, i, turns)
                if at_b:
                    s, n, _, free_at = at_b
                    dve.wait_ge(sg("w_hi_made"), free_at)
                    dve.tensor_tensor(WLO[:, s, 0:n], RAW[:, s, 0:n], WHI[:, s, 0:n].bitcast(F32), ALU.subtract
                                      ).then_inc(sg("w_lo_made"), 1)

            for tau in range(5):
                t0, L = CHUNKS[tau]
                dve.wait_ge(sg("x_turned"), 2 * tau + 2)
                dve.tensor_copy(H[:, 4:8, t0:t0 + L],
                                PS[:, 4 + (2 * tau + 1) % 4, :].rearrange("p (k t) -> p k t", k=4)[:, :, 0:L]
                                ).then_inc(sg("x_in_dve"), 1)
            dve.wait_ge(sg("vecs_turned"), 2)
            dve.tensor_copy(VA[:, :], PS[:, 0, 0:ROWS_A]).then_inc(sg("vecs_ready"), 1)
            dve.tensor_copy(VB[:, :], PS[:, 1, 0:ROWS_B]).then_inc(sg("vecs_ready"), 1)
            dve.wait_ge(sg("vecs_ready"), 2)
            dve.wait_ge(sg("consts_landed"), 16 * CONSTS)
            for o in range(2):
                dve.tensor_copy(dskip[64 * o:64 * (o + 1), :],
                                heads_in[64 * o:64 * (o + 1), 1, :].rearrange("p (j o) -> p j o", o=2)[:, :, o]
                                ).then_inc(sg("d_skip_ready"), 1)
            split(0)
            split(1)

            def rstd(name, dst, c0=0):
                root, n = (step(name, "root"), BEFORE[name][1] + 1) if name in BEFORE else (sg("fuse_root"), int(name[4:]) + 1)
                dve.wait_ge(root, n)
                dve.reciprocal(dst[:, c0:T], dst[:, c0:T]).then_inc(sg("rstd_made"), 1)
                rstd.made += 1
                dve.wait_ge(sg("rstd_made"), rstd.made)
            rstd.made = 0

            def low_part(u, k, name, layer, c0):
                dve.wait_ge(step(f"prep{u}", "hi"), KT * u + k + 1)
                dve.scalar_tensor_tensor(out=ALO[:, k, c0:T], in0=H[:, k, c0:T], scalar=vec(name, KT * layer + k),
                                         in1=AHI[:, k, c0:T].bitcast(F32), op0=ALU.mult, op1=ALU.subtract
                                         ).then_inc(step(f"prep{u}", "lo"), 1)

            dve.wait_ge(sg("x_in_dve"), 5)
            for k in range(KT):
                low_part(0, k, "mix_pre_g", 0, 0)
            rstd("prep0", RS)

            def tile_out(dst, q, c0=0, rows=slice(0, P)):
                return dve.tensor_tensor(two(dst), g_tile(q, T - c0, rows), two(RS[rows, c0:T]), ALU.mult)

            def done(stage, q, block_no, i, per_i, tiles_i):
                if q == 0:
                    dve.wait_ge(sg("tile_done"), i * tiles_i + DONE[stage] + block_no + 1)
                else:
                    dve.wait_ge(sg("w_used"), i * per_i + FIRST[stage] + block_no + 3)

            def taps(x, acc, weight, m, names, n, own):
                dve.wait_ge(sg(names[3]), n)
                dve.wait_ge(sg("g_evac"), own)
                for j in range(3):
                    dve.scalar_tensor_tensor(out=acc, in0=x[:, j:T + j], scalar=vec(weight, m(j)), in1=acc,
                                             op0=ALU.mult, op1=ALU.add).then_inc(sg(names[j]), 1)
                    if j < 2:
                        dve.wait_ge(sg(names[j]), n)

            dve.wait_ge(sg("halo_ready"), 1)
            names = ["conv_tap0", "conv_tap1", "conv_tap2", "conv_tap3"]
            with dve.Fori(0, 3) as i:
                for s in range(2):
                    for q in range(2):
                        m = i * 4 + 2 * s + q
                        done("win", q, s, i, 2, 2)
                        tile_out(XRAW[:, q, 3:T + 3], q).then_inc(sg("g_evac"), 1)
                        if q == 1:
                            split(s + 2, i, 3)
                        taps(XRAW[:, q, :], CACC[:, q, :], "ssd_conv_w", lambda j: m + 12 * j, names, m + 1, m + 3)
            with dve.Fori(0, 2) as i:
                for s in range(2):
                    for q in range(2):
                        done("win", q, 6 + s, i, 2, 2)
                        tile_out(Z[:, bass.ds(i * 4 + 2 * s + q, 1), :], q).then_inc(sg("g_evac"), 1)
                        if q == 1:
                            split(s + 8, i, 2)
            outs = [C5[:, 0, :], C5[:, 1, :], C5[:, 2, :], MISC[:, :], C5[:, 3, :], C5[:, 4, :]]
            for n, stage in enumerate(("cq", "misc", "ckv")):
                for q in range(2):
                    done(stage, q, 0, 0, 0, 0)
                    tile_out(outs[2 * n + q], q).then_inc(sg("g_evac"), 1)
                    if q == 1:
                        split(12 + n)

            def norm_split(name, src, g, n, hi, lo):
                rstd(name, RS)
                t, _ = BEFORE[name]
                for k in range(n + 1):
                    if k < n:
                        if k >= 2:
                            dve.wait_ge(step(name, "lo"), t + k - 1)
                        dve.scalar_tensor_tensor(out=TMP[:, k % 2, :], in0=src(k), scalar=vec(g, k), in1=RS[:, :],
                                                 op0=ALU.mult, op1=ALU.mult).then_inc(step(name, "full"), 1)
                    if k:
                        dve.wait_ge(step(name, "hi"), t + k)
                        dve.tensor_tensor(lo(k - 1), TMP[:, (k - 1) % 2, :], hi(k - 1).bitcast(F32), ALU.subtract
                                          ).then_inc(step(name, "lo"), 1)

            dve.wait_ge(sg("g_evac"), 28)
            norm_split("qn", lambda k: C5[:, k, :], "mla_q_norm_g", 3,
                       lambda k: LHI[:, k, :], lambda k: LLO[:, k, :])
            norm_split("kvn", lambda k: C5[:, 3 + k, :], "mla_kv_norm_g", 2,
                       lambda k: LHI[:, 3 + k, :], lambda k: LLO[:, 3 + k, :])
            dve.wait_ge(step("kvn", "lo"), 5)
            dve.tensor_tensor(TMP[64:128, 0, :], MISC[64:128, :], CS[64:128, :], ALU.mult).then_inc(sg("k_rope_terms"), 1)
            dve.wait_ge(sg("k_rope_moved"), 1)
            dve.tensor_tensor(KRS[64:96, :], TMP[64:96, 0, :], TMP[64:96, 1, :], ALU.add).then_inc(sg("k_rope"), 1)

            def softplus(name, x, first):
                step, done_act = sg(f"{name}_step"), sg(f"{name}_act")
                x0, x1, e, ln = (x[:, j, :] for j in range(4))
                first().then_inc(step, 1)
                dve.wait_ge(step, 1)
                dve.scalar_tensor_tensor(out=x1, in0=x0, scalar=-1.0, in1=x0, op0=ALU.mult, op1=ALU.min
                                         ).then_inc(step, 1)
                dve.wait_ge(done_act, 1)
                dve.tensor_scalar(x1, e, 1.0, None, ALU.add).then_inc(step, 1)
                dve.wait_ge(done_act, 2)
                dve.wait_ge(step, 3)
                dve.tensor_scalar(x1, x1, -1.0, 1e-30, ALU.add, ALU.max).then_inc(step, 1)
                dve.wait_ge(step, 4)
                dve.reciprocal(x1, x1).then_inc(step, 1)
                dve.tensor_tensor(ln, ln, e, ALU.mult).then_inc(step, 1)
                dve.wait_ge(step, 6)
                dve.tensor_tensor(ln, ln, x1, ALU.mult).then_inc(step, 1)
                dve.wait_ge(step, 7)
                dve.tensor_scalar(x1, e, -0.5, 1.0, ALU.mult, ALU.add).then_inc(step, 1)
                dve.wait_ge(step, 8)
                dve.tensor_tensor(x1, x1, e, ALU.mult).then_inc(step, 1)
                dve.wait_ge(step, 9)
                dve.tensor_tensor(ln, ln, x1, ALU.max).then_inc(step, 1)
                dve.wait_ge(step, 10)
                dve.scalar_tensor_tensor(out=x0, in0=x0, scalar=0.0, in1=ln, op0=ALU.max, op1=ALU.add
                                         ).then_inc(step, 1)
                dve.wait_ge(step, DT_STEPS)

            softplus("dt", DTC, lambda: dve.tensor_scalar(DTC[:, 0, :], MISC[0:HEADS, :], dtb[:, :], None, ALU.add))
            dve.wait_ge(sg("dt_turned"), 1)
            dve.wait_ge(sg("exp_a"), 1)
            turned = PS[:, 7, 0:5 * HEADS].rearrange("p (c h) -> p c h", c=5)
            dve.tensor_copy(DTT[0:META, 0, :], turned[0:META, 0, :]).then_inc(sg("dt_rows"), 1)
            dve.tensor_copy(DTT[:, 1:5, :], turned[:, 1:5, :]).then_inc(sg("dt_rows"), 1)
            dve.wait_ge(sg("dt_rows"), 2)
            dve.scalar_tensor_tensor(out=DA[0:META, 0, :], in0=DTT[0:META, 0, :], scalar=-1.0, in1=expA[0:META, :],
                                     op0=ALU.mult, op1=ALU.mult).then_inc(sg("da_rows"), 1)
            dve.scalar_tensor_tensor(out=DA[:, 1:5, :], in0=DTT[:, 1:5, :], scalar=-1.0,
                                     in1=expA[:, :].unsqueeze(1).to_broadcast([P, 4, HEADS]),
                                     op0=ALU.mult, op1=ALU.mult).then_inc(sg("da_rows"), 1)
            dve.wait_ge(sg("da_rows"), 2)

            def heads_of(b):
                return b.rearrange("p b (h d) -> p b h d", h=8)

            def ssd(c, it=None):
                t0, L, v = chunk(c, it)
                tau = slice(0, 1) if c == 0 else bass.ds(it + 1, 1)
                rows = slice(0, L)
                if c > 0:
                    dve.wait_ge(sg("ssd_y_mm"), v - 1)
                dve.tensor_copy(DAC[rows, :].unsqueeze(1), DA[rows, tau, :]).then_inc(sg("ssd_da_staged"), 1)
                dve.wait_ge(sg("ssd_cb_mm"), v)
                dve.tensor_copy(ACS[rows, :], PS[rows, 6, 0:HEADS]).then_inc(sg("ssd_acs"), 1)
                dve.tensor_tensor(CBM[rows, :, 0:L],
                                  PS[rows, 6, P:3 * P].rearrange("p (g l) -> p g l", g=2)[:, :, 0:L],
                                  triu[rows, 0:L].unsqueeze(1).to_broadcast([L, 2, L]), ALU.mult).then_inc(sg("ssd_cb"), 1)
                dve.wait_ge(sg("ssd_r_mm"), v)
                dve.wait_ge(sg("ssd_acs"), v)
                acs4 = ACS[rows, :].rearrange("p (b h) -> p b h", b=4)
                r4 = PS[rows, 0:4, :].rearrange("p b (h l) -> p b h l", h=4)
                dve.tensor_tensor(DTE[rows, :].rearrange("p (b h) -> p b h", b=4), r4[:, :, :, L - 1], acs4,
                                  ALU.subtract).then_inc(sg("ssd_to_end_arg"), 1)
                e4 = E[rows, :, 0:L].rearrange("p (b h) l -> p b h l", b=4)
                dve.tensor_tensor(e4, r4[:, :, :, 0:L], acs4.unsqueeze(3).to_broadcast([L, 4, 4, L]), ALU.subtract
                                  ).then_inc(sg("ssd_e_arg"), 1)
                dve.wait_ge(sg("ssd_e_arg"), v)
                dve.tensor_scalar(E[rows, :, 0:L], E[rows, :, 0:L], 0.0, None, ALU.min).then_inc(sg("ssd_e_min"), 1)
                dve.wait_ge(sg("ssd_x_turned"), v)
                dtt = DTT[rows, tau, :].rearrange("p o (b h) -> p (o b) h", b=2)
                dve.tensor_tensor(XDT[rows, :, :].rearrange("p (b h) d -> p b h d", b=2), heads_of(PS[rows, 4:6, :]),
                                  dtt.unsqueeze(3).to_broadcast([L, 2, 8, VD]), ALU.mult).then_inc(sg("ssd_xdt"), 1)
                dve.wait_ge(sg("ssd_er"), v)
                dve.tensor_copy(CD[:, :], ER[:, :, L - 1]).then_inc(sg("ssd_cd"), 1)
                dve.wait_ge(sg("ssd_cd"), v)
                er = ER[:, :, 0:L].rearrange("p (g h) l -> p g h l", g=2)
                dve.tensor_tensor(er, er, XS[:, 10:12, 0:L].unsqueeze(2).to_broadcast([P, 2, 8, L]), ALU.mult
                                  ).then_inc(sg("ssd_c_decayed"), 1)
                dve.wait_ge(sg("ssd_e"), v)
                dve.wait_ge(sg("ssd_cb"), v)
                dve.tensor_tensor(MT[rows, :, 0:L].rearrange("p (g h) l -> p g h l", g=2),
                                  E[rows, :, 0:L].rearrange("p (g h) l -> p g h l", g=2),
                                  CBM[rows, :, 0:L].unsqueeze(2).to_broadcast([L, 2, 8, L]), ALU.mult
                                  ).then_inc(sg("ssd_mt"), 1)
                dve.wait_ge(sg("ssd_to_end"), v)
                dve.wait_ge(sg("ssd_xdt"), v)
                dve.tensor_tensor(XDE[rows, :, :], XDT[rows, :, :], DTE[rows, :].unsqueeze(2).to_broadcast([L, HEADS, VD]),
                                  ALU.mult).then_inc(sg("ssd_xde"), 1)
                if c > 0:
                    dve.wait_ge(sg("ssd_y_mm"), v)
                    dve.tensor_tensor(HST[:, :, :], HST[:, :, :], CD[:, :].unsqueeze(2).to_broadcast([P, HEADS, VD]),
                                      ALU.mult).then_inc(sg("ssd_state_decayed"), 1)
                dve.wait_ge(sg("ssd_y_mm"), v)
                dve.wait_ge(sg("ssd_skip"), v)
                yt = YT[:, :, 0:L].rearrange("p (b j) l -> p b j l", b=2)
                dve.tensor_tensor(yt, PS[:, 6:8, :].rearrange("p b (j l) -> p b j l", j=4)[:, :, :, 0:L], yt, ALU.add
                                  ).then_inc(sg("ssd_y_out"), 1)
                dve.wait_ge(sg("ssd_s_mm"), v)
                hst = HST[:, :, :].rearrange("p (b h) d -> p b h d", b=2)
                if c == 0:
                    dve.tensor_copy(hst, heads_of(PS[:, 4:6, :])).then_inc(sg("ssd_state"), 1)
                else:
                    dve.wait_ge(sg("ssd_state_decayed"), v - 1)
                    dve.tensor_tensor(hst, heads_of(PS[:, 4:6, :]), hst, ALU.add).then_inc(sg("ssd_state"), 1)
                dve.wait_ge(sg("ssd_y_out"), v)
                z = Z[:, :, bass.ds(t0, L)]
                dve.tensor_tensor(z, z, YT[:, :, 0:L], ALU.mult).then_inc(sg("ssd_y_done"), 1)

            dve.wait_ge(sg("z_ready"), 8)
            ssd(0)
            with dve.Fori(0, 4) as it:
                ssd(1, it)
            dve.wait_ge(sg("ssd_y_done"), 5)
            norm_split("yn", lambda k: Z[:, k, :], "ssd_norm_g", KT,
                       lambda k: UHI[:, k, :], lambda k: ULO[:, k, :])

            def queries_out(i, s, h):
                dve.wait_ge(sg("tile_done"), i * 6 + (3 * s + DONE["att"] + h + 1))
                dve.scalar_tensor_tensor(out=two(QB[:, s, h, :]), in0=g_tile(3, T), scalar=SCALE, in1=two(CS[:, :]),
                                         op0=ALU.mult, op1=ALU.mult).then_inc(sg("q_ready"), 1)

            def turn_out(before):
                _, n, u = before
                _, L, _ = unit(n)
                b = 2 * (n % 2)
                dve.wait_ge(sg("pt_mm"), u + 1)
                if n % 5:
                    dve.tensor_copy(PTS[:, n % 2, 1:n % 5 + 1, 0:L],
                             PS[:, b, :].rearrange("p (j l) -> p j l", j=4)[:, 0:n % 5, 0:L]).then_inc(sg("pt_part"), 1)
                dve.tensor_copy(PTS[0:META, n % 2, 0, 0:L], PS[0:META, b + 1, 256:256 + L]).then_inc(sg("pt_ready"), 1)

            def normalise(i, s, n):
                _, L, w = unit(n)
                u = i * 20 + (10 * s + n)
                dve.wait_ge(sg("exp_ready"), u + 1)
                dve.reciprocal(SUM[0:L, n % 2, :], SUM[0:L, n % 2, :]).then_inc(sg("sum_recip"), 1)
                dve.wait_ge(sg("sum_recip"), u + 1)
                dve.tensor_scalar(PR[0:L, n % 2, 0:w], PR[0:L, n % 2, 0:w], SUM[0:L, n % 2, :], None, ALU.mult
                                  ).then_inc(sg("p_ready"), 1)

            def att_low(i, s):
                dve.wait_ge(sg("att_hi"), i * 2 + (s + 1))
                at_pair = bass.ds(i * 2 + (s + KT), 1)
                dve.tensor_tensor(ULO[:, at_pair, META:T], PS[:, 4 + s:5 + s, :], UHI[:, at_pair, META:T].bitcast(F32),
                                  ALU.subtract).then_inc(sg("att_lo"), 1)

            def meta_low(i, s):
                dve.wait_ge(sg("meta_hi"), i * 2 + (s + 1))
                at_pair = bass.ds(i * 2 + (s + KT), 1)
                dve.tensor_tensor(ULO[:, at_pair, 0:META], PS[:, 7:8, META_OUT], UHI[:, at_pair, 0:META].bitcast(F32),
                                  ALU.subtract).then_inc(sg("meta_lo"), 1)

            def attend(i, turns):
                for s in range(2):
                    last = isinstance(i, int) and i * 2 + s == 7
                    first = isinstance(i, int) and i * 2 + s == 0
                    i2, s2 = (i + 1, 0) if s else (i, 1)
                    for n in range(10):
                        _, L, w = unit(n)
                        dve.wait_ge(sg("s_mm"), i * 20 + (10 * s + n + 1))
                        dve.tensor_reduce(MX[0:L, n % 2, :], PS[0:L, 2 * (n % 2):2 * (n % 2) + 2, :].rearrange(
                            "p b t -> p (b t)")[:, 0:w], AX.X, ALU.max, negate=True).then_inc(sg("neg_max"), 1)
                        if ago(i, s, n, 1):
                            turn_out(ago(i, s, n, 1))
                        if n == 3 and not first:
                            att_low(*((i, 0) if s else (i - 1, 1)))
                        normalise(i, s, n)
                        if n == 1:
                            split(FIRST["att"] + s + 2, i, turns)
                        if n == 8:
                            meta_low(i, s)
                        if last:
                            continue
                        if n in Q_STEPS:
                            queries_out(i2, s2, Q_STEPS.index(n))

            dve.wait_ge(sg("probs_zero"), 1)
            queries_out(0, 0, 0)
            queries_out(0, 0, 1)
            attend(0, 1)
            with dve.Fori(1, 3) as i:
                attend(i, 3)
            attend(3, 1)
            turn_out(ago(4, 0, 0, 1))
            att_low(3, 1)

            def out_tile(m, q, c0, add):
                dst, src = two(M[:, bass.ds(m, 1), c0:T]), g_tile(q, T - c0)
                if add:
                    return dve.tensor_tensor(dst, src, dst, ALU.add)
                return dve.tensor_copy(dst, src)

            def outputs(stage, b, td, c0, uniform, add=False):
                n = 4 if uniform else 3

                def turn(i):
                    split(b + 2, i, n)
                    dve.wait_ge(sg("tile_done"), i + DONE[stage] + td + 1)
                    out_tile(i * 2, 0, c0, add).then_inc(sg("g_evac"), 1)
                    dve.wait_ge(sg("w_used"), i * 2 + b + 2 + 2)
                    out_tile(i * 2 + 1, 1, c0, add).then_inc(sg("g_evac"), 1)
                    split(b + 3, i, n)
                with dve.Fori(0, n) as i:
                    turn(i)
                if not uniform:
                    turn(3)

            def fuse(u, post, pre, layer, pre_layer, t_end, c0):
                rstd(f"fuse{u}", RP, c0)
                dve.wait_ge(sg("g_evac"), t_end + 2)
                for k in range(KT + 1):
                    if k < KT:
                        if k >= 2:
                            dve.wait_ge(sg("fuse_h"), KT * u + k - 1)
                        dve.scalar_tensor_tensor(out=TMP[:, k % 2, c0:T], in0=M[:, k, c0:T],
                                                 scalar=vec(post, KT * layer + k), in1=RP[:, c0:T],
                                                 op0=ALU.mult, op1=ALU.mult).then_inc(sg("fuse_term"), 1)
                    if k and pre:
                        low_part(u + 1, k - 1, pre, pre_layer, c0)
                if pre:
                    rstd(f"prep{u + 1}", RS, c0)

            def mlp(layer, c0):
                b0, first = FIRST[f"mlp{layer}"], 32 * layer
                stage = f"mlp{layer}"
                for f in range(2):
                    with dve.Fori(0, 4) as i:
                        for s in range(2):
                            for q in range(2):
                                n = i * 4 + 2 * s + q
                                if q == 0:
                                    dve.wait_ge(sg("tile_done"), i * 2 + DONE[stage] + 12 * f + s + 1)
                                else:
                                    dve.wait_ge(sg("w_used"), i * 2 + b0 + 16 * f + s + 3)
                                dve.scalar_tensor_tensor(out=two(TMP[:, q, c0:T]), in0=g_tile(q, T - c0), scalar=0.0,
                                                         in1=two(RS[:, c0:T]), op0=ALU.max, op1=ALU.mult
                                                         ).then_inc(sg("g_evac"), 1)
                                up_low(n, q, c0, first + 16 * f)
                                if q == 1:
                                    split(b0 + 16 * f + 2 + s, i, 4)
                    if f == 0:
                        outputs(stage, b0 + 8, 8, c0, True)
                outputs(stage, b0 + 24, 20, c0, layer == 0, add=True)

            def up_low(n, q, c0, first):
                dve.wait_ge(sg("up_square"), n + first + 1)
                dve.wait_ge(sg("up_hi"), n + first + 1)
                dve.tensor_tensor(ULO[:, bass.ds(n, 1), c0:T], SQT[:, q:q + 1, c0:T],
                                  UHI[:, bass.ds(n, 1), c0:T].bitcast(F32), ALU.subtract).then_inc(sg("up_lo"), 1)

            outputs("wout", FIRST["wout"], 0, 0, True)
            fuse(0, "mix_post_g", "mlp_pre_g", 0, 0, G_FIRST["mlp0"], 0)
            mlp(0, 0)
            fuse(1, "mlp_post_g", "mix_pre_g", 0, 1, G_FIRST["lru"], 0)

            lam = VB[:, PACK_B["rg_lambda"][0]:PACK_B["rg_lambda"][0] + LT]
            softplus("lam", LAM, lambda: dve.tensor_scalar(LAM[:, 0, :], lam, -1.0, None, ALU.mult))
            dve.tensor_scalar(cl[:, :], LAM[:, 0, :], -8.0, None, ALU.mult).then_inc(sg("lru_c"), 1)
            dve.wait_ge(sg("halo_ready"), 2)
            lnames = ["lconv_tap0", "lconv_tap1", "lconv_tap2", "lconv_tap3"]

            b_lru, t_lru = FIRST["lru"], G_FIRST["lru"]

            def lru_conv(i, s):
                if s == 0:
                    dve.wait_ge(sg("tile_done"), i * 2 + DONE["lru"] + 1)
                else:
                    dve.wait_ge(sg("w_used"), i * 2 + b_lru + 3)
                tile_out(LRAW[:, s, 3:T + 3], s).then_inc(sg("g_evac"), 1)
                taps(LRAW[:, s, :], LACC[:, s, :], "rg_conv_w", lambda j: i * 2 + (s + 10 * j), lnames, i * 2 + s + 1,
                     i * 4 + s + t_lru + 3)

            def lru_gate_out(i, s):
                if s == 0:
                    dve.wait_ge(sg("tile_done"), i * 2 + DONE["lru"] + 2)
                else:
                    dve.wait_ge(sg("w_used"), i * 2 + b_lru + 4)
                tile_out(GATE[:, bass.ds(i * 2 + s, 1), :], s).then_inc(sg("g_evac"), 1)

            def lru_expm1(j):
                for s in range(2):
                    dve.wait_ge(sg("lru_th"), j * 2 + (s + 1))
                    dve.wait_ge(sg("lru_a2"), j * 2 + (s + 1))
                    dve.scalar_tensor_tensor(out=TH[:, s, :], in0=A2[:, s, :], scalar=1.0, in1=TH[:, s, :],
                                             op0=ALU.add, op1=ALU.mult).then_inc(sg("lru_q"), 1)

            def lru_scan(j):
                for s in range(2):
                    dve.wait_ge(sg("lru_root"), j * 2 + (s + 1))
                    dve.wait_ge(sg("lru_ix"), j * 2 + (s + 1))
                    dve.tensor_tensor(TMP[:, s, :], TH[:, s, :], IG[:, s, :], ALU.mult).then_inc(sg("lru_u"), 1)
                for s in range(2):
                    dve.wait_ge(sg("lru_u"), j * 2 + (s + 1))
                    dve.tensor_tensor_scan(A2[:, s, :], RG[:, s, :], TMP[:, s, :], 0.0, ALU.mult, ALU.add
                                           ).then_inc(sg("lru_scan"), 1)
                for s in range(2):
                    dve.wait_ge(sg("lru_scan"), j * 2 + (s + 1))
                    dve.wait_ge(sg("gelu_ready"), j * 2 + (s + 1))
                    dve.tensor_tensor(SQT[:, s:s + 1, :], A2[:, s:s + 1, :], GATE[:, bass.ds(j * 2 + s, 1), :], ALU.mult
                                      ).then_inc(sg("lru_gated"), 1)

            def lru_low(j):
                for s in range(2):
                    dve.wait_ge(sg("lru_hi"), j * 2 + (s + 1))
                    dve.tensor_tensor(GLO[:, bass.ds(j * 2 + s, 1), :], SQT[:, s:s + 1, :],
                                      GHI[:, bass.ds(j * 2 + s, 1), :].bitcast(F32), ALU.subtract
                                      ).then_inc(sg("lru_lo"), 1)

            def lru_turn(i, j, turns):
                split(b_lru + 1, i, turns)
                lru_conv(i, 0)
                lru_expm1(j)
                lru_conv(i, 1)
                lru_scan(j)
                split(b_lru + 2, i, turns)
                lru_gate_out(i, 0)
                lru_low(j)
                lru_gate_out(i, 1)

            lru_conv(0, 0)
            lru_conv(0, 1)
            split(b_lru + 2)
            lru_gate_out(0, 0)
            lru_gate_out(0, 1)
            with dve.Fori(1, LT // 2 - 1) as i:
                lru_turn(i, i - 1, LT // 2 - 1)
            lru_turn(LT // 2 - 1, LT // 2 - 2, 1)
            j = LT // 2 - 1
            split(b_lru + 1, LT // 2)
            lru_expm1(j)
            lru_scan(j)
            lru_low(j)

            def rgo(i):
                b = FIRST["rgo"]
                for s in range(2):
                    dve.wait_ge(sg("w_used"), i * 2 + b + s + 3)
                    out_tile(i * 2 + s, s, META, False).then_inc(sg("g_evac"), 1)
                    split(b + 2 + s, i, 3)

            with dve.Fori(0, 3) as i:
                rgo(i)
            rgo(3)
            fuse(2, "mix_post_g", "mlp_pre_g", 1, 1, G_FIRST["mlp1"], META)
            mlp(1, META)
            fuse(3, "mlp_post_g", None, 1, 0, G_FIRST["mlp1"] + 48, META)
            for c in range(4):
                dve.wait_ge(sg("out_turned"), 2 * c + 2)
                dve.tensor_copy(OUTN[:, c, 512:1024], PS[:, 4 + (2 * c + 1) % 4, :]).then_inc(sg("out_rows_dve"), 1)



def shape_constants():
    import numpy as np
    rows, cols = np.arange(P)[:, None], np.arange(P)[None, :]
    freq = np.float32(10000.0) ** (-np.arange(0, ROPE, 2, dtype=np.float32) / np.float32(ROPE))
    angle = (freq[:, None] * np.arange(T, dtype=np.float32)[None, :]).astype(np.float64)
    cos, sin = np.cos(angle), np.sin(angle)
    return {"c_ident": np.eye(P, dtype=np.float32),
            "c_neg": np.where(cols <= rows, 0.0, -1e30).astype(np.float32),
            "c_triu": (rows <= cols).astype(np.float32),
            "c_cs": np.concatenate([np.ones((NOPE, T)), cos, cos, -sin, sin]).astype(np.float32)}


def kernel(**inputs):
    import numpy as np
    import concourse.bacc as bacc
    from concourse.bass_utils import run_bass_kernel_spmd

    nc = bacc.Bacc("TRN2", target_bir_lowering=False, num_devices=1)
    arrays, args = {}, {}
    for name, value in {**inputs, **shape_constants()}.items():
        a = np.ascontiguousarray(value)
        arrays[f"in_{name}_dram"] = a
        args[name] = nc.dram_tensor(f"in_{name}_dram", a.shape, mybir.dt.from_np(a.dtype), kind="ExternalInput").ap()
    out = nc.dram_tensor("out_0_dram", (1, SEQ, D), F32, kind="ExternalOutput").ap()
    build(nc, args, out)
    result = run_bass_kernel_spmd(nc, [arrays], core_ids=[0])
    return result.results[0]["out_0_dram"]
```

```python
from contextlib import ExitStack

import concourse.bass as bass
from concourse import mybir

F32 = mybir.dt.float32
F32R = mybir.dt.float32r
ACT = mybir.ActivationFunctionType
ALU = mybir.AluOpType
AX = mybir.AxisListType

P = 128
D = 1024
KT = D // P
SEQ = 512
META = 16
T = META + SEQ
HALF = T // 2
DFF = 4 * D
EPS = 1e-6

INNER = 1024
XBC = 1536
DT_COL = INNER + XBC
CQ_COL = DT_COL + 16
CKV_COL = CQ_COL + 384
KR_COL = CKV_COL + 256
HEADS = 16
NOPE, ROPE, VD = 64, 32, 64
QRANK, KVRANK = 384, 256
SCALE = float(NOPE + ROPE) ** -0.5
CHUNKS = [(0, META)] + [(META + P * c, P) for c in range(SEQ // P)]

LRU = 1280
LT = LRU // P

PACK_A = {"mix_pre_g": (0, 16), "mix_post_g": (16, 16), "mlp_pre_g": (32, 16), "mlp_post_g": (48, 16),
          "ssd_conv_w": (64, 48), "ssd_conv_b": (112, 12)}
PACK_B = {"ssd_norm_g": (0, 8), "mla_q_norm_g": (8, 3), "mla_kv_norm_g": (11, 2), "rg_conv_w": (13, 40),
          "rg_conv_b": (53, 10), "rg_b_a": (63, 10), "rg_b_i": (73, 10), "rg_lambda": (83, 10)}
ROWS_A, ROWS_B = 124, 93
FIRST_SMALL = 2 + len(PACK_A)
CONSTS = 3 + len(PACK_B) + 3
BEFORE = {"qn": (0, 0), "kvn": (3, 1), "yn": (5, 2), "prep0": (0, 0), "prep1": (KT, 1), "prep2": (2 * KT, 2),
          "prep3": (3 * KT, 3)}
SQUARES_AHEAD = 3
DT_STEPS = 11

STREAM = [("cq", 1, 1, 2048), ("misc", 1, 5, 2048), ("ckv", 1, 1, 2048), ("win", 10, 1, 2048),
          ("att", 8, 13, 1280), ("wout", 8, 1, 2048), ("mlp0", 32, 1, 2048),
          ("lru", 10, 1, 2048), ("rgo", 8, 1, 1280), ("mlp1", 32, 1, 2048)]
FIRST, _b = {}, 0
for _n, _k, _, _ in STREAM:
    FIRST[_n] = _b
    _b += _k
BLOCKS = _b
_of = [row for row in STREAM for _ in range(row[1])]


def landed(b):
    return 16 * sum(_of[i][2] for i in range(b % 2, b + 1, 2))


def floats(b):
    return _of[b][3]

G_FIRST, _t = {}, 0
for _n, _k in [("cq", 2), ("misc", 2), ("ckv", 2), ("win", 20), ("wout", 8), ("mlp0", 48), ("lru", 20),
               ("rgo", 8), ("mlp1", 48)]:
    G_FIRST[_n] = _t
    _t += _k

DONE = {}
_t = 0
for _n, _k in [("cq", 1), ("misc", 1), ("ckv", 1), ("win", 10), ("att", 24), ("wout", 4), ("mlp0", 24),
               ("lru", 10), ("rgo", 0), ("mlp1", 24)]:
    DONE[_n] = _t
    _t += _k


def build(nc, A, out):
    with ExitStack() as ctx:
        TB = 4 * T
        base = (nc.sbuf_base + 31) // 32 * 32

        def at(name, tile, shape, dt=F32, extra=0):
            return nc.alloc_sbuf_tensor_at(name, shape, dt, offset=base + tile * TB + extra)

        H = at("h_res", 0, [P, KT, T])
        RAW = at("w_raw", 8, [P, 2, 2048])
        WHI = at("w_hi", 8, [P, 2, 2048], F32R, 16384)
        WLO = at("w_lo", 8, [P, 2, 2048], F32R, 32768)
        Z0 = 32
        RS = at("rstd", Z0, [P, T])
        SQA = at("sq_sum", Z0 + 1, [P, T])
        SQT = at("sq_tmp", Z0 + 2, [P, 2, T])
        TMP = at("tmp", Z0 + 4, [P, 2, T])
        U0 = Z0 + 6
        UHI = at("u_hi", U0, [P, 16, T], F32R)
        ULO = at("u_lo", U0 + 16, [P, 16, T], F32R)
        A0 = U0 + 32
        AHI = at("a_hi", A0, [P, KT, T], F32R)
        ALO = at("a_lo", A0 + 8, [P, KT, T], F32R)
        M0 = A0 + 16
        M = at("mix_out", M0, [P, KT, T])
        C0 = M0 + 10
        ident = at("ident", C0, [P, P])
        neg = at("neg_mask", C0, [P, P], F32, 512)
        triu = at("triu", C0, [P, P], F32, 1024)
        ones = at("ones", C0, [P, P], F32, 1536)
        CS = at("rope_cs", C0 + 1, [P, T])
        VA = at("vec_a", C0 + 2, [P, ROWS_A])
        VB = at("vec_b", C0 + 2, [P, ROWS_B], F32, 512)
        heads_in = at("heads_in", C0 + 2, [P, 2, HEADS], F32, 1024)
        expA = at("exp_a", C0 + 2, [P, HEADS], F32, 1152)
        dskip = at("d_skip", C0 + 2, [P, KT], F32, 1216)
        dtb = at("dt_bias", C0 + 2, [HEADS, 1], F32, 1248)
        cl = at("lru_c", C0 + 2, [P, LT], F32, 1280)
        eps = at("eps", C0 + 2, [P, 1], F32, 1600)
        RT = at("rstd_post", C0 + 2, [P, 5], F32, 1632)
        LAM = at("lam_work", C0 + 2, [P, 4, LT], F32, 1440)
        assert base + (C0 + 4) * TB <= nc.sbuf_usable_end, (base, C0)
        XN = at("x_rows", U0, [P, 4, D])
        MN = at("meta_rows", U0 + 8, [META, D])
        PKA = at("pack_a", U0 + 10, [ROWS_A, P])
        PKB = at("pack_b", U0 + 10, [ROWS_B, P], F32, 512)
        C5 = at("latent_raw", U0, [P, 5, T])
        MISC = at("misc", U0 + 5, [P, T])
        CACC = at("conv_acc", U0 + 6, [P, 2, T])
        Z = at("z_gate", U0 + 8, [P, KT, T])
        XC = at("xbc_conv", U0 + 16, [P, 12, T])
        XRAW = at("conv_in", U0 + 28, [P, 2, T + 3])
        RLQ = at("rstd_latent_q", U0 + 31, [P, T])
        RLK = at("rstd_latent_kv", C0 + 3, [P, T])
        LHI = at("latent_hi", M0, [P, 5, T], F32R)
        LLO = at("latent_lo", M0 + 5, [P, 5, T], F32R)
        KRS = at("k_rope", C0 + 3, [P, T])
        DTC = at("dt_work", U0, [HEADS, 4, T])
        YT = at("ssd_y", U0 + 1, [P, KT, P])
        XS = at("ssd_chunk", U0 + 3, [P, 12, P])
        DTT = at("ssd_dt", U0 + 6, [P, 5, HEADS])
        DA = at("ssd_da", U0 + 6, [P, 5, HEADS], F32, 320)
        DTE = at("ssd_to_end", U0 + 6, [P, HEADS], F32, 640)
        CD = at("ssd_chunk_decay", U0 + 6, [P, HEADS], F32, 704)
        ACS = at("ssd_acs", U0 + 6, [P, HEADS], F32, 768)
        DAC = at("ssd_da_chunk", U0 + 6, [P, HEADS], F32, 832)
        MT = at("ssd_mt", U0 + 28, [P, HEADS, P])
        E = at("ssd_decay", A0, [P, HEADS, P])
        ER = at("ssd_exp", A0 + 4, [P, HEADS, P])
        HST = at("ssd_state", A0 + 8, [P, HEADS, VD])
        XDT = at("ssd_xdt", A0 + 10, [P, HEADS, VD])
        XDE = at("ssd_xde", A0 + 12, [P, HEADS, VD])
        BT = at("ssd_bt", A0 + 14, [P, 2, P])
        CBM = at("ssd_cb", A0 + 14, [P, 2, P], F32, 1024)
        QB = at("q_heads", A0, [P, 2, 2, T])
        KB = at("k_heads", A0 + 4, [P, 2, 2, T])
        VH = at("v_heads", A0 + 8, [P, 2, 5, 2, VD])
        PTS = at("probs_t", A0 + 13, [P, 2, 5, P])
        neg_r = at("neg_mask_r", A0 + 15, [P, P], F32R, 1024)
        ident_r = at("ident_r", A0 + 15, [P, P], F32R, 1536)
        MX = at("row_max", A0 + 12, [P, 2, 1])
        SUM = at("row_sum", A0 + 12, [P, 2, 1], F32, 32)
        PR = at("probs", Z0 + 2, [P, 2, T])
        GATE = at("lru_gate", U0, [P, LT, T])
        GHI = at("lru_hi", U0, [P, LT, T], F32R)
        GLO = at("lru_lo", U0 + 10, [P, LT, T], F32R)
        GWR = at("gate_w_raw", M0, [P, 2, 2, P])
        GWH = at("gate_w_hi", M0 + 1, [P, 2, 2, P], F32R)
        GWL = at("gate_w_lo", M0 + 2, [P, 2, 2, P], F32R)
        LRAW = at("lru_in", U0 + 20, [P, 2, T + 3])
        LACC = at("lru_conv", U0 + 23, [P, 2, T])
        XRH = at("lru_x_hi", U0 + 25, [P, 2, T], F32R)
        XRL = at("lru_x_lo", U0 + 27, [P, 2, T], F32R)
        IG = at("lru_i", U0 + 29, [P, 2, T])
        RG = at("lru_r", M0 + 3, [P, 2, T])
        TH = at("lru_tanh", M0 + 5, [P, 2, T])
        A2 = at("lru_a_squared", M0 + 7, [P, 2, T])
        OUTN = at("out_rows", U0, [P, 4, D])

        PS = ctx.enter_context(nc.psum_tensor("psum", [P, 8, 512], F32))

        made = {}

        def sg(name):
            if name not in made:
                made[name] = ctx.enter_context(nc.semaphore(name))
            return made[name]

        def post_rstd(c0):
            return PS[:, 6:8, :].rearrange("p b t -> p (b t)")[:, 512 - META + c0:512 - META + T]

        def chunks_from(c0):
            return [(c, t0, L) for c, (t0, L) in enumerate(CHUNKS) if t0 >= c0]

        LATENT_SQUARES = [SQT[:, 0, :], SQT[:, 1, :], TMP[:, 0, :], TMP[:, 1, :], SQA[:, :]]

        def step(name, what):
            return sg(("pre_" if name.startswith("prep") else "norm_") + what)

        def g_tile(q, w, rows=slice(0, P)):
            return PS[rows, 2 * q:2 * q + 2, 0:w // 2]

        def two(ap):
            if len(ap.shape) == 3:
                return ap.rearrange("p o (h t) -> p (o h) t", h=2)
            return ap.rearrange("p (h t) -> p h t", h=2)

        def vec(name, j):
            if name in PACK_A:
                return VA[:, bass.ds(PACK_A[name][0] + j, 1)]
            return VB[:, bass.ds(PACK_B[name][0] + j, 1)]

        def placed(b, i, turns):
            if isinstance(i, int):
                b += 2 * i
                return (b % 2, floats(b), landed(b), b + 1) if b < BLOCKS else None
            step = landed(b + 2) - landed(b)
            for j in range(turns):
                assert landed(b + 2 * j) == landed(b) + step * j and floats(b + 2 * j) == floats(b)
            return b % 2, floats(b), i * step + landed(b), i * 2 + b + 1

        def chunk(c, it):
            return (0, META, 1) if c == 0 else (it * P + META, P, it + 2)

        def unit(n):
            t0, L = CHUNKS[n % 5]
            return t0, L, t0 + L

        Q_TERMS = {2: (0, [0]), 3: (0, [1, 2]), 4: (1, [0]), 5: (1, [1]), 6: (1, [2])}
        K_TERMS = {7: [0, 1]}
        V_BLOCKS = {8: [1, 2], 9: [3, 4, 0]}
        Q_STEPS, K_STEP, V_STEP = (3, 6), 7, 9
        Y_FULL, Y_HIGH, Y_LOW = 7, 8, 9
        META_OUT = slice(384, 384 + META)

        def ago(i, s, n, k):
            s, n = (s, n - k) if n >= k else (s - 1, n - k + 10)
            number = i * 20 + (10 * s + n)
            if isinstance(i, int) and number < 0:
                return None
            return s % 2, n, number

        block = ctx.enter_context(nc.Block())

        @block.sync
        def _(sp):
            for c in range(4):
                sp.dma_start(XN[:, c, :], A["x"][0, P * c:P * (c + 1), :]).then_inc(sg(f"x_landed_{c}"), 16)

            def wait_slot(b):
                sp.wait_ge(sg("w_hi_made"), b - 1)
                sp.wait_ge(sg("w_lo_made"), b - 1)

            def put(s, src, k=KT):
                m = src.shape[1]
                sp.dma_start(RAW[:, s, 0:k * m].rearrange("p (k m) -> p k m", k=k),
                             src.rearrange("(k p) m -> p k m", p=P)).then_inc(sg(f"w_landed_{s}"), 16)

            w_in = A["w_in"][0]
            put(0, w_in[:, CQ_COL:CQ_COL + 256])
            slot = RAW[:, 1, :].rearrange("p (k m) -> p k m", k=KT)
            for dst, src, n in [(0, CQ_COL + 256, P), (P, DT_COL, HEADS), (P + 64, KR_COL, ROPE),
                                (P + 96, KR_COL + ROPE // 2, ROPE // 2), (P + 112, KR_COL, ROPE // 2)]:
                sp.dma_start(slot[:, :, dst:dst + n], w_in[:, src:src + n].rearrange("(k p) m -> p k m", p=P)
                             ).then_inc(sg("w_landed_1"), 16)
            wait_slot(FIRST["ckv"])
            put(0, w_in[:, CKV_COL:CKV_COL + 256])
            b0 = FIRST["win"]
            with sp.Fori(0, 3) as i:
                for s in range(2):
                    wait_slot(i * 2 + b0 + s)
                    put((b0 + s) % 2, w_in[:, bass.ds(i * 512 + INNER + 256 * s, 256)])
            with sp.Fori(0, 2) as i:
                for s in range(2):
                    wait_slot(i * 2 + b0 + 6 + s)
                    put((b0 + s) % 2, w_in[:, bass.ds(i * 512 + 256 * s, 256)])

            wq = A["mla_w_q_up"][0].rearrange("(k p) (h c) -> p k h c", p=P, h=HEADS)
            wkv = A["mla_w_kv_up"][0].rearrange("(k p) (h c) -> p k h c", p=P, h=HEADS)

            def put_heads(s, pair):
                landed_s = sg(f"w_landed_{s}")
                q = RAW[:, s, 0:768].rearrange("p (k h c) -> p k h c", k=3, h=2)
                kv = RAW[:, s, 768:1280].rearrange("p (v k h c) -> p v k h c", v=2, k=2, h=2)
                hs = bass.ds(pair * 2, 2)
                for k in range(3):
                    sp.dma_start(q[:, k, :, 0:96], wq[:, k, hs, :]).then_inc(landed_s, 16)
                    sp.dma_start(q[:, k, :, 96:112], wq[:, k, hs, 80:96]).then_inc(landed_s, 16)
                    sp.dma_start(q[:, k, :, 112:128], wq[:, k, hs, 64:80]).then_inc(landed_s, 16)
                for k in range(2):
                    for v in range(2):
                        sp.dma_start(kv[:, v, k], wkv[:, k, hs, VD * v:VD * (v + 1)]).then_inc(landed_s, 16)

            b0 = FIRST["att"]
            with sp.Fori(0, 4) as i:
                for s in range(2):
                    wait_slot(i * 2 + b0 + s)
                    put_heads((b0 + s) % 2, i * 2 + s)

            b0 = FIRST["wout"]
            with sp.Fori(0, 4) as i:
                for s in range(2):
                    wait_slot(i * 2 + b0 + s)
                    put((b0 + s) % 2, A["w_out_ab"][0, D * s:D * (s + 1), bass.ds(i * 256, 256)])

            def mlp(layer):
                b0 = FIRST[f"mlp{layer}"]
                for f in range(2):
                    with sp.Fori(0, 4) as i:
                        for s in range(2):
                            wait_slot(i * 2 + b0 + 16 * f + s)
                            put((b0 + s) % 2, A["w_up"][layer, :, bass.ds(i * 512 + DFF // 2 * f + 256 * s, 256)])
                    with sp.Fori(0, 4) as i:
                        for s in range(2):
                            wait_slot(i * 2 + b0 + 16 * f + 8 + s)
                            r = DFF // 2 * f + D * s
                            put((b0 + s) % 2, A["w_down"][layer, r:r + D, bass.ds(i * 256, 256)])

            def put_gates(s, n):
                for g, name in enumerate(("rg_w_a", "rg_w_i")):
                    sp.dma_start(GWR[:, s, g, :], A[name][0, bass.ds(n, 1), :, :].rearrange("o i j -> (o i) j")
                                 ).then_inc(sg(f"gw_landed_{s}"), 16)

            mlp(0)
            b0 = FIRST["lru"]
            names = ("rg_w_x", "rg_w_y")
            for s in range(2):
                wait_slot(b0 + s)
                put((b0 + s) % 2, A[names[s]][0, :, 0:256])
            sp.wait_ge(sg("fuse_term"), 2 * KT)
            for s in range(2):
                put_gates(s, s)
            with sp.Fori(1, LT // 2) as i:
                for s in range(2):
                    wait_slot(i * 2 + b0 + s)
                    put((b0 + s) % 2, A[names[s]][0, :, bass.ds(i * 256, 256)])
                for s in range(2):
                    sp.wait_ge(sg("gw_hi_made"), i * 2 + s - 1)
                    sp.wait_ge(sg("gw_lo_made"), i * 2 + s - 1)
                    put_gates(s, i * 2 + s)
            b0 = FIRST["rgo"]
            with sp.Fori(0, 4) as i:
                for s in range(2):
                    wait_slot(i * 2 + b0 + s)
                    put((b0 + s) % 2, A["rg_w_out"][0, :, bass.ds(i * 256 + P * s, P)], k=LT)
            mlp(1)
            for c in range(4):
                sp.wait_ge(sg("out_rows_act"), c + 1)
                sp.wait_ge(sg("out_rows_dve"), c + 1)
                sp.dma_start(out[0, P * c:P * (c + 1), :], OUTN[:, c, :]).then_inc(sg("out_stored"), 16)
            sp.wait_ge(sg("out_stored"), 64)

        @block.gpsimd
        def _(pool):
            pool.memset(ones[:, :], 1.0).then_inc(sg("ones_ready"), 1)
            gap = RAW[:, 1, :].rearrange("p (k m) -> p k m", k=KT)[:, :, P + HEADS:P + 64]
            pool.memset(gap, 0.0).then_inc(sg("gap_zero"), 1)
            pool.memset(eps[:, :], EPS).then_inc(sg("ones_ready"), 1)
            pool.sem_inc(sg("m_summed"), 2)

            def sums(first, n, c0):
                with pool.Fori(0, n // 2) as i:
                    for s in range(2):
                        pool.wait_ge(sg("m_squared"), i * 2 + first + s + 1)
                        pool.wait_ge(sg("m_summed"), i * 2 + first + s + 2)
                        pool.tensor_tensor(SQA[:, c0:T], SQA[:, c0:T], SQT[:, s, c0:T], ALU.add
                                           ).then_inc(sg("m_summed"), 1)

            def residual(u, c0):
                for k in range(0, KT, 1 if u < 3 else 2):
                    pool.wait_ge(sg("fuse_term"), KT * u + k + 1)
                    pool.tensor_tensor(H[:, k, c0:T], H[:, k, c0:T], TMP[:, k % 2, c0:T], ALU.add
                                       ).then_inc(sg("fuse_h"), 1)
                if u < 3:
                    pool.memset(SQA[:, :], 0.0).then_inc(sg("sqa_zero"), 1)
                    pool.wait_ge(sg("sqa_zero"), u + 2)

            def squares_up(first, c0):
                with pool.Fori(0, 8) as i:
                    for s in range(2):
                        pool.wait_ge(sg("g_evac"), i * 2 + first + s + 3)
                        pool.tensor_tensor(SQT[:, s, c0:T], TMP[:, s, c0:T], TMP[:, s, c0:T], ALU.mult
                                           ).then_inc(sg("up_square"), 1)

            def ssd(c, it=None):
                t0, L, v = chunk(c, it)
                pool.wait_ge(sg("ssd_staged"), v)
                if c > 0:
                    pool.wait_ge(sg("ssd_y_done"), v - 1)
                pool.tensor_tensor(YT[:, :, 0:L], XS[:, 0:KT, 0:L],
                                   dskip[:, :].unsqueeze(2).to_broadcast([P, KT, L]), ALU.mult
                                   ).then_inc(sg("ssd_skip"), 1)
                if c > 0:
                    pool.wait_ge(sg("ssd_cd"), v)
                    pool.wait_ge(sg("ssd_y_mm"), v)
                    pool.tensor_tensor(HST[:, :, :], HST[:, :, :], CD[:, :].unsqueeze(2).to_broadcast([P, HEADS, VD]),
                                       ALU.mult).then_inc(sg("ssd_state_decayed"), 1)
                pool.wait_ge(sg("ssd_y_out"), v)
                z = Z[:, :, bass.ds(t0, L)]
                pool.tensor_tensor(z, z, YT[:, :, 0:L], ALU.mult).then_inc(sg("ssd_y_done"), 1)

            pool.memset(XRAW[:, :, 0:3], 0.0).then_inc(sg("halo_ready"), 1)
            pool.wait_ge(sg("d_skip_ready"), 2)
            pool.wait_ge(step("kvn", "ss"), 5)
            pool.memset(SQA[:, :], 0.0).then_inc(sg("sqa_zero"), 1)
            pool.wait_ge(sg("z_ready"), 8)
            ssd(0)
            with pool.Fori(0, 4) as it:
                ssd(1, it)

            pool.wait_ge(sg("ssd_y_done"), 5)
            pool.wait_ge(sg("ssd_state"), 5)
            pool.wait_ge(step("yn", "ss"), 5 + KT)
            pool.memset(PR[:, :, :], 0.0).then_inc(sg("probs_zero"), 1)

            pool.wait_ge(sg("sqa_zero"), 1)
            sums(0, 8, 0)
            residual(0, 0)
            for f in range(2):
                squares_up(G_FIRST["mlp0"] + 24 * f, 0)
            sums(8, 8, 0)
            residual(1, 0)
            pool.memset(LRAW[:, :, 0:3], 0.0).then_inc(sg("halo_ready"), 1)


            def lru_lows(i):
                for s in range(2):
                    pool.wait_ge(sg("gw_hi_made"), i * 2 + s + 1)
                    pool.tensor_tensor(GWL[:, s, :, :], GWR[:, s, :, :], GWH[:, s, :, :].bitcast(F32), ALU.subtract
                                       ).then_inc(sg("gw_lo_made"), 1)
                for s in range(2):
                    pool.wait_ge(sg("xr_hi"), i * 2 + s + 1)
                    pool.tensor_tensor(XRL[:, s, :], LACC[:, s, :], XRH[:, s, :].bitcast(F32), ALU.subtract
                                       ).then_inc(sg("xr_lo"), 1)

            def lru_input_gated(j):
                for s in range(2):
                    pool.wait_ge(sg("lru_i"), j * 2 + (s + 2))
                    pool.tensor_tensor(IG[:, s, :], IG[:, s, :], LACC[:, s, :], ALU.mult).then_inc(sg("lru_ix"), 1)

            lru_lows(0)
            with pool.Fori(1, LT // 2) as i:
                lru_input_gated(i - 1)
                lru_lows(i)
            lru_input_gated(LT // 2 - 1)
            sums(16, 8, META)
            residual(2, META)
            for f in range(2):
                squares_up(G_FIRST["mlp1"] + 24 * f, META)
            sums(24, 8, META)
            residual(3, META)

        @block.scalar
        def _(act):
            landed_c, landed_first = sg("consts_landed"), sg("first_consts_landed")

            def load_pack(pack, dst, landed_by):
                for name, (row, n) in pack.items():
                    src = A[name]
                    src = src.rearrange("a b c -> (a b c)") if len(src.shape) == 3 else src.rearrange("a b -> (a b)")
                    act.dma_start(dst[row:row + n, :], src.rearrange("(n p) -> n p", p=P)).then_inc(landed_by, 16)

            act.dma_start(ident[:, :], A["c_ident"]).then_inc(landed_first, 16)
            act.dma_start(MN[:, :], A["meta_tokens"]).then_inc(landed_first, 16)
            load_pack(PACK_A, PKA, landed_first)
            load_pack(PACK_B, PKB, landed_c)
            for name, dst in (("c_neg", neg), ("c_triu", triu), ("c_cs", CS)):
                act.dma_start(dst[:, :], A[name]).then_inc(landed_c, 16)
            act.dma_start(heads_in[:, 0, :], A["ssd_a_log"].to_broadcast([P, HEADS])).then_inc(landed_c, 16)
            act.dma_start(heads_in[:, 1, :], A["ssd_d"].to_broadcast([P, HEADS])).then_inc(landed_c, 16)
            act.dma_start(dtb[:, :], A["ssd_dt_bias"].rearrange("a b -> b a"), allow_slow_non_contiguous=True
                          ).then_inc(landed_c, 16)

            def split(b, i=0, turns=1):
                at_b = placed(b, i, turns)
                if at_b:
                    s, n, landed_at, free_at = at_b
                    act.wait_ge(sg(f"w_landed_{s}"), landed_at)
                    act.wait_ge(sg("w_used"), free_at)
                    act.activation(WHI[:, s, 0:n], RAW[:, s, 0:n], ACT.Copy).then_inc(sg("w_hi_made"), 1)

            for tau in range(5):
                t0, L = CHUNKS[tau]
                act.wait_ge(sg("x_turned"), 2 * tau + 1)
                act.copy(H[:, 0:4, t0:t0 + L], PS[:, 4 + 2 * tau % 4, :].rearrange("p (k t) -> p k t", k=4)[:, :, 0:L]
                         ).then_inc(sg("x_in_act"), 1)
            split(0)

            def prep(u, name, layer, c0, after):
                name_u, t = f"prep{u}", KT * u
                for k in range(KT):
                    if after:
                        act.wait_ge(sg("fuse_h"), t - KT + k + 1)
                    act.activation(AHI[:, k, c0:T], H[:, k, c0:T], ACT.Identity, scale=vec(name, KT * layer + k)
                                   ).then_inc(step(name_u, "hi"), 1)
                    if k >= 2:
                        act.wait_ge(step(name_u, "ss"), t + k - 1)
                    act.activation(SQT[:, k % 2, c0:T], H[:, k, c0:T], ACT.Square).then_inc(step(name_u, "sq"), 1)
                act.wait_ge(step(name_u, "ss"), t + KT)
                act.activation(two(RS[:, c0:T]), g_tile(2, T - c0), ACT.Sqrt, scale=1.0 / D, bias=eps[:, :]
                               ).then_inc(step(name_u, "root"), 1)

            act.wait_ge(sg("vecs_ready"), 1)
            act.wait_ge(sg("x_in_act"), 5)
            act.wait_ge(sg("x_in_dve"), 5)
            act.wait_ge(sg("ones_ready"), 2)
            prep(0, "mix_pre_g", 0, 0, False)
            act.wait_ge(sg("gap_zero"), 1)
            split(1)

            act.wait_ge(sg("halo_ready"), 1)

            def conv_tap3(m, q):
                act.wait_ge(sg("g_evac"), m + G_FIRST["win"] + 3)
                act.activation(CACC[:, q, :], XRAW[:, q, 3:T + 3], ACT.Identity, scale=vec("ssd_conv_w", m + 36),
                               bias=vec("ssd_conv_b", m)).then_inc(sg("conv_tap3"), 1)

            def conv_silu(m, q):
                act.wait_ge(sg("conv_tap2"), m + 1)
                act.activation(XC[:, bass.ds(m, 1), :], CACC[:, q:q + 1, :], ACT.Silu).then_inc(sg("xbc_ready"), 1)

            def conv_block(i, s, turns=1):
                m = i * 4 + 2 * s
                conv_tap3(m, 0)
                conv_silu(m, 0)
                conv_tap3(m + 1, 1)
                split(FIRST["win"] + 2 + s, i, turns)
                conv_silu(m + 1, 1)

            def highs(name, n, dst):
                t, _ = BEFORE[name]
                for k in range(n):
                    act.wait_ge(step(name, "full"), t + k + 1)
                    act.activation(dst(k), TMP[:, k % 2, :], ACT.Copy).then_inc(step(name, "hi"), 1)

            def squares_root(name, src, n, width):
                t, _ = BEFORE[name]
                for k in range(n):
                    if k >= 2:
                        act.wait_ge(step(name, "ss"), t + k - 1)
                    act.activation(SQT[:, k % 2, :], src(k), ACT.Square).then_inc(step(name, "sq"), 1)
                act.wait_ge(step(name, "ss"), t + n)
                act.activation(two(RS[:, :]), g_tile(2, T), ACT.Sqrt, scale=1.0 / width, bias=eps[:, :]
                               ).then_inc(step(name, "root"), 1)

            for b in (2, 3, 4):
                split(b)
            act.wait_ge(sg("g_evac"), G_FIRST["win"] + 2)
            for k, sq in enumerate(LATENT_SQUARES):
                act.activation(sq, C5[:, k, :], ACT.Square).then_inc(step("qn", "sq"), 1)
            conv_block(0, 0)
            for name, bank, dst, width, n in (("qn", 2, RLQ, QRANK, 5), ("kvn", 3, RLK, KVRANK, 5)):
                act.wait_ge(step(name, "ss"), n)
                act.activation(two(dst[:, :]), g_tile(bank, T), ACT.Sqrt, scale=1.0 / width, bias=eps[:, :]
                               ).then_inc(step(name, "root"), 1)
            conv_block(0, 1)
            with act.Fori(1, 3) as i:
                for s in range(2):
                    conv_block(i, s, 3)

            act.wait_ge(landed_c, 16 * CONSTS)
            act.activation(expA[:, :], heads_in[:, 0, :], ACT.Exp).then_inc(sg("exp_a"), 1)

            def softplus_exp(name, x):
                act.wait_ge(sg(f"{name}_step"), 2)
                act.activation(x[:, 2, :], x[:, 1, :], ACT.Exp).then_inc(sg(f"{name}_act"), 1)

            def softplus_log(name, x):
                act.wait_ge(sg(f"{name}_step"), 3)
                act.activation(x[:, 3, :], x[:, 1, :], ACT.Ln).then_inc(sg(f"{name}_act"), 1)

            for n in range(8):
                if n == 1:
                    highs("qn", 3, lambda k: LHI[:, k, :])
                if n == 2:
                    highs("kvn", 2, lambda k: LHI[:, 3 + k, :])
                if n == 4:
                    softplus_exp("dt", DTC)
                if n == 5:
                    softplus_log("dt", DTC)
                if n == 3:
                    act.wait_ge(sg("k_rope_terms"), 1)
                    act.copy(TMP[64:96, 1, :], TMP[96:128, 0, :]).then_inc(sg("k_rope_moved"), 1)
                act.wait_ge(sg("g_evac"), G_FIRST["win"] + 12 + n + 3)
                act.activation(Z[:, n, :], Z[:, n, :], ACT.Silu).then_inc(sg("z_ready"), 1)
                if n % 2:
                    split(FIRST["win"] + 8 + n // 2)

            def stage(t0, L):
                act.copy(XS[:, :, 0:L], XC[:, :, bass.ds(t0, L)]).then_inc(sg("ssd_staged"), 1)

            def ssd(c, it=None, ahead=True):
                t0, L, v = chunk(c, it)
                act.wait_ge(sg("ssd_r_mm"), v)
                if c > 0:
                    act.wait_ge(sg("ssd_y_mm"), v - 1)
                act.activation(ER[:, :, 0:L].rearrange("p (b h) l -> p b h l", b=4),
                               PS[:, 0:4, :].rearrange("p b (h l) -> p b h l", h=4)[:, :, :, 0:L], ACT.Exp
                               ).then_inc(sg("ssd_er"), 1)
                act.wait_ge(sg("ssd_bt_mm"), v)
                if c > 0:
                    act.wait_ge(sg("ssd_s_mm"), v - 1)
                act.copy(BT[0:L, :, :], PS[0:L, 7, 0:256].rearrange("p (g n) -> p g n", g=2)).then_inc(sg("ssd_bt"), 1)
                act.wait_ge(sg("ssd_to_end_arg"), v)
                act.activation(DTE[0:L, :], DTE[0:L, :], ACT.Exp).then_inc(sg("ssd_to_end"), 1)
                act.wait_ge(sg("ssd_e_min"), v)
                act.activation(E[0:L, :, 0:L], E[0:L, :, 0:L], ACT.Exp).then_inc(sg("ssd_e"), 1)
                if ahead:
                    act.wait_ge(sg("ssd_c_decayed"), v)
                    act.wait_ge(sg("ssd_skip"), v)
                    act.wait_ge(sg("ssd_x_turned"), v)
                    stage(META if c == 0 else it * P + (META + P), P)

            act.wait_ge(sg("xbc_ready"), 12)
            act.wait_ge(sg("k_rope"), 1)
            act.wait_ge(sg("dt_turned"), 1)
            stage(0, META)
            ssd(0)
            with act.Fori(0, 3) as it:
                ssd(1, it)
            ssd(1, 3, ahead=False)
            act.wait_ge(sg("ssd_y_mm"), 5)

            for s in range(2):
                for h in range(2):
                    for rows in (slice(64, 96), slice(96, 128)):
                        act.copy(KB[rows, s, h, :], KRS[64:96, :]).then_inc(sg("k_rope_placed"), 1)
            act.activation(ident_r[:, :], ident[:, :], ACT.Copy).then_inc(sg("mask_r"), 1)
            act.activation(neg_r[:, :], neg[:, :], ACT.Copy).then_inc(sg("mask_r"), 1)

            def keys_out(i, s):
                act.wait_ge(sg("tile_done"), i * 6 + (3 * s + DONE["att"] + 3))
                act.copy(two(KB[0:64, s, 0, :]), g_tile(3, T, slice(0, 64))).then_inc(sg("k_first"), 1)
                act.copy(two(KB[0:64, s, 1, :]), g_tile(3, T, slice(64, 128))).then_inc(sg("k_ready"), 1)

            def values_out(i, s):
                act.wait_ge(sg("w_used"), i * 2 + (s + FIRST["att"] + 3))
                act.copy(VH[:, s, 1:5, :, :], PS[:, 6, :].rearrange("p (j h d) -> p j h d", j=4, h=2)
                         ).then_inc(sg("v_rows"), 1)
                act.copy(VH[0:META, s, 0, :, :], PS[0:META, 7, 0:P].rearrange("p (h d) -> p h d", h=2)
                         ).then_inc(sg("v_ready"), 1)

            def att_high(i, s):
                act.wait_ge(sg("o_mm"), i * 20 + (10 * s + 10))
                act.activation(UHI[:, bass.ds(i * 2 + (s + KT), 1), META:T], PS[:, 4 + s:5 + s, :], ACT.Copy
                               ).then_inc(sg("att_hi"), 1)

            def meta_high(i, s):
                act.wait_ge(sg("o_mm"), i * 20 + (10 * s + 6))
                act.activation(UHI[:, bass.ds(i * 2 + (s + KT), 1), 0:META], PS[:, 7:8, META_OUT], ACT.Copy
                               ).then_inc(sg("meta_hi"), 1)

            def attend(i, turns):
                for s in range(2):
                    for n in range(10):
                        _, L, w = unit(n)
                        act.wait_ge(sg("neg_max"), i * 20 + (10 * s + n + 1))
                        act.activation(PR[0:L, n % 2, 0:w], PS[0:L, 2 * (n % 2):2 * (n % 2) + 2, :].rearrange(
                            "p b t -> p (b t)")[:, 0:w], ACT.Exp, bias=MX[0:L, n % 2, :],
                            accum_out=SUM[0:L, n % 2, :]).then_inc(sg("exp_ready"), 1)
                        if n == Y_HIGH:
                            act.wait_ge(step("yn", "full"), i * 2 + (s + 6))
                            act.activation(UHI[:, bass.ds(i * 2 + s, 1), :], TMP[:, s:s + 1, :], ACT.Copy
                                           ).then_inc(step("yn", "hi"), 1)
                        if n == 4:
                            split(FIRST["att"] + s + 2, i, turns)
                        if n == 2 and not (isinstance(i, int) and i + s == 0):
                            att_high(*((i, 0) if s else (i - 1, 1)))
                        if n == K_STEP and not (isinstance(i, int) and i * 2 + s == 7):
                            keys_out(*((i + 1, 0) if s else (i, 1)))
                        if n == 8:
                            meta_high(i, s)
                        if n == V_STEP and not (isinstance(i, int) and i * 2 + s == 7):
                            values_out(*((i + 1, 0) if s else (i, 1)))

            keys_out(0, 0)
            values_out(0, 0)
            act.wait_ge(sg("ssd_y_done"), 5)
            squares_root("yn", lambda k: Z[:, k, :], KT, INNER)
            attend(0, 1)
            with act.Fori(1, 3) as i:
                attend(i, 3)
            attend(3, 1)
            att_high(3, 1)

            def square(t, m, s, c0, i):
                act.wait_ge(sg("g_evac"), i * 2 + t + s + 3)
                act.wait_ge(sg("m_summed"), i * 2 + m + s + 1)
                act.activation(SQT[:, s:s + 1, c0:T], M[:, bass.ds(i * 2 + s, 1), c0:T], ACT.Square
                               ).then_inc(sg("m_squared"), 1)

            def outputs(b, t, m, c0, two_blocks=True):
                def turn(i, turns=1):
                    if two_blocks:
                        split(b + 2, i, turns)
                    square(t, m, 0, c0, i)
                    if not two_blocks:
                        split(b + 2, i, turns)
                    square(t, m, 1, c0, i)
                    if not isinstance(i, int):
                        split(b + 3, i, turns)
                with act.Fori(0, 3) as i:
                    turn(i, 3)
                turn(3)

            def post_root(u, c0):
                act.wait_ge(sg("fuse_ss"), u + 1)
                if c0 == 0:
                    act.activation(RT[0:META, 0:1], PS[0:META, 4, 0:1], ACT.Sqrt, scale=1.0 / D, bias=eps[0:META, :]
                                   ).then_inc(sg("fuse_root_meta"), 1)
                act.activation(RT[:, 1:5], PS[:, 4, 1:5], ACT.Sqrt, scale=1.0 / D, bias=eps[:, :]
                               ).then_inc(sg("fuse_root"), 1)
                if u < 3:
                    split(FIRST[("mlp0", "lru", "mlp1")[u]] + 1)

            def mlp(layer, c0):
                b0, t0 = FIRST[f"mlp{layer}"], G_FIRST[f"mlp{layer}"]
                for f in range(2):
                    with act.Fori(0, 4) as i:
                        for s in range(2):
                            for q in range(2):
                                n = i * 4 + 2 * s + q
                                act.wait_ge(sg("g_evac"), n + t0 + 24 * f + 3)
                                act.activation(UHI[:, bass.ds(n, 1), c0:T], TMP[:, q:q + 1, c0:T], ACT.Square
                                               ).then_inc(sg("up_hi"), 1)
                                if q == 1:
                                    split(b0 + 16 * f + 2 + s, i, 4)
                    if f == 0:
                        with act.Fori(0, 4) as i:
                            for s in range(2):
                                split(b0 + 8 + 2 + s, i, 4)
                outputs(b0 + 24, t0 + 40, 8 + 16 * layer, c0)

            outputs(FIRST["wout"], G_FIRST["wout"], 0, 0)
            post_root(0, 0)
            prep(1, "mlp_pre_g", 0, 0, True)
            mlp(0, 0)
            post_root(1, 0)
            prep(2, "mix_pre_g", 1, 0, True)
            softplus_exp("lam", LAM)
            softplus_log("lam", LAM)
            act.sem_inc(sg("lru_i"), 1)
            act.wait_ge(sg("halo_ready"), 2)

            b_lru, t_lru = FIRST["lru"], G_FIRST["lru"]

            def gate_weights(i):
                for s in range(2):
                    act.wait_ge(sg(f"gw_landed_{s}"), i * 32 + 32)
                    act.activation(GWH[:, s, :, :], GWR[:, s, :, :], ACT.Copy).then_inc(sg("gw_hi_made"), 1)

            def lru_tap3(i, s):
                if not isinstance(i, int) or i > 0:
                    act.wait_ge(sg("lru_ix"), i * 2 + (s - 1))
                act.wait_ge(sg("g_evac"), i * 4 + s + t_lru + 3)
                act.activation(LACC[:, s, :], LRAW[:, s, 3:T + 3], ACT.Identity, scale=vec("rg_conv_w", i * 2 + s + 30),
                               bias=vec("rg_conv_b", i * 2 + s)).then_inc(sg("lconv_tap3"), 1)

            def lru_x_high(i, s):
                act.wait_ge(sg("lconv_tap2"), i * 2 + s + 1)
                act.activation(XRH[:, s, :], LACC[:, s, :], ACT.Copy).then_inc(sg("xr_hi"), 1)

            def lru_gates(i):
                for s in range(2):
                    n = i * 2 + s
                    act.wait_ge(sg("gates_mm"), n + 1)
                    act.activation(two(RG[:, s, :]), g_tile(2, T), ACT.Sigmoid, bias=vec("rg_b_a", n)
                                   ).then_inc(sg("lru_r"), 1)
                    act.activation(two(IG[:, s, :]), g_tile(3, T), ACT.Sigmoid, bias=vec("rg_b_i", n)
                                   ).then_inc(sg("lru_i"), 1)

            def lru_decays(j):
                for s in range(2):
                    n1 = j * 2 + (s + 1)
                    act.wait_ge(sg("lru_r"), n1)
                    act.activation(TH[:, s, :], RG[:, s, :], ACT.Tanh, scale=cl[:, bass.ds(j * 2 + s, 1)]
                                   ).then_inc(sg("lru_th"), 1)
                    act.activation(RG[:, s, :], RG[:, s, :], ACT.Exp, scale=cl[:, bass.ds(j * 2 + s, 1)]
                                   ).then_inc(sg("lru_a"), 1)
                    act.wait_ge(sg("lru_a"), n1)
                    act.activation(A2[:, s, :], RG[:, s, :], ACT.Square).then_inc(sg("lru_a2"), 1)

            def lru_roots(j):
                for s in range(2):
                    act.wait_ge(sg("lru_q"), j * 2 + (s + 1))
                    act.activation(TH[:, s, :], TH[:, s, :], ACT.Sqrt, scale=-1.0).then_inc(sg("lru_root"), 1)

            def lru_gelu(j):
                for s in range(2):
                    act.wait_ge(sg("g_evac"), j * 4 + (s + 2 + t_lru + 3))
                    gt = GATE[:, bass.ds(j * 2 + s, 1), :]
                    act.activation(gt, gt, ACT.Gelu_apprx_tanh).then_inc(sg("gelu_ready"), 1)

            def lru_high(j):
                for s in range(2):
                    act.wait_ge(sg("lru_gated"), j * 2 + (s + 1))
                    act.activation(GHI[:, :, :].rearrange("p n t -> p (n t)")[:, bass.ds(j * (2 * T) + s * T, T)],
                                   SQT[:, s, :], ACT.Copy).then_inc(sg("lru_hi"), 1)

            def lru_turn(i, j, turns):
                split(b_lru + 1, i, turns)
                lru_decays(j)
                gate_weights(i)
                lru_tap3(i, 0)
                lru_roots(j)
                lru_x_high(i, 0)
                lru_tap3(i, 1)
                lru_gelu(j)
                lru_x_high(i, 1)
                split(b_lru + 2, i, turns)
                lru_high(j)
                lru_gates(i)

            gate_weights(0)
            lru_tap3(0, 0)
            lru_x_high(0, 0)
            lru_tap3(0, 1)
            lru_x_high(0, 1)
            split(b_lru + 2)
            lru_gates(0)
            with act.Fori(1, LT // 2 - 1) as i:
                lru_turn(i, i - 1, LT // 2 - 1)
            lru_turn(LT // 2 - 1, LT // 2 - 2, 1)
            j = LT // 2 - 1
            split(b_lru + 1, LT // 2)
            lru_decays(j)
            lru_roots(j)
            lru_gelu(j)
            lru_high(j)
            outputs(FIRST["rgo"], G_FIRST["rgo"], 16, META, two_blocks=False)
            post_root(2, META)
            prep(3, "mlp_pre_g", 1, META, True)
            mlp(1, META)
            post_root(3, META)
            for c in range(4):
                act.wait_ge(sg("out_turned"), 2 * c + 1)
                act.copy(OUTN[:, c, 0:512], PS[:, 4 + 2 * c % 4, :]).then_inc(sg("out_rows_act"), 1)

        @block.tensor
        def _(pe):
            pe.sem_inc(sg("w_used"), 2)

            pe.wait_ge(sg("first_consts_landed"), 16 * FIRST_SMALL)
            for tau in range(5):
                t0, L = CHUNKS[tau]
                if tau:
                    pe.wait_ge(sg(f"x_landed_{tau - 1}"), 16)
                for j in range(2):
                    if tau >= 2:
                        pe.wait_ge(sg("x_in_dve" if j else "x_in_act"), tau - 1)
                    for k in range(4):
                        cols = slice(P * (4 * j + k), P * (4 * j + k + 1))
                        src = XN[:, tau - 1, cols] if tau else MN[:, cols]
                        mm = pe.transpose(PS[:, 4 + (2 * tau + j) % 4, P * k:P * k + L], src, ident[0:L, 0:L])
                    mm.then_inc(sg("x_turned"), 1)
            pe.transpose(PS[:, 0, 0:ROWS_A], PKA[:, :], ident[0:ROWS_A, 0:ROWS_A]).then_inc(sg("vecs_turned"), 1)
            pe.wait_ge(sg("ones_ready"), 2)

            def sum_squares(name, n, c0=0):
                w = (T - c0) // 2
                t, _ = BEFORE[name]
                for k in range(n):
                    pe.wait_ge(step(name, "sq"), t + k + 1)
                    for h in range(2):
                        mm = pe.matmul(PS[:, 4 + h, 0:w], ones[:, :], SQT[:, k % 2, c0 + h * w:c0 + (h + 1) * w],
                                       start=(k == 0), stop=(k == n - 1))
                    mm.then_inc(step(name, "ss"), 1)

            def product(q, ks, weight, x, c0=0, first=True, last=True):
                w = (T - c0) // 2
                for k in ks:
                    (whi, wlo), (xhi, xlo) = weight(k), x(k)
                    for p, (a, b) in enumerate(((whi, xhi), (whi, xlo), (wlo, xhi))):
                        for h in range(2):
                            mm = pe.matmul(PS[:, 2 * q + h, 0:w], a, b[:, c0 + h * w:c0 + (h + 1) * w],
                                           start=(first and k == ks[0] and p == 0),
                                           stop=(last and k == ks[-1] and p == 2))
                return mm

            def take(b, i=0):
                pe.wait_ge(sg("w_hi_made"), i * 2 + b + 1)
                pe.wait_ge(sg("w_lo_made"), i * 2 + b + 1)

            def weights(s, m, width=256, ks=KT, base=0):
                def get(k):
                    c = base + k % ks * width + m * P
                    return WHI[:, s, c:c + P], WLO[:, s, c:c + P]
                return get

            def stream_of(hi, lo, base=0):
                return lambda k: (hi[:, base + k, :], lo[:, base + k, :])

            normed = stream_of(AHI, ALO)

            def two_tiles(b, t, i=0, c0=0, per=4, between=None):
                take(b, i)
                pe.wait_ge(sg("g_evac"), i * per + t + 1)
                product(0, range(KT), weights(b % 2, 0), normed, c0).then_inc(sg("tile_done"), 1)
                if between:
                    between()
                pe.wait_ge(sg("g_evac"), i * per + t + 2)
                product(1, range(KT), weights(b % 2, 1), normed, c0).then_inc(sg("w_used"), 1)

            def first_block(name, b, t, c0=0):
                w = (T - c0) // 2
                before, _ = BEFORE[name]
                take(b)
                pe.wait_ge(sg("g_evac"), t + 2)
                if before:
                    pe.wait_ge(sg("fuse_root"), BEFORE[name][1])
                for n in range(KT + SQUARES_AHEAD):
                    k = n
                    if k < KT:
                        pe.wait_ge(step(name, "sq"), before + k + 1)
                        for h in range(2):
                            mm = pe.matmul(PS[:, 4 + h, 0:w], ones[:, :], SQT[:, k % 2, c0 + h * w:c0 + (h + 1) * w],
                                           start=(k == 0), stop=(k == KT - 1))
                        mm.then_inc(step(name, "ss"), 1)
                    k = n - SQUARES_AHEAD
                    if k >= 0:
                        pe.wait_ge(step(name, "lo"), before + k + 1)
                        for q in range(2):
                            mm = product(q, [k], weights(b % 2, q), normed, c0, first=(k == 0), last=(k == KT - 1))
                            if k == KT - 1:
                                mm.then_inc(sg("w_used" if q else "tile_done"), 1)

            first_block("prep0", 0, 0)
            pe.wait_ge(sg("consts_landed"), 16 * CONSTS)
            pe.wait_ge(sg("x_in_dve"), 5)
            pe.transpose(PS[:, 7, 0:ROWS_B], PKB[:, :], ident[0:ROWS_B, 0:ROWS_B]).then_inc(sg("vecs_turned"), 1)
            two_tiles(1, 2)
            two_tiles(2, 4)
            b, t = FIRST["win"], G_FIRST["win"]
            two_tiles(b, t)

            def sum_latents():
                pe.wait_ge(step("prep0", "root"), 1)
                for j, sq in enumerate(LATENT_SQUARES):
                    pe.wait_ge(step("qn", "sq"), j + 1)
                    for h in range(2):
                        mm = pe.matmul(PS[:, (4 if j < 3 else 6) + h, 0:HALF], ones[:, :], sq[:, h * HALF:(h + 1) * HALF],
                                       start=(j in (0, 3)), stop=(j in (2, 4)))
                    mm.then_inc(step("qn", "ss"), 1)

            two_tiles(b + 1, t + 2, between=sum_latents)
            two_tiles(b + 2, t + 4)
            two_tiles(b + 3, t + 6)
            with pe.Fori(2, 5) as i:
                for s in range(2):
                    two_tiles(b + s, t + 2 * s, i)

            pe.wait_ge(sg("dt_step"), DT_STEPS)
            pe.wait_ge(step("kvn", "root"), 2)
            for tau in range(5):
                t0, L = CHUNKS[tau]
                mm = pe.transpose(PS[0:L, 7, HEADS * tau:HEADS * (tau + 1)], DTC[:, 0, t0:t0 + L],
                                  ident[0:HEADS, 0:HEADS])
            mm.then_inc(sg("dt_turned"), 1)

            def decay_sums(c, it, v_before):
                _, L, v = chunk(c, it)
                pe.wait_ge(sg("ssd_da_staged"), v)
                if c > 0:
                    pe.wait_ge(sg("ssd_e_arg"), v_before)
                for h in range(HEADS):
                    mm = pe.matmul(PS[:, h // 4, P * (h % 4):P * (h % 4) + L],
                                   DAC[0:L, h:h + 1].to_broadcast([L, P]), triu[0:L, 0:L], start=True, stop=True)
                mm.then_inc(sg("ssd_r_mm"), 1)

            def ssd(c, it=None, ahead=True):
                _, L, v = chunk(c, it)
                pe.wait_ge(sg("ssd_staged"), v)
                if c > 0:
                    pe.wait_ge(sg("ssd_y_out"), v - 1)
                    pe.wait_ge(sg("ssd_bt"), v - 1)
                pe.matmul(PS[0:L, 6, 0:HEADS], triu[0:L, 0:L], DAC[0:L, :], start=True, stop=True)
                for g in range(2):
                    mm = pe.matmul(PS[0:L, 6, P + P * g:P + P * g + L], XS[:, 8 + g, 0:L], XS[:, 10 + g, 0:L],
                                   start=True, stop=True)
                mm.then_inc(sg("ssd_cb_mm"), 1)
                for g in range(2):
                    mm = pe.transpose(PS[0:L, 7, P * g:P * (g + 1)], XS[:, 8 + g, 0:L], ident[:, :])
                mm.then_inc(sg("ssd_bt_mm"), 1)
                if c > 0:
                    pe.wait_ge(sg("ssd_state"), v - 1)
                for j in range(KT):
                    mm = pe.transpose(PS[0:L, 4 + j // 4, P * (j % 4):P * (j % 4 + 1)], XS[:, j, 0:L], ident[:, :])
                mm.then_inc(sg("ssd_x_turned"), 1)
                if ahead:
                    decay_sums(1, 0 if c == 0 else it + 1, v)

                for name in ("ssd_c_decayed", "ssd_bt", "ssd_cb", "ssd_xdt"):
                    pe.wait_ge(sg(name), v)
                for h in range(HEADS):
                    if h % 8 == 0:
                        pe.wait_ge(sg(f"ssd_mt_{h // 8}"), v)
                    j = h // 2
                    o = PS[64 * (h % 2):64 * (h % 2 + 1), 6 + j // 4, P * (j % 4):P * (j % 4) + L]
                    if c > 0:
                        pe.matmul(o, HST[:, h, :], ER[:, h, 0:L], start=True, stop=False)
                    mm = pe.matmul(o, XDT[0:L, h, :], MT[0:L, h, 0:L], start=(c == 0), stop=True)
                mm.then_inc(sg("ssd_y_mm"), 1)
                pe.wait_ge(sg("ssd_xde"), v)
                for g in range(2):
                    mm = pe.matmul(PS[:, 4 + g, :], BT[0:L, g, :], XDE[0:L, 8 * g:8 * g + 8, :],
                                   start=True, stop=True)
                mm.then_inc(sg("ssd_s_mm"), 1)

            decay_sums(0, None, 0)
            ssd(0)
            with pe.Fori(0, 3) as it:
                ssd(1, it)
            ssd(1, 3, ahead=False)
            pe.wait_ge(sg("ssd_state"), 5)
            pe.wait_ge(sg("ssd_y_out"), 5)

            latent = stream_of(LHI, LLO)
            latent_kv = stream_of(LHI, LLO, 3)
            pe.wait_ge(step("kvn", "lo"), 5)

            def scores(i, s, n):
                t0, L, w = unit(n)
                u = i * 20 + (10 * s + n)
                if n % 5 == 0:
                    pe.wait_ge(sg("q_ready"), i * 4 + 2 * s + n // 5 + 1)
                if n == 0:
                    pe.wait_ge(sg("k_ready"), i * 2 + s + 1)
                if ago(i, s, n, 2):
                    pe.wait_ge(sg("pt_ready"), u - 1)
                o = PS[0:L, 2 * (n % 2):2 * (n % 2) + 2, :].rearrange("p b t -> p (b t)")
                q = QB[:, s, n // 5, t0:t0 + L]
                for a in range(0, w, 512):
                    e = min(w, a + 512)
                    pe.matmul(o[:, a:e], q, KB[:, s, n // 5, a:e], start=True, stop=(e <= w - L))
                d = w - L
                for a, e in ((d, 512), (512, w)) if d < 512 < w else ((d, w),):
                    one, mask = (ident_r, neg_r) if L == P else (ident, neg)
                    mm = pe.matmul(o[:, a:e], one[0:L, 0:L], mask[0:L, a - d:e - d], start=False, stop=True)
                mm.then_inc(sg("s_mm"), 1)

            def turn(before):
                s, n, u = before
                _, L, _ = unit(n)
                b = 2 * (n % 2)
                pe.wait_ge(sg("p_ready"), u + 1)
                m = META if n % 5 else P
                mm = pe.matmul(PS[0:m, b + 1, 256:256 + L], PR[0:L, n % 2, 0:m], ident[0:L, 0:L], start=True, stop=True)
                for j in range(n % 5):
                    mm = pe.transpose(PS[:, b, P * j:P * j + L], PR[0:L, n % 2, META + P * j:META + P * (j + 1)],
                                      ident[0:L, 0:L])
                mm.then_inc(sg("pt_mm"), 1)

            def values(before, i, s):
                sv, n, u = before
                _, L, _ = unit(n)
                c, h = n % 5, n // 5
                pe.wait_ge(sg("pt_ready"), u + 1)
                if n == 0:
                    pe.wait_ge(sg("v_ready"), i * 2 + s + 1)
                if c == 0:
                    pe.wait_ge(sg("v_ready"), i * 2 + s + 1)
                    if h == 1 and not last_pair(i, s):
                        pe.wait_ge(sg("q_ready"), i * 4 + 2 * s + 4)
                pairs_out = i * 2 + (s - 1)
                if n == 1 and not (isinstance(i, int) and pairs_out <= 0):
                    pe.wait_ge(sg("att_lo"), pairs_out)
                rows_h = slice(VD * h, VD * (h + 1))
                o = PS[rows_h, 4 + sv, P * (c - 1):P * c] if c else PS[rows_h, 7, META_OUT]
                for j in range(c + 1):
                    rows = P if j else META
                    mm = pe.matmul(o, VH[0:rows, sv, j, h, :], PTS[0:rows, n % 2, j, 0:L], start=(j == 0), stop=(j == c))
                mm.then_inc(sg("o_mm"), 1)

            def last_pair(i, s):
                return isinstance(i, int) and i * 2 + s == 7

            def query(i, s, h, ks):
                if h == 0 and ks[0] == 0:
                    take(FIRST["att"] + s, i)
                    if not isinstance(i, int) or i + s > 0:
                        pe.wait_ge(sg("v_ready"), i * 2 + s)
                elif ks[0] == 0:
                    pe.wait_ge(sg("q_ready"), i * 4 + (2 * s + 1))
                mm = product(3, ks, weights((FIRST["att"] + s) % 2, h), latent, first=(ks[0] == 0), last=(ks[-1] == 2))
                if ks[-1] == 2:
                    mm.then_inc(sg("tile_done"), 1)

            def key(i, s, ks):
                if ks[0] == 0:
                    pe.wait_ge(sg("q_ready"), i * 4 + (2 * s + 2))
                mm = product(3, ks, weights((FIRST["att"] + s) % 2, 0, width=P, base=768), latent_kv,
                             first=(ks[0] == 0), last=(ks[-1] == 1))
                if ks[-1] == 1:
                    mm.then_inc(sg("tile_done"), 1)

            def value(i, s, js):
                if js[0] == 1:
                    pe.wait_ge(sg("k_ready"), i * 2 + s + 1)
                for j in js:
                    if j == 0 and (not isinstance(i, int) or i + s > 0):
                        pe.wait_ge(sg("meta_lo"), i * 2 + s)
                    t0 = CHUNKS[j][0]
                    o = PS[:, 6, P * (j - 1):P * j] if j else PS[:, 7, 0:P]
                    for k in range(2):
                        (whi, wlo), (xhi, xlo) = weights((FIRST["att"] + s) % 2, 0, width=P, base=1024)(k), latent_kv(k)
                        for p, (a, x) in enumerate(((whi, xhi), (whi, xlo), (wlo, xhi))):
                            mm = pe.matmul(o, x[:, t0:t0 + P], a, start=(k == 0 and p == 0), stop=(k == 1 and p == 2))
                if js[-1] == 0:
                    mm.then_inc(sg("w_used"), 1)

            def attend(i):
                for s in range(2):
                    i2, s2 = (i, 1) if s == 0 else (i + 1, 0)
                    for n in range(10):
                        scores(i, s, n)
                        if ago(i, s, n, 1):
                            turn(ago(i, s, n, 1))
                        if ago(i, s, n, 2):
                            values(ago(i, s, n, 2), i, s)
                        if last_pair(i, s):
                            continue
                        if n in Q_TERMS:
                            query(i2, s2, *Q_TERMS[n])
                        if n in K_TERMS:
                            key(i2, s2, K_TERMS[n])
                        if n in V_BLOCKS:
                            value(i2, s2, V_BLOCKS[n])

            query(0, 0, 0, [0, 1, 2])
            query(0, 0, 1, [0, 1, 2])
            key(0, 0, [0, 1])
            value(0, 0, [1, 2, 3, 4, 0])
            sum_squares("yn", KT)
            pe.wait_ge(step("yn", "root"), 3)
            pe.wait_ge(sg("k_rope_placed"), 8)
            pe.wait_ge(sg("mask_r"), 2)
            pe.wait_ge(sg("probs_zero"), 1)
            attend(0)
            with pe.Fori(1, 3) as i:
                attend(i)
            attend(3)
            turn(ago(4, 0, 0, 1))
            values(ago(4, 0, 0, 2), 4, 0)
            values(ago(4, 0, 1, 2), 4, 0)
            pe.wait_ge(sg("pt_ready"), 80)

            pe.wait_ge(step("yn", "lo"), 5 + KT)

            def down(b, t, c0, i, ready=None):
                for s in range(2):
                    take(b + s, i)
                    if s == 1 and ready:
                        ready()
                    x = stream_of(UHI, ULO, KT * s)
                    for q in range(2):
                        if s == 0:
                            pe.wait_ge(sg("g_evac"), i * 2 + t + q + 1)
                        mm = product(q, range(KT), weights((b + s) % 2, q), x, c0, first=(s == 0), last=(s == 1))
                        if q == 1:
                            mm.then_inc(sg("w_used"), 1)
                        elif s == 1:
                            mm.then_inc(sg("tile_done"), 1)

            def post_sum(u, c0):
                pe.wait_ge(sg("m_summed"), 8 * (u + 1) + 2)
                for c, t0, L in chunks_from(c0):
                    mm = pe.matmul(PS[0:L, 4, c:c + 1], SQA[:, t0:t0 + L], ones[:, 0:1], start=True, stop=True)
                mm.then_inc(sg("fuse_ss"), 1)
                pe.wait_ge(sg("fuse_recip"), u + 1)
                for c, t0, L in chunks_from(c0):
                    mm = pe.matmul(post_rstd(0)[:, t0:t0 + L], RT[0:L, c:c + 1].to_broadcast([L, P]), ident[0:L, 0:L],
                                   start=True, stop=True)
                mm.then_inc(sg("fuse_spread"), 1)

            def mlp(layer, c0):
                b0, t0 = FIRST[f"mlp{layer}"], G_FIRST[f"mlp{layer}"]
                for f in range(2):
                    if f == 0:
                        first_block(f"prep{2 * layer + 1}", b0, t0, c0)
                        two_tiles(b0 + 1, t0 + 2, c0=c0)
                    with pe.Fori(1 if f == 0 else 0, 4) as i:
                        for s in range(2):
                            two_tiles(b0 + 16 * f + s, t0 + 24 * f + 2 * s, i, c0)
                    pe.wait_ge(sg("up_lo"), 32 * layer + 16 * f + 8)
                    down(b0 + 16 * f + 8, t0 + 24 * f + 16, c0, 0,
                         lambda: pe.wait_ge(sg("up_lo"), 32 * layer + 16 * (f + 1)))
                    with pe.Fori(1, 4) as i:
                        down(b0 + 16 * f + 8, t0 + 24 * f + 16, c0, i)

            down(FIRST["wout"], G_FIRST["wout"], 0, 0, lambda: (pe.wait_ge(sg("att_lo"), 8), pe.wait_ge(sg("meta_lo"), 8)))
            with pe.Fori(1, 4) as i:
                down(FIRST["wout"], G_FIRST["wout"], 0, i)
            post_sum(0, 0)
            mlp(0, 0)
            post_sum(1, 0)

            b0, t0 = FIRST["lru"], G_FIRST["lru"]
            def lru_turn(i):
                if isinstance(i, int):
                    first_block("prep2", b0, t0)
                    pe.wait_ge(step("prep2", "root"), 3)
                else:
                    two_tiles(b0, t0, i)
                take(b0 + 1, i)
                for s in range(2):
                    pe.wait_ge(sg("g_evac"), i * 4 + t0 + 2 + s + 1)
                    mm = product(s, range(KT), weights((b0 + 1) % 2, s), normed)
                    mm.then_inc(sg("w_used" if s else "tile_done"), 1)
                    n = i * 2 + s
                    pe.wait_ge(sg("xr_hi"), n + 1)
                    pe.wait_ge(sg("xr_lo"), n + 1)
                    pe.wait_ge(sg("gw_hi_made"), n + 1)
                    pe.wait_ge(sg("gw_lo_made"), n + 1)
                    pe.wait_ge(sg("lru_i"), n + 1)
                    for g in range(2):
                        mm = product(2 + g, [0], lambda k: (GWH[:, s, g, :], GWL[:, s, g, :]),
                                     lambda k: (XRH[:, s, :], XRL[:, s, :]))
                    mm.then_inc(sg("gates_mm"), 1)

            lru_turn(0)
            with pe.Fori(1, LT // 2) as i:
                lru_turn(i)

            b, t, gated = FIRST["rgo"], G_FIRST["rgo"], stream_of(GHI, GLO)
            pe.wait_ge(sg("lru_lo"), LT - 2)
            for ks in (range(LT - 2), range(LT - 2, LT)):
                for s in range(2):
                    if ks[0] == 0:
                        take(b + s)
                        pe.wait_ge(sg("g_evac"), t + s + 1)
                    else:
                        pe.wait_ge(sg("lru_lo"), LT)
                    mm = product(s, ks, weights((b + s) % 2, 0, width=P, ks=LT), gated, META,
                                 first=(ks[0] == 0), last=(ks[0] > 0))
                    if ks[0] > 0:
                        mm.then_inc(sg("w_used"), 1)
            with pe.Fori(1, 4) as i:
                for s in range(2):
                    take(b + s, i)
                    pe.wait_ge(sg("g_evac"), i * 2 + t + s + 1)
                    product(s, range(LT), weights((b + s) % 2, 0, width=P, ks=LT), gated, META
                            ).then_inc(sg("w_used"), 1)
            post_sum(2, META)
            mlp(1, META)
            post_sum(3, META)
            pe.wait_ge(sg("fuse_root"), 4)

            for c in range(4):
                for j in range(2):
                    if c == 0:
                        pe.wait_ge(sg("fuse_h"), 3 * KT + 2 * j + 2)
                        pe.wait_ge(sg("last_h"), 2 * j + 2)
                    if c >= 2:
                        pe.wait_ge(sg("out_rows_dve" if j else "out_rows_act"), c - 1)
                    for k in range(4):
                        mm = pe.transpose(PS[:, 4 + (2 * c + j) % 4, P * k:P * (k + 1)],
                                          H[:, 4 * j + k, META + P * c:META + P * (c + 1)], ident[:, :])
                    mm.then_inc(sg("out_turned"), 1)

        @block.vector
        def _(dve):
            dve.sem_inc(sg("g_evac"), 2)

            def split(b, i=0, turns=1):
                at_b = placed(b, i, turns)
                if at_b:
                    s, n, _, free_at = at_b
                    dve.wait_ge(sg("w_hi_made"), free_at)
                    dve.tensor_tensor(WLO[:, s, 0:n], RAW[:, s, 0:n], WHI[:, s, 0:n].bitcast(F32), ALU.subtract
                                      ).then_inc(sg("w_lo_made"), 1)

            for tau in range(5):
                t0, L = CHUNKS[tau]
                dve.wait_ge(sg("x_turned"), 2 * tau + 2)
                dve.tensor_copy(H[:, 4:8, t0:t0 + L],
                                PS[:, 4 + (2 * tau + 1) % 4, :].rearrange("p (k t) -> p k t", k=4)[:, :, 0:L]
                                ).then_inc(sg("x_in_dve"), 1)
            dve.wait_ge(sg("vecs_turned"), 1)
            dve.tensor_copy(VA[:, :], PS[:, 0, 0:ROWS_A]).then_inc(sg("vecs_ready"), 1)
            dve.wait_ge(sg("vecs_ready"), 1)
            split(0)

            def rstd(name, dst, c0=0):
                dve.wait_ge(step(name, "root"), BEFORE[name][1] + 1)
                dve.reciprocal(dst[:, c0:T], dst[:, c0:T]).then_inc(sg("rstd_made"), 1)
                rstd.made += 1
                dve.wait_ge(sg("rstd_made"), rstd.made)
            rstd.made = 0

            def low_part(u, k, name, layer, c0):
                dve.wait_ge(step(f"prep{u}", "hi"), KT * u + k + 1)
                dve.scalar_tensor_tensor(out=ALO[:, k, c0:T], in0=H[:, k, c0:T], scalar=vec(name, KT * layer + k),
                                         in1=AHI[:, k, c0:T].bitcast(F32), op0=ALU.mult, op1=ALU.subtract
                                         ).then_inc(step(f"prep{u}", "lo"), 1)

            dve.wait_ge(sg("x_in_dve"), 5)
            for k in range(KT):
                low_part(0, k, "mix_pre_g", 0, 0)
            rstd("prep0", RS)
            split(1)
            dve.wait_ge(sg("vecs_turned"), 2)
            dve.tensor_copy(VB[:, :], PS[:, 7, 0:ROWS_B]).then_inc(sg("vecs_ready"), 1)
            dve.wait_ge(sg("vecs_ready"), 2)
            for o in range(2):
                dve.tensor_copy(dskip[64 * o:64 * (o + 1), :],
                                heads_in[64 * o:64 * (o + 1), 1, :].rearrange("p (j o) -> p j o", o=2)[:, :, o]
                                ).then_inc(sg("d_skip_ready"), 1)

            def tile_out(dst, q, c0=0, rows=slice(0, P)):
                return dve.tensor_tensor(two(dst), g_tile(q, T - c0, rows), two(RS[rows, c0:T]), ALU.mult)

            def done(stage, q, block_no, i, per_i, tiles_i):
                if q == 0:
                    dve.wait_ge(sg("tile_done"), i * tiles_i + DONE[stage] + block_no + 1)
                else:
                    dve.wait_ge(sg("w_used"), i * per_i + FIRST[stage] + block_no + 3)

            def taps(x, acc, weight, m, names, n, own):
                dve.wait_ge(sg(names[3]), n)
                dve.wait_ge(sg("g_evac"), own)
                for j in range(3):
                    dve.scalar_tensor_tensor(out=acc, in0=x[:, j:T + j], scalar=vec(weight, m(j)), in1=acc,
                                             op0=ALU.mult, op1=ALU.add).then_inc(sg(names[j]), 1)
                    if j < 2:
                        dve.wait_ge(sg(names[j]), n)

            dve.wait_ge(sg("halo_ready"), 1)
            names = ["conv_tap0", "conv_tap1", "conv_tap2", "conv_tap3"]
            def norm_split(name, src, g, n, hi, lo, mean_root):
                t, _ = BEFORE[name]
                for k in range(n + 1):
                    if k < n:
                        if k >= 2:
                            dve.wait_ge(step(name, "lo"), t + k - 1)
                        dve.scalar_tensor_tensor(out=TMP[:, k % 2, :], in0=src(k), scalar=vec(g, k), in1=mean_root[:, :],
                                                 op0=ALU.mult, op1=ALU.mult).then_inc(step(name, "full"), 1)
                    if k:
                        dve.wait_ge(step(name, "hi"), t + k)
                        dve.tensor_tensor(lo(k - 1), TMP[:, (k - 1) % 2, :], hi(k - 1).bitcast(F32), ALU.subtract
                                          ).then_inc(step(name, "lo"), 1)

            def softplus_start(name, x, first):
                steps = sg(f"{name}_step")
                first().then_inc(steps, 1)
                dve.wait_ge(steps, 1)
                dve.scalar_tensor_tensor(out=x[:, 1, :], in0=x[:, 0, :], scalar=-1.0, in1=x[:, 0, :], op0=ALU.mult,
                                         op1=ALU.min).then_inc(steps, 1)

            def softplus_recip(name, x):
                steps, done_act = sg(f"{name}_step"), sg(f"{name}_act")
                x1, e = x[:, 1, :], x[:, 2, :]
                dve.wait_ge(done_act, 1)
                dve.tensor_scalar(x1, e, 1.0, None, ALU.add).then_inc(steps, 1)
                dve.wait_ge(done_act, 2)
                dve.wait_ge(steps, 3)
                dve.tensor_scalar(x1, x1, -1.0, 1e-30, ALU.add, ALU.max).then_inc(steps, 1)
                dve.wait_ge(steps, 4)
                dve.reciprocal(x1, x1).then_inc(steps, 1)

            def softplus_end(name, x):
                steps = sg(f"{name}_step")
                x0, x1, e, ln = (x[:, j, :] for j in range(4))
                dve.tensor_tensor(ln, ln, e, ALU.mult).then_inc(steps, 1)
                dve.wait_ge(steps, 6)
                dve.tensor_tensor(ln, ln, x1, ALU.mult).then_inc(steps, 1)
                dve.wait_ge(steps, 7)
                dve.tensor_scalar(x1, e, -0.5, 1.0, ALU.mult, ALU.add).then_inc(steps, 1)
                dve.wait_ge(steps, 8)
                dve.tensor_tensor(x1, x1, e, ALU.mult).then_inc(steps, 1)
                dve.wait_ge(steps, 9)
                dve.tensor_tensor(ln, ln, x1, ALU.max).then_inc(steps, 1)
                dve.wait_ge(steps, 10)
                dve.scalar_tensor_tensor(out=x0, in0=x0, scalar=0.0, in1=ln, op0=ALU.max, op1=ALU.add
                                         ).then_inc(steps, 1)
                dve.wait_ge(steps, DT_STEPS)

            outs = [C5[:, 0, :], C5[:, 1, :], C5[:, 2, :], MISC[:, :], C5[:, 3, :], C5[:, 4, :]]
            for n, stage in enumerate(("cq", "misc", "ckv")):
                for q in range(2):
                    done(stage, q, 0, 0, 0, 0)
                    tile_out(outs[2 * n + q], q).then_inc(sg("g_evac"), 1)
                split(2 + n)

            def conv_block(i, s, turns=1):
                for q in range(2):
                    m = i * 4 + 2 * s + q
                    done("win", q, s, i, 2, 2)
                    tile_out(XRAW[:, q, 3:T + 3], q).then_inc(sg("g_evac"), 1)
                    taps(XRAW[:, q, :], CACC[:, q, :], "ssd_conv_w", lambda j: m + 12 * j, names, m + 1,
                         m + G_FIRST["win"] + 3)
                split(FIRST["win"] + 2 + s, i, turns)

            conv_block(0, 0)
            rstd("qn", RLQ)
            conv_block(0, 1)
            rstd("kvn", RLK)
            with dve.Fori(1, 3) as i:
                for s in range(2):
                    conv_block(i, s, 3)
            for n in range(8):
                if n == 4:
                    softplus_start("dt", DTC, lambda: dve.tensor_scalar(DTC[:, 0, :], MISC[0:HEADS, :], dtb[:, :], None,
                                                                        ALU.add))
                if n == 5:
                    softplus_recip("dt", DTC)
                if n == 6:
                    softplus_end("dt", DTC)
                if n == 1:
                    norm_split("qn", lambda k: C5[:, k, :], "mla_q_norm_g", 3,
                               lambda k: LHI[:, k, :], lambda k: LLO[:, k, :], RLQ)
                if n == 2:
                    norm_split("kvn", lambda k: C5[:, 3 + k, :], "mla_kv_norm_g", 2,
                               lambda k: LHI[:, 3 + k, :], lambda k: LLO[:, 3 + k, :], RLK)
                if n == 3:
                    dve.wait_ge(step("kvn", "lo"), 5)
                    dve.tensor_tensor(TMP[64:128, 0, :], MISC[64:128, :], CS[64:128, :], ALU.mult
                                      ).then_inc(sg("k_rope_terms"), 1)
                    dve.wait_ge(sg("k_rope_moved"), 1)
                    dve.tensor_tensor(KRS[64:96, :], TMP[64:96, 0, :], TMP[64:96, 1, :], ALU.add
                                      ).then_inc(sg("k_rope"), 1)
                done("win", n % 2, 6 + n // 2, 0, 0, 0)
                tile_out(Z[:, n, :], n % 2).then_inc(sg("g_evac"), 1)
                if n % 2:
                    split(FIRST["win"] + 8 + n // 2)
            dve.wait_ge(sg("dt_turned"), 1)
            dve.wait_ge(sg("exp_a"), 1)
            turned = PS[:, 7, 0:5 * HEADS].rearrange("p (c h) -> p c h", c=5)
            dve.tensor_copy(DTT[0:META, 0, :], turned[0:META, 0, :]).then_inc(sg("dt_rows"), 1)
            dve.tensor_copy(DTT[:, 1:5, :], turned[:, 1:5, :]).then_inc(sg("dt_rows"), 1)
            dve.wait_ge(sg("dt_rows"), 2)
            dve.scalar_tensor_tensor(out=DA[0:META, 0, :], in0=DTT[0:META, 0, :], scalar=-1.0, in1=expA[0:META, :],
                                     op0=ALU.mult, op1=ALU.mult).then_inc(sg("da_rows"), 1)
            dve.scalar_tensor_tensor(out=DA[:, 1:5, :], in0=DTT[:, 1:5, :], scalar=-1.0,
                                     in1=expA[:, :].unsqueeze(1).to_broadcast([P, 4, HEADS]),
                                     op0=ALU.mult, op1=ALU.mult).then_inc(sg("da_rows"), 1)
            dve.wait_ge(sg("da_rows"), 2)

            def heads_of(b):
                return b.rearrange("p b (h d) -> p b h d", h=8)

            def stage_decay(c, tau):
                rows = slice(0, META if c == 0 else P)
                dve.tensor_copy(DAC[rows, :].unsqueeze(1), DA[rows, tau, :]).then_inc(sg("ssd_da_staged"), 1)

            def ssd(c, it=None, ahead=True):
                t0, L, v = chunk(c, it)
                tau = slice(0, 1) if c == 0 else bass.ds(it + 1, 1)
                rows = slice(0, L)
                dve.wait_ge(sg("ssd_cb_mm"), v)
                dve.tensor_copy(ACS[rows, :], PS[rows, 6, 0:HEADS]).then_inc(sg("ssd_acs"), 1)
                dve.tensor_tensor(CBM[rows, :, 0:L],
                                  PS[rows, 6, P:3 * P].rearrange("p (g l) -> p g l", g=2)[:, :, 0:L],
                                  triu[rows, 0:L].unsqueeze(1).to_broadcast([L, 2, L]), ALU.mult).then_inc(sg("ssd_cb"), 1)
                dve.wait_ge(sg("ssd_r_mm"), v)
                if ahead:
                    stage_decay(1, bass.ds(1 if c == 0 else it + 2, 1))
                dve.wait_ge(sg("ssd_er"), v)
                dve.wait_ge(sg("ssd_acs"), v)
                acs4 = ACS[rows, :].rearrange("p (b h) -> p b h", b=4)
                r4 = PS[rows, 0:4, :].rearrange("p b (h l) -> p b h l", h=4)
                dve.tensor_tensor(DTE[rows, :].rearrange("p (b h) -> p b h", b=4), r4[:, :, :, L - 1], acs4,
                                  ALU.subtract).then_inc(sg("ssd_to_end_arg"), 1)
                e4 = E[rows, :, 0:L].rearrange("p (b h) l -> p b h l", b=4)
                dve.tensor_tensor(e4, r4[:, :, :, 0:L], acs4.unsqueeze(3).to_broadcast([L, 4, 4, L]), ALU.subtract
                                  ).then_inc(sg("ssd_e_arg"), 1)
                dve.wait_ge(sg("ssd_e_arg"), v)
                dve.tensor_scalar(E[rows, :, 0:L], E[rows, :, 0:L], 0.0, None, ALU.min).then_inc(sg("ssd_e_min"), 1)
                dve.tensor_copy(CD[:, :], ER[:, :, L - 1]).then_inc(sg("ssd_cd"), 1)
                dve.wait_ge(sg("ssd_cd"), v)
                er = ER[:, :, 0:L].rearrange("p (g h) l -> p g h l", g=2)
                dve.tensor_tensor(er, er, XS[:, 10:12, 0:L].unsqueeze(2).to_broadcast([P, 2, 8, L]), ALU.mult
                                  ).then_inc(sg("ssd_c_decayed"), 1)
                dve.wait_ge(sg("ssd_x_turned"), v)
                dtt = DTT[rows, tau, :].rearrange("p o (b h) -> p (o b) h", b=2)
                dve.tensor_tensor(XDT[rows, :, :].rearrange("p (b h) d -> p b h d", b=2), heads_of(PS[rows, 4:6, :]),
                                  dtt.unsqueeze(3).to_broadcast([L, 2, 8, VD]), ALU.mult).then_inc(sg("ssd_xdt"), 1)
                dve.wait_ge(sg("ssd_e"), v)
                dve.wait_ge(sg("ssd_cb"), v)
                for g in range(2):
                    dve.tensor_tensor(MT[rows, 8 * g:8 * g + 8, 0:L], E[rows, 8 * g:8 * g + 8, 0:L],
                                      CBM[rows, g:g + 1, 0:L].to_broadcast([L, 8, L]), ALU.mult
                                      ).then_inc(sg(f"ssd_mt_{g}"), 1)
                dve.wait_ge(sg("ssd_to_end"), v)
                dve.wait_ge(sg("ssd_xdt"), v)
                dve.tensor_tensor(XDE[rows, :, :], XDT[rows, :, :], DTE[rows, :].unsqueeze(2).to_broadcast([L, HEADS, VD]),
                                  ALU.mult).then_inc(sg("ssd_xde"), 1)
                dve.wait_ge(sg("ssd_y_mm"), v)
                dve.wait_ge(sg("ssd_skip"), v)
                yt = YT[:, :, 0:L].rearrange("p (b j) l -> p b j l", b=2)
                dve.tensor_tensor(yt, PS[:, 6:8, :].rearrange("p b (j l) -> p b j l", j=4)[:, :, :, 0:L], yt, ALU.add
                                  ).then_inc(sg("ssd_y_out"), 1)
                dve.wait_ge(sg("ssd_s_mm"), v)
                hst = HST[:, :, :].rearrange("p (b h) d -> p b h d", b=2)
                if c == 0:
                    dve.tensor_copy(hst, heads_of(PS[:, 4:6, :])).then_inc(sg("ssd_state"), 1)
                else:
                    dve.wait_ge(sg("ssd_state_decayed"), v - 1)
                    dve.tensor_tensor(hst, heads_of(PS[:, 4:6, :]), hst, ALU.add).then_inc(sg("ssd_state"), 1)

            stage_decay(0, slice(0, 1))
            ssd(0)
            with dve.Fori(0, 3) as it:
                ssd(1, it)
            ssd(1, 3, ahead=False)


            def queries_out(i, s, h):
                dve.wait_ge(sg("tile_done"), i * 6 + (3 * s + DONE["att"] + h + 1))
                dve.scalar_tensor_tensor(out=two(QB[:, s, h, :]), in0=g_tile(3, T), scalar=SCALE, in1=two(CS[:, :]),
                                         op0=ALU.mult, op1=ALU.mult).then_inc(sg("q_ready"), 1)

            def turn_out(before):
                _, n, u = before
                _, L, _ = unit(n)
                b = 2 * (n % 2)
                dve.wait_ge(sg("pt_mm"), u + 1)
                if n % 5:
                    dve.tensor_copy(PTS[:, n % 2, 1:n % 5 + 1, 0:L],
                             PS[:, b, :].rearrange("p (j l) -> p j l", j=4)[:, 0:n % 5, 0:L]).then_inc(sg("pt_part"), 1)
                dve.tensor_copy(PTS[0:META, n % 2, 0, 0:L], PS[0:META, b + 1, 256:256 + L]).then_inc(sg("pt_ready"), 1)

            def normalise(i, s, n):
                _, L, w = unit(n)
                u = i * 20 + (10 * s + n)
                dve.wait_ge(sg("exp_ready"), u + 1)
                dve.reciprocal(SUM[0:L, n % 2, :], SUM[0:L, n % 2, :]).then_inc(sg("sum_recip"), 1)
                dve.wait_ge(sg("sum_recip"), u + 1)
                dve.tensor_scalar(PR[0:L, n % 2, 0:w], PR[0:L, n % 2, 0:w], SUM[0:L, n % 2, :], None, ALU.mult
                                  ).then_inc(sg("p_ready"), 1)

            def y_full(i, s):
                if not (isinstance(i, int) and i == 0):
                    dve.wait_ge(step("yn", "lo"), i * 2 + (s + 4))
                dve.scalar_tensor_tensor(out=TMP[:, s:s + 1, :], in0=Z[:, bass.ds(i * 2 + s, 1), :],
                                         scalar=vec("ssd_norm_g", i * 2 + s), in1=RS[:, :].unsqueeze(1),
                                         op0=ALU.mult, op1=ALU.mult).then_inc(step("yn", "full"), 1)

            def y_low(i, s):
                dve.wait_ge(step("yn", "hi"), i * 2 + (s + 6))
                at_tile = bass.ds(i * 2 + s, 1)
                dve.tensor_tensor(ULO[:, at_tile, :], TMP[:, s:s + 1, :], UHI[:, at_tile, :].bitcast(F32), ALU.subtract
                                  ).then_inc(step("yn", "lo"), 1)

            def att_low(i, s):
                dve.wait_ge(sg("att_hi"), i * 2 + (s + 1))
                at_pair = bass.ds(i * 2 + (s + KT), 1)
                dve.tensor_tensor(ULO[:, at_pair, META:T], PS[:, 4 + s:5 + s, :], UHI[:, at_pair, META:T].bitcast(F32),
                                  ALU.subtract).then_inc(sg("att_lo"), 1)

            def meta_low(i, s):
                dve.wait_ge(sg("meta_hi"), i * 2 + (s + 1))
                at_pair = bass.ds(i * 2 + (s + KT), 1)
                dve.tensor_tensor(ULO[:, at_pair, 0:META], PS[:, 7:8, META_OUT], UHI[:, at_pair, 0:META].bitcast(F32),
                                  ALU.subtract).then_inc(sg("meta_lo"), 1)

            def attend(i, turns):
                for s in range(2):
                    last = isinstance(i, int) and i * 2 + s == 7
                    first = isinstance(i, int) and i * 2 + s == 0
                    i2, s2 = (i + 1, 0) if s else (i, 1)
                    for n in range(10):
                        _, L, w = unit(n)
                        dve.wait_ge(sg("s_mm"), i * 20 + (10 * s + n + 1))
                        dve.tensor_reduce(MX[0:L, n % 2, :], PS[0:L, 2 * (n % 2):2 * (n % 2) + 2, :].rearrange(
                            "p b t -> p (b t)")[:, 0:w], AX.X, ALU.max, negate=True).then_inc(sg("neg_max"), 1)
                        if ago(i, s, n, 1):
                            turn_out(ago(i, s, n, 1))
                        if n == 3 and not first:
                            att_low(*((i, 0) if s else (i - 1, 1)))
                        normalise(i, s, n)
                        if n == Y_FULL:
                            if first:
                                rstd("yn", RS)
                            y_full(i, s)
                        if n == Y_LOW:
                            y_low(i, s)
                        if n == 4:
                            split(FIRST["att"] + s + 2, i, turns)
                        if n == 8:
                            meta_low(i, s)
                        if last:
                            continue
                        if n in Q_STEPS:
                            queries_out(i2, s2, Q_STEPS.index(n))

            queries_out(0, 0, 0)
            queries_out(0, 0, 1)
            dve.wait_ge(sg("probs_zero"), 1)
            attend(0, 1)
            with dve.Fori(1, 3) as i:
                attend(i, 3)
            attend(3, 1)
            turn_out(ago(4, 0, 0, 1))
            att_low(3, 1)

            def out_tile(m, q, c0, add):
                dst, src = two(M[:, bass.ds(m, 1), c0:T]), g_tile(q, T - c0)
                if add:
                    return dve.tensor_tensor(dst, src, dst, ALU.add)
                return dve.tensor_copy(dst, src)

            def outputs(stage, b, td, c0, add=False, final=True):
                def turn(i, turns=1):
                    split(b + 2, i, turns)
                    dve.wait_ge(sg("tile_done"), i + DONE[stage] + td + 1)
                    out_tile(i * 2, 0, c0, add).then_inc(sg("g_evac"), 1)
                    dve.wait_ge(sg("w_used"), i * 2 + b + 2 + 2)
                    out_tile(i * 2 + 1, 1, c0, add).then_inc(sg("g_evac"), 1)
                    if not isinstance(i, int):
                        split(b + 3, i, turns)
                n = 3 if final else 4
                with dve.Fori(0, n) as i:
                    turn(i, n)
                if final:
                    turn(3)

            def fuse(u, post, pre, layer, pre_layer, t_end, c0):
                dve.wait_ge(sg("fuse_root"), u + 1)
                if c0 == 0:
                    dve.reciprocal(RT[0:META, 0:1], RT[0:META, 0:1]).then_inc(sg("fuse_recip_meta"), 1)
                dve.reciprocal(RT[:, 1:5], RT[:, 1:5]).then_inc(sg("fuse_recip"), 1)
                if u < 3:
                    split(FIRST[("mlp0", "lru", "mlp1")[u]] + 1)
                dve.wait_ge(sg("fuse_spread"), u + 1)
                dve.wait_ge(sg("g_evac"), t_end + 2)
                for k in range(KT + 1):
                    if k < KT:
                        if k >= 2 and u < 3:
                            dve.wait_ge(sg("fuse_h"), KT * u + k - 1)
                        elif k >= 2 and k % 2 == 0:
                            dve.wait_ge(sg("fuse_h"), KT * u + k // 2)
                        elif k >= 2:
                            dve.wait_ge(sg("last_h"), k // 2)
                        dve.scalar_tensor_tensor(out=TMP[:, k % 2, c0:T], in0=M[:, k, c0:T],
                                                 scalar=vec(post, KT * layer + k), in1=post_rstd(c0),
                                                 op0=ALU.mult, op1=ALU.mult).then_inc(sg("fuse_term"), 1)
                    if u == 3 and k % 2 == 1:
                        dve.wait_ge(sg("fuse_term"), KT * u + k + 1)
                        dve.tensor_tensor(H[:, k, c0:T], H[:, k, c0:T], TMP[:, 1, c0:T], ALU.add
                                          ).then_inc(sg("last_h"), 1)
                    if k and pre:
                        low_part(u + 1, k - 1, pre, pre_layer, c0)
                if pre:
                    rstd(f"prep{u + 1}", RS, c0)

            def mlp(layer, c0):
                b0, first = FIRST[f"mlp{layer}"], 32 * layer
                stage = f"mlp{layer}"
                for f in range(2):
                    with dve.Fori(0, 4) as i:
                        for s in range(2):
                            for q in range(2):
                                n = i * 4 + 2 * s + q
                                if q == 0:
                                    dve.wait_ge(sg("tile_done"), i * 2 + DONE[stage] + 12 * f + s + 1)
                                else:
                                    dve.wait_ge(sg("w_used"), i * 2 + b0 + 16 * f + s + 3)
                                dve.scalar_tensor_tensor(out=two(TMP[:, q, c0:T]), in0=g_tile(q, T - c0), scalar=0.0,
                                                         in1=two(RS[:, c0:T]), op0=ALU.max, op1=ALU.mult
                                                         ).then_inc(sg("g_evac"), 1)
                                up_low(n, q, c0, first + 16 * f)
                                if q == 1:
                                    split(b0 + 16 * f + 2 + s, i, 4)
                    if f == 0:
                        outputs(stage, b0 + 8, 8, c0, final=False)
                outputs(stage, b0 + 24, 20, c0, add=True)

            def up_low(n, q, c0, first):
                dve.wait_ge(sg("up_square"), n + first + 1)
                dve.wait_ge(sg("up_hi"), n + first + 1)
                dve.tensor_tensor(ULO[:, bass.ds(n, 1), c0:T], SQT[:, q:q + 1, c0:T],
                                  UHI[:, bass.ds(n, 1), c0:T].bitcast(F32), ALU.subtract).then_inc(sg("up_lo"), 1)

            outputs("wout", FIRST["wout"], 0, 0)
            fuse(0, "mix_post_g", "mlp_pre_g", 0, 0, G_FIRST["mlp0"], 0)
            mlp(0, 0)
            fuse(1, "mlp_post_g", "mix_pre_g", 0, 1, G_FIRST["lru"], 0)

            lam = VB[:, PACK_B["rg_lambda"][0]:PACK_B["rg_lambda"][0] + LT]
            softplus_start("lam", LAM, lambda: dve.tensor_scalar(LAM[:, 0, :], lam, -1.0, None, ALU.mult))
            softplus_recip("lam", LAM)
            softplus_end("lam", LAM)
            dve.tensor_scalar(cl[:, :], LAM[:, 0, :], -8.0, None, ALU.mult).then_inc(sg("lru_c"), 1)
            dve.wait_ge(sg("halo_ready"), 2)
            lnames = ["lconv_tap0", "lconv_tap1", "lconv_tap2", "lconv_tap3"]

            b_lru, t_lru = FIRST["lru"], G_FIRST["lru"]

            def lru_conv(i, s):
                if s == 0:
                    dve.wait_ge(sg("tile_done"), i * 2 + DONE["lru"] + 1)
                else:
                    dve.wait_ge(sg("w_used"), i * 2 + b_lru + 3)
                tile_out(LRAW[:, s, 3:T + 3], s).then_inc(sg("g_evac"), 1)
                taps(LRAW[:, s, :], LACC[:, s, :], "rg_conv_w", lambda j: i * 2 + (s + 10 * j), lnames, i * 2 + s + 1,
                     i * 4 + s + t_lru + 3)

            def lru_gate_out(i, s):
                if s == 0:
                    dve.wait_ge(sg("tile_done"), i * 2 + DONE["lru"] + 2)
                else:
                    dve.wait_ge(sg("w_used"), i * 2 + b_lru + 4)
                tile_out(GATE[:, bass.ds(i * 2 + s, 1), :], s).then_inc(sg("g_evac"), 1)

            def lru_expm1(j):
                for s in range(2):
                    dve.wait_ge(sg("lru_th"), j * 2 + (s + 1))
                    dve.wait_ge(sg("lru_a2"), j * 2 + (s + 1))
                    dve.scalar_tensor_tensor(out=TH[:, s, :], in0=A2[:, s, :], scalar=1.0, in1=TH[:, s, :],
                                             op0=ALU.add, op1=ALU.mult).then_inc(sg("lru_q"), 1)

            def lru_scan(j):
                for s in range(2):
                    dve.wait_ge(sg("lru_root"), j * 2 + (s + 1))
                    dve.wait_ge(sg("lru_ix"), j * 2 + (s + 1))
                    dve.tensor_tensor(TMP[:, s, :], TH[:, s, :], IG[:, s, :], ALU.mult).then_inc(sg("lru_u"), 1)
                for s in range(2):
                    dve.wait_ge(sg("lru_u"), j * 2 + (s + 1))
                    dve.tensor_tensor_scan(A2[:, s, :], RG[:, s, :], TMP[:, s, :], 0.0, ALU.mult, ALU.add
                                           ).then_inc(sg("lru_scan"), 1)
                for s in range(2):
                    dve.wait_ge(sg("lru_scan"), j * 2 + (s + 1))
                    dve.wait_ge(sg("gelu_ready"), j * 2 + (s + 1))
                    dve.tensor_tensor(SQT[:, s:s + 1, :], A2[:, s:s + 1, :], GATE[:, bass.ds(j * 2 + s, 1), :], ALU.mult
                                      ).then_inc(sg("lru_gated"), 1)

            def lru_low(j):
                for s in range(2):
                    dve.wait_ge(sg("lru_hi"), j * 2 + (s + 1))
                    dve.tensor_tensor(GLO[:, bass.ds(j * 2 + s, 1), :], SQT[:, s:s + 1, :],
                                      GHI[:, bass.ds(j * 2 + s, 1), :].bitcast(F32), ALU.subtract
                                      ).then_inc(sg("lru_lo"), 1)

            def lru_turn(i, j, turns):
                split(b_lru + 1, i, turns)
                lru_conv(i, 0)
                lru_expm1(j)
                lru_conv(i, 1)
                lru_scan(j)
                split(b_lru + 2, i, turns)
                lru_gate_out(i, 0)
                lru_low(j)
                lru_gate_out(i, 1)

            lru_conv(0, 0)
            lru_conv(0, 1)
            split(b_lru + 2)
            lru_gate_out(0, 0)
            lru_gate_out(0, 1)
            with dve.Fori(1, LT // 2 - 1) as i:
                lru_turn(i, i - 1, LT // 2 - 1)
            lru_turn(LT // 2 - 1, LT // 2 - 2, 1)
            j = LT // 2 - 1
            split(b_lru + 1, LT // 2)
            lru_expm1(j)
            lru_scan(j)
            lru_low(j)

            def rgo(i, turns=1):
                b = FIRST["rgo"]
                for s in range(2):
                    dve.wait_ge(sg("w_used"), i * 2 + b + s + 3)
                    out_tile(i * 2 + s, s, META, False).then_inc(sg("g_evac"), 1)
                    if s == 0 or not isinstance(i, int):
                        split(b + 2 + s, i, turns)

            with dve.Fori(0, 3) as i:
                rgo(i, 3)
            rgo(3)
            fuse(2, "mix_post_g", "mlp_pre_g", 1, 1, G_FIRST["mlp1"], META)
            mlp(1, META)
            fuse(3, "mlp_post_g", None, 1, 0, G_FIRST["mlp1"] + 48, META)
            for c in range(4):
                dve.wait_ge(sg("out_turned"), 2 * c + 2)
                dve.tensor_copy(OUTN[:, c, 512:1024], PS[:, 4 + (2 * c + 1) % 4, :]).then_inc(sg("out_rows_dve"), 1)



def shape_constants():
    import numpy as np
    rows, cols = np.arange(P)[:, None], np.arange(P)[None, :]
    freq = np.float32(10000.0) ** (-np.arange(0, ROPE, 2, dtype=np.float32) / np.float32(ROPE))
    angle = (freq[:, None] * np.arange(T, dtype=np.float32)[None, :]).astype(np.float64)
    cos, sin = np.cos(angle), np.sin(angle)
    return {"c_ident": np.eye(P, dtype=np.float32),
            "c_neg": np.where(cols <= rows, 0.0, -1e30).astype(np.float32),
            "c_triu": (rows <= cols).astype(np.float32),
            "c_cs": np.concatenate([np.ones((NOPE, T)), cos, cos, -sin, sin]).astype(np.float32)}


def kernel(**inputs):
    import numpy as np
    import concourse.bacc as bacc
    from concourse.bass_utils import run_bass_kernel_spmd

    nc = bacc.Bacc("TRN2", target_bir_lowering=False, num_devices=1)
    arrays, args = {}, {}
    for name, value in {**inputs, **shape_constants()}.items():
        a = np.ascontiguousarray(value)
        arrays[f"in_{name}_dram"] = a
        args[name] = nc.dram_tensor(f"in_{name}_dram", a.shape, mybir.dt.from_np(a.dtype), kind="ExternalInput").ap()
    out = nc.dram_tensor("out_0_dram", (1, SEQ, D), F32, kind="ExternalOutput").ap()
    build(nc, args, out)
    result = run_bass_kernel_spmd(nc, [arrays], core_ids=[0])
    return result.results[0]["out_0_dram"]
```
